# Optimizing a Trainium2 kernel written in Bass

```python
import math
import jax, jax.numpy as jnp
from jax import lax
import numpy as np

D_MODEL = 1024
BATCH = 1
SEQ = 256
DEPTH = 2

GRID_W = 64
CTX_LEN = 256
CHUNK = 64
SHORT_CONV = 3
GLA_HEADS = 4
GLA_DK = 128
GLA_DV = 256
GLA_GATE_RANK = 16
GLA_GATE_TAU = 16.0
SSD_HEADS = 16
SSD_HEADDIM = 64
SSD_STATE = 128
SSD_GROUPS = 2
DT_MIN = 0.001
DT_MAX = 0.1
CONF_CH = D_MODEL
CONF_KERNEL = 31
GDN_HEADS = 8
GDN_DK = 128
GDN_DV = 128
N_EXPERTS = 16
EC_CAPACITY = 2
EXPERT_FF = D_MODEL

GLA_QK = GLA_HEADS * GLA_DK
GLA_V = GLA_HEADS * GLA_DV
SSD_INNER = SSD_HEADS * SSD_HEADDIM
SSD_BC = SSD_GROUPS * SSD_STATE
GDN_QK = GDN_HEADS * GDN_DK
GDN_V = GDN_HEADS * GDN_DV
AB_SPLITS = (GLA_QK, GLA_QK, GLA_V, GLA_V, 2 * GLA_GATE_RANK, SSD_INNER, SSD_INNER, SSD_BC, SSD_BC, 2 * SSD_HEADS)
IN_AB = 2 * GLA_QK + 2 * GLA_V + 2 * GLA_GATE_RANK + 2 * SSD_INNER + 2 * SSD_BC + 2 * SSD_HEADS
AB_MIX = GLA_V + SSD_INNER
CD_SPLITS = (CONF_CH, CONF_CH, GDN_QK, GDN_QK, GDN_V, GDN_V, 2 * GDN_HEADS, 2 * GDN_HEADS)
IN_CD = 2 * CONF_CH + 2 * GDN_QK + 2 * GDN_V + 4 * GDN_HEADS
CD_MIX = CONF_CH + GDN_V

kernel_name = "hybrid_gla_ssd_conformer_gdn_ec_moe_prefix"

F32 = jnp.float32

def split_cols(a, sizes):
    return jnp.split(a, np.cumsum(sizes)[:-1].tolist(), axis=-1)

def rmsnorm(x, g, eps=1e-6):
    xf = x.astype(F32)
    y = xf * lax.rsqrt(jnp.mean(jnp.square(xf), axis=-1, keepdims=True) + eps)
    return (y * g.astype(F32)).astype(x.dtype)

def head_rmsnorm(x, g):
    return rmsnorm(x, g.reshape(x.shape[-2:]))

def layernorm(x, g, b, eps=1e-5):
    xf = x.astype(F32)
    mu = jnp.mean(xf, axis=-1, keepdims=True)
    var = jnp.mean(jnp.square(xf - mu), axis=-1, keepdims=True)
    return ((xf - mu) * lax.rsqrt(var + eps) * g.astype(F32) + b.astype(F32)).astype(x.dtype)

def l2norm(x, eps=1e-6):
    return x * lax.rsqrt(jnp.sum(jnp.square(x), axis=-1, keepdims=True) + eps)

def modulate(h, shift, scale):
    return h * (1 + scale) + shift

def dwconv(x, w, b=None):
    k, ch = w.shape
    pad = (k - 1) // 2
    y = lax.conv_general_dilated(x, w[:, None, :].astype(x.dtype), (1,), [(pad, pad)],
                                 dimension_numbers=('NWC', 'WIO', 'NWC'), feature_group_count=ch)
    return y if b is None else y + b.astype(x.dtype)

def gla_scan(q, k, v, logg, s0, with_out):
    bsz, nh, t, dk = q.shape
    dv = v.shape[-1]
    nc = t // CHUNK
    chunks = lambda z: z.reshape(bsz, nh, nc, CHUNK, z.shape[-1])
    q, k, v, logg = chunks(q), chunks(k), chunks(v), chunks(logg)
    gc = jnp.cumsum(logg, axis=3)
    glast = gc[:, :, :, -1]
    kd = k * jnp.exp(glast[:, :, :, None] - gc)
    front = lambda z: jnp.moveaxis(z, 2, 0)

    def advance(s, kd_c, v_c, gl_c):
        return jnp.exp(gl_c)[..., None] * s + jnp.einsum('bhjd,bhje->bhde', kd_c, v_c)

    xs = (front(kd), front(v), front(glast))
    if not with_out:
        s_fin, _ = lax.scan(lambda s, xc: (advance(s, *xc), None), s0, xs)
        return None, s_fin
    tril = jnp.tril(jnp.ones((CHUNK, CHUNK), dtype=bool))
    qg = q * jnp.exp(gc)
    att = jnp.where(tril, jnp.einsum('bhcid,bhcjd->bhcij', qg, k * jnp.exp(-gc)), 0.0)
    o_intra = jnp.einsum('bhcij,bhcje->bhcie', att, v)

    def step(s, xc):
        kd_c, v_c, gl_c, qg_c = xc
        return advance(s, kd_c, v_c, gl_c), jnp.einsum('bhid,bhde->bhie', qg_c, s)

    s_fin, o_inter = lax.scan(step, s0, xs + (front(qg),))
    o = o_intra + jnp.moveaxis(o_inter, 0, 2)
    return o.reshape(bsz, nh, t, dv), s_fin

def ssd_scan(v, loga, bm, cm, s0, with_out):
    bsz, t, nh, p = v.shape
    ng, n = bm.shape[2:]
    r = nh // ng
    nc = t // CHUNK
    v = v.reshape(bsz, nc, CHUNK, ng, r, p)
    acum = jnp.cumsum(loga.reshape(bsz, nc, CHUNK, ng, r), axis=2)
    bm = bm.reshape(bsz, nc, CHUNK, ng, n)
    cm = cm.reshape(bsz, nc, CHUNK, ng, n)
    alast = acum[:, :, -1]
    wgt = jnp.exp(alast[:, :, None] - acum)
    front = lambda z: jnp.moveaxis(z, 1, 0)

    def advance(s, bm_c, wgt_c, v_c, al_c):
        return (jnp.exp(al_c)[..., None, None] * s
                + jnp.einsum('bjgn,bjgr,bjgrp->bgrnp', bm_c, wgt_c, v_c))

    xs = (front(bm), front(wgt), front(v), front(alast))
    if not with_out:
        s_fin, _ = lax.scan(lambda s, xc: (advance(s, *xc), None), s0, xs)
        return None, s_fin
    tril = jnp.tril(jnp.ones((CHUNK, CHUNK), dtype=bool))[:, :, None, None]
    seg = jnp.exp(jnp.where(tril, acum[:, :, :, None] - acum[:, :, None], -jnp.inf))
    cb = jnp.einsum('bcign,bcjgn->bcijg', cm, bm)
    y_intra = jnp.einsum('bcijgr,bcjgrp->bcigrp', seg * cb[..., None], v)
    cdec = jnp.exp(acum)

    def step(s, xc):
        bm_c, wgt_c, v_c, al_c, cm_c, cd_c = xc
        y = jnp.einsum('bign,bgrnp->bigrp', cm_c, s) * cd_c[..., None]
        return advance(s, bm_c, wgt_c, v_c, al_c), y

    s_fin, y_inter = lax.scan(step, s0, xs + (front(cm), front(cdec)))
    y = y_intra + jnp.moveaxis(y_inter, 0, 1)
    return y.reshape(bsz, t, nh, p), s_fin

def gdn_scan(q, k, v, beta, logg, s0, with_out):
    bsz, nh, t, dk = q.shape
    dv = v.shape[-1]
    nc = t // CHUNK
    chunks = lambda z: z.reshape(bsz, nh, nc, CHUNK, *z.shape[3:])
    q, k, v, beta, logg = (chunks(z) for z in (q, k, v, beta, logg))
    gc = jnp.cumsum(logg, axis=-1)
    glast = gc[..., -1]
    tril = jnp.tril(jnp.ones((CHUNK, CHUNK), dtype=bool))
    strict = jnp.tril(jnp.ones((CHUNK, CHUNK), dtype=bool), k=-1)
    decay = jnp.exp(jnp.where(tril, gc[..., :, None] - gc[..., None, :], -jnp.inf))
    kb = k * beta[..., None]
    m = jnp.eye(CHUNK, dtype=k.dtype) + jnp.where(strict, jnp.einsum('bhcid,bhcjd->bhcij', kb, k) * decay, 0.0)
    rhs = jnp.concatenate([v * beta[..., None], kb * jnp.exp(gc)[..., None]], axis=-1)
    sol = lax.linalg.triangular_solve(m, rhs, left_side=True, lower=True, unit_diagonal=True)
    u, w = sol[..., :dv], sol[..., dv:]
    kd = k * jnp.exp(glast[..., None] - gc)[..., None]
    dec = jnp.exp(glast)
    front = lambda z: jnp.moveaxis(z, 2, 0)

    def advance(s, w_c, u_c, kd_c, dec_c):
        vn = u_c - jnp.einsum('bhid,bhde->bhie', w_c, s)
        return vn, dec_c[..., None, None] * s + jnp.einsum('bhjd,bhje->bhde', kd_c, vn)

    xs = (front(w), front(u), front(kd), front(dec))
    if not with_out:
        s_fin, _ = lax.scan(lambda s, xc: (advance(s, *xc)[1], None), s0, xs)
        return None, s_fin
    aqk = jnp.einsum('bhcid,bhcjd->bhcij', q, k) * decay
    qg = q * jnp.exp(gc)[..., None]

    def step(s, xc):
        w_c, u_c, kd_c, dec_c, aqk_c, qg_c = xc
        vn, s_new = advance(s, w_c, u_c, kd_c, dec_c)
        o = jnp.einsum('bhid,bhde->bhie', qg_c, s) + jnp.einsum('bhij,bhje->bhie', aqk_c, vn)
        return s_new, o

    s_fin, o = lax.scan(step, s0, xs + (front(aqk), front(qg)))
    return jnp.moveaxis(o, 0, 2).reshape(bsz, nh, t, dv), s_fin

def bidir_scan(scan_fn, args_f, args_b, t_axis, init_f, init_b, with_out):
    flip = lambda a: jnp.flip(a, axis=t_axis)
    o_f, s_f = scan_fn(*args_f, init_f, with_out)
    o_b, s_b = scan_fn(*[flip(a) for a in args_b], init_b, with_out)
    o = o_f + flip(o_b) if with_out else None
    return o, s_f, s_b

def ab_stream(h, w_in, b_in, gla_w_gate2, gla_b_gate2, ssd_conv_w, ssd_conv_b, ssd_dt_bias, ssd_a_log):
    bsz, t, _ = h.shape
    q, k, v, r, glr, z, xs, bm, cm, dt = split_cols(h @ w_in + b_in, AB_SPLITS)
    heads = lambda a, nh: a.astype(F32).reshape(bsz, t, nh, -1).transpose(0, 2, 1, 3)
    q = heads(q, GLA_HEADS) * GLA_DK ** -0.5
    k = heads(k, GLA_HEADS)
    v = heads(v, GLA_HEADS)
    gz = (jnp.einsum('btsr,srk->sbtk', glr.astype(F32).reshape(bsz, t, 2, GLA_GATE_RANK), gla_w_gate2.astype(F32))
          + gla_b_gate2.astype(F32)[:, None, None])
    logg = (jax.nn.log_sigmoid(gz) / GLA_GATE_TAU).reshape(2, bsz, t, GLA_HEADS, GLA_DK).transpose(0, 1, 3, 2, 4)
    xbc = jax.nn.silu(dwconv(jnp.concatenate([xs, bm, cm], axis=-1), ssd_conv_w, ssd_conv_b)).astype(F32)
    xs, bm, cm = split_cols(xbc, (SSD_INNER, SSD_BC, SSD_BC))
    xs = xs.reshape(bsz, t, SSD_HEADS, SSD_HEADDIM)
    bm = bm.reshape(bsz, t, SSD_GROUPS, SSD_STATE)
    cm = cm.reshape(bsz, t, SSD_GROUPS, SSD_STATE)
    dt = jax.nn.softplus(dt.astype(F32).reshape(bsz, t, 2, SSD_HEADS) + ssd_dt_bias.astype(F32))
    loga = -dt * jnp.exp(ssd_a_log.astype(F32))
    gla_f = (q, k, v, logg[0])
    gla_b = (q, k, v, logg[1])
    ssd_f = (xs * dt[:, :, 0, :, None], loga[:, :, 0], bm, cm)
    ssd_b = (xs * dt[:, :, 1, :, None], loga[:, :, 1], bm, cm)
    return gla_f, gla_b, ssd_f, ssd_b, (r, z, xs)

def ab_merge(o_gla, y_ssd, extras, w_out, b_out, gla_norm_g, ssd_d, ssd_norm_g, dtype):
    r, z, xs = extras
    bsz, t = r.shape[:2]
    o = head_rmsnorm(jnp.swapaxes(o_gla, 1, 2), gla_norm_g) * jax.nn.silu(r.astype(F32)).reshape(bsz, t, GLA_HEADS, GLA_DV)
    y = (y_ssd + ssd_d.astype(F32)[:, None] * xs).reshape(bsz, t, SSD_INNER) * jax.nn.silu(z.astype(F32))
    y = rmsnorm(y.reshape(bsz, t, SSD_GROUPS, -1), ssd_norm_g.reshape(SSD_GROUPS, -1))
    mixed = jnp.concatenate([o.reshape(bsz, t, GLA_V), y.reshape(bsz, t, SSD_INNER)], axis=-1).astype(dtype)
    return mixed @ w_out + b_out

def mixer_ab(h, hc, w_in, b_in, w_out, b_out, gla_w_gate2, gla_b_gate2, gla_norm_g,
             ssd_conv_w, ssd_conv_b, ssd_dt_bias, ssd_a_log, ssd_d, ssd_norm_g, need_ctx):
    stream = lambda s: ab_stream(s, w_in, b_in, gla_w_gate2, gla_b_gate2, ssd_conv_w, ssd_conv_b, ssd_dt_bias, ssd_a_log)
    cg_f, cg_b, cs_f, cs_b, c_ext = stream(hc)
    lg_f, lg_b, ls_f, ls_b, l_ext = stream(h)
    bsz = h.shape[0]
    zg = jnp.zeros((bsz, GLA_HEADS, GLA_DK, GLA_DV), F32)
    zs = jnp.zeros((bsz, SSD_GROUPS, SSD_HEADS // SSD_GROUPS, SSD_STATE, SSD_HEADDIM), F32)
    og_c, sg_f, sg_b = bidir_scan(gla_scan, cg_f, cg_b, 2, zg, zg, need_ctx)
    os_c, ss_f, ss_b = bidir_scan(ssd_scan, cs_f, cs_b, 1, zs, zs, need_ctx)
    og_l, _, _ = bidir_scan(gla_scan, lg_f, lg_b, 2, sg_f, sg_b, True)
    os_l, _, _ = bidir_scan(ssd_scan, ls_f, ls_b, 1, ss_f, ss_b, True)
    merge = lambda og, osd, ext: ab_merge(og, osd, ext, w_out, b_out, gla_norm_g, ssd_d, ssd_norm_g, h.dtype)
    out_l = merge(og_l, os_l, l_ext)
    out_c = merge(og_c, os_c, c_ext) if need_ctx else None
    return out_l, out_c

def conformer_conv(u, rows, dw_w, dw_b, ln_g, ln_b):
    bsz, t, ch = u.shape
    y = dwconv(u.reshape(bsz * rows, t // rows, ch), dw_w, dw_b).reshape(bsz, t, ch)
    return jax.nn.silu(layernorm(y, ln_g, ln_b))

def cd_stream(h, w_in, b_in, gdn_conv_w, gdn_a_log, gdn_dt_bias):
    bsz, t, _ = h.shape
    ga, gb, q, k, v, og, a_raw, b_raw = split_cols(h @ w_in + b_in, CD_SPLITS)
    glu = ga * jax.nn.sigmoid(gb)
    qkv = jax.nn.silu(dwconv(jnp.concatenate([q, k, v], axis=-1), gdn_conv_w)).astype(F32)
    q, k, v = split_cols(qkv, (GDN_QK, GDN_QK, GDN_V))
    heads = lambda a: a.reshape(bsz, t, GDN_HEADS, -1).transpose(0, 2, 1, 3)
    q = l2norm(heads(q)) * GDN_DK ** -0.5
    k = l2norm(heads(k))
    v = heads(v)
    beta = jax.nn.sigmoid(b_raw.astype(F32).reshape(bsz, t, 2, GDN_HEADS)).transpose(2, 0, 3, 1)
    logg = (-jnp.exp(gdn_a_log.astype(F32))
            * jax.nn.softplus(a_raw.astype(F32).reshape(bsz, t, 2, GDN_HEADS) + gdn_dt_bias.astype(F32))).transpose(2, 0, 3, 1)
    return (q, k, v, beta[0], logg[0]), (q, k, v, beta[1], logg[1]), glu, og

def mixer_cd(h, hc, rows, w_in, b_in, w_out, b_out, conf_dw_w, conf_dw_b, conf_ln_g, conf_ln_b,
             gdn_conv_w, gdn_a_log, gdn_dt_bias, gdn_norm_g, need_ctx):
    c_f, c_b, c_glu, c_og = cd_stream(hc, w_in, b_in, gdn_conv_w, gdn_a_log, gdn_dt_bias)
    l_f, l_b, l_glu, l_og = cd_stream(h, w_in, b_in, gdn_conv_w, gdn_a_log, gdn_dt_bias)
    bsz = h.shape[0]
    z0 = jnp.zeros((bsz, GDN_HEADS, GDN_DK, GDN_DV), F32)
    od_c, s_f, s_b = bidir_scan(gdn_scan, c_f, c_b, 2, z0, z0, need_ctx)
    od_l, _, _ = bidir_scan(gdn_scan, l_f, l_b, 2, s_f, s_b, True)

    def merge(od, glu, og, n_rows):
        t = glu.shape[1]
        conv = conformer_conv(glu, n_rows, conf_dw_w, conf_dw_b, conf_ln_g, conf_ln_b)
        o = head_rmsnorm(jnp.swapaxes(od, 1, 2), gdn_norm_g) * jax.nn.silu(og.astype(F32)).reshape(bsz, t, GDN_HEADS, GDN_DV)
        mixed = jnp.concatenate([conv, o.reshape(bsz, t, GDN_V).astype(conv.dtype)], axis=-1)
        return mixed @ w_out + b_out

    out_l = merge(od_l, l_glu, l_og, rows)
    out_c = merge(od_c, c_glu, c_og, 1) if need_ctx else None
    return out_l, out_c

def expert_choice_ffn(h, router_w, w1, w3, w2):
    bsz, n, d = h.shape
    cap = n * EC_CAPACITY // N_EXPERTS
    aff = jax.nn.softmax((h @ router_w).astype(F32), axis=-1)
    gates, idx = lax.top_k(jnp.swapaxes(aff, 1, 2), cap)
    idx = idx.reshape(bsz, N_EXPERTS * cap)
    xe = jnp.take_along_axis(h, idx[..., None], axis=1).reshape(bsz, N_EXPERTS, cap, d)
    hid = jax.nn.silu(jnp.einsum('becd,edf->becf', xe, w1)) * jnp.einsum('becd,edf->becf', xe, w3)
    ye = jnp.einsum('becf,efd->becd', hid, w2) * gates[..., None].astype(h.dtype)
    return jnp.zeros_like(h).at[jnp.arange(bsz)[:, None], idx].add(ye.reshape(bsz, N_EXPERTS * cap, d))

def setup_inputs(seed: int = 0) -> dict:
    key = jax.random.key(seed)
    ks = iter(jax.random.split(key, 48))

    def nrm(shape, scale):
        return jax.random.normal(next(ks), shape, jnp.float32) * scale

    def gain(shape):
        return 1.0 + nrm(shape, 0.1)

    def dt_bias(shape):
        u = jax.random.uniform(next(ks), shape, jnp.float32)
        dt = jnp.exp(u * (math.log(DT_MAX) - math.log(DT_MIN)) + math.log(DT_MIN))
        return dt + jnp.log(-jnp.expm1(-dt))

    def a_log(shape):
        return jnp.log(jax.random.uniform(next(ks), shape, jnp.float32, 1.0, 16.0))

    d = D_MODEL
    ne, no = (DEPTH + 1) // 2, DEPTH // 2
    return {
        "x": nrm((BATCH, SEQ, d), 1.0),
        "c": nrm((BATCH, d), 1.0),
        "ctx": nrm((BATCH, CTX_LEN, d), 1.0),
        "c_ctx": nrm((d,), 1.0),
        "mod_w": nrm((DEPTH, d, 6 * d), 0.5 * d ** -0.5),
        "mod_b": nrm((DEPTH, 6 * d), 0.02),
        "norm1_g": gain((DEPTH, d)),
        "norm2_g": gain((DEPTH, d)),
        "ab_w_in": nrm((ne, d, IN_AB), d ** -0.5),
        "ab_b_in": nrm((ne, IN_AB), 0.02),
        "ab_w_out": nrm((ne, AB_MIX, d), AB_MIX ** -0.5),
        "ab_b_out": nrm((ne, d), 0.02),
        "gla_w_gate2": nrm((ne, 2, GLA_GATE_RANK, GLA_QK), GLA_GATE_RANK ** -0.5),
        "gla_b_gate2": nrm((ne, 2, GLA_QK), 0.1),
        "gla_norm_g": gain((ne, GLA_V)),
        "ssd_conv_w": nrm((ne, SHORT_CONV, SSD_INNER + 2 * SSD_BC), SHORT_CONV ** -0.5),
        "ssd_conv_b": nrm((ne, SSD_INNER + 2 * SSD_BC), 0.02),
        "ssd_dt_bias": dt_bias((ne, 2, SSD_HEADS)),
        "ssd_a_log": a_log((ne, 2, SSD_HEADS)),
        "ssd_d": gain((ne, SSD_HEADS)),
        "ssd_norm_g": gain((ne, SSD_INNER)),
        "cd_w_in": nrm((no, d, IN_CD), d ** -0.5),
        "cd_b_in": nrm((no, IN_CD), 0.02),
        "cd_w_out": nrm((no, CD_MIX, d), CD_MIX ** -0.5),
        "cd_b_out": nrm((no, d), 0.02),
        "conf_dw_w": nrm((no, CONF_KERNEL, CONF_CH), CONF_KERNEL ** -0.5),
        "conf_dw_b": nrm((no, CONF_CH), 0.02),
        "conf_ln_g": gain((no, CONF_CH)),
        "conf_ln_b": nrm((no, CONF_CH), 0.02),
        "gdn_conv_w": nrm((no, SHORT_CONV, 2 * GDN_QK + GDN_V), SHORT_CONV ** -0.5),
        "gdn_a_log": a_log((no, 2, GDN_HEADS)),
        "gdn_dt_bias": dt_bias((no, 2, GDN_HEADS)),
        "gdn_norm_g": gain((no, GDN_V)),
        "moe_router": nrm((DEPTH, d, N_EXPERTS), d ** -0.5),
        "moe_w1": nrm((DEPTH, N_EXPERTS, d, EXPERT_FF), d ** -0.5),
        "moe_w3": nrm((DEPTH, N_EXPERTS, d, EXPERT_FF), d ** -0.5),
        "moe_w2": nrm((DEPTH, N_EXPERTS, EXPERT_FF, d), EXPERT_FF ** -0.5),
        "final_norm_g": gain((d,)),
    }

def reference(x, c, ctx, c_ctx, mod_w, mod_b, norm1_g, norm2_g,
              ab_w_in, ab_b_in, ab_w_out, ab_b_out, gla_w_gate2, gla_b_gate2, gla_norm_g,
              ssd_conv_w, ssd_conv_b, ssd_dt_bias, ssd_a_log, ssd_d, ssd_norm_g,
              cd_w_in, cd_b_in, cd_w_out, cd_b_out, conf_dw_w, conf_dw_b, conf_ln_g, conf_ln_b,
              gdn_conv_w, gdn_a_log, gdn_dt_bias, gdn_norm_g,
              moe_router, moe_w1, moe_w3, moe_w2, final_norm_g):
    rows = x.shape[1] // GRID_W
    xc = ctx
    for i in range(DEPTH):
        last = i == DEPTH - 1
        j = i // 2
        sh1, sc1, g1, sh2, sc2, g2 = (m[:, None, :] for m in
                                      jnp.split(jax.nn.silu(c) @ mod_w[i] + mod_b[i], 6, axis=-1))
        sh1c, sc1c, g1c, sh2c, sc2c, g2c = jnp.split(jax.nn.silu(c_ctx) @ mod_w[i] + mod_b[i], 6, axis=-1)
        h = modulate(rmsnorm(x, norm1_g[i]), sh1, sc1)
        hc = modulate(rmsnorm(xc, norm1_g[i]), sh1c, sc1c)
        if i % 2 == 0:
            m, mc = mixer_ab(h, hc, ab_w_in[j], ab_b_in[j], ab_w_out[j], ab_b_out[j],
                             gla_w_gate2[j], gla_b_gate2[j], gla_norm_g[j],
                             ssd_conv_w[j], ssd_conv_b[j], ssd_dt_bias[j], ssd_a_log[j], ssd_d[j], ssd_norm_g[j],
                             not last)
        else:
            m, mc = mixer_cd(h, hc, rows, cd_w_in[j], cd_b_in[j], cd_w_out[j], cd_b_out[j],
                             conf_dw_w[j], conf_dw_b[j], conf_ln_g[j], conf_ln_b[j],
                             gdn_conv_w[j], gdn_a_log[j], gdn_dt_bias[j], gdn_norm_g[j], not last)
        x = x + g1 * m
        h = modulate(rmsnorm(x, norm2_g[i]), sh2, sc2)
        x = x + g2 * expert_choice_ffn(h, moe_router[i], moe_w1[i], moe_w3[i], moe_w2[i])
        if not last:
            xc = xc + g1c * mc
            hc = modulate(rmsnorm(xc, norm2_g[i]), sh2c, sc2c)
            xc = xc + g2c * expert_choice_ffn(hc, moe_router[i], moe_w1[i], moe_w3[i], moe_w2[i])
    return rmsnorm(x, final_norm_g)


_drawn_inputs = setup_inputs


def setup_inputs(seed=0):
    import zlib

    import numpy as np

    out = dict(_drawn_inputs(seed))
    spreads = {}
    factors = {'ab_b_in': 4.264,
     'ab_b_out': 8.0,
     'gla_b_gate2': 6.667,
     'gla_norm_g': 3.45,
     'ssd_conv_b': 7.09,
     'ssd_d': 57.501,
     'cd_b_in': 8.0,
     'cd_b_out': 8.0,
     'conf_dw_b': 8.0,
     'conf_ln_g': 3.943,
     'conf_ln_b': 24.352,
     'gdn_norm_g': 3.892,
     'ssd_dt_bias': 21.352,
     'ssd_a_log': 8.0}
    for name, (base, spread) in spreads.items():
        noise = np.random.default_rng([zlib.crc32(name.encode()), seed]).standard_normal(out[name].shape)
        drawn = base * np.exp(spread * noise) if base else spread * noise
        out[name] = __import__('jax').numpy.asarray(drawn.astype(out[name].dtype))
    for name, factor in factors.items():
        out[name] = (out[name] * factor).astype(out[name].dtype)
    return out
```

```python
from contextlib import ExitStack

import concourse.bass as bass
from concourse import mybir

ALU = mybir.AluOpType
ACT = mybir.ActivationFunctionType
F32 = mybir.dt.float32
I32 = mybir.dt.int32
BF16 = mybir.dt.bfloat16
AX = mybir.AxisListType

P = 128
D = 1024
KD = D // P
SEQ = 256
T = 2 * SEQ
NT = T // P
CH = 64
NC = T // CH
GH, GDV = 4, 256
SH = 16
CK = 31
GW, ROWS = 64, SEQ // 64
PADW = GW + CK - 1
E, CAP = 16, 32
Q = E // 4
TINY = 1e-30

COLS = [("mod_b0", 48), ("mod_b1", 48), ("norm1", 16), ("norm2", 16), ("final", 8), ("cvec", 16),
        ("ab_b", 45), ("ab_bout", 8), ("gla_bg", 8), ("gla_g", 8), ("ssd_cw", 36), ("ssd_cb", 12),
        ("ssd_g", 8), ("ssd_dtb", 1), ("ssd_alog", 1), ("cd_b", 49), ("cd_bout", 8), ("conf_w", 248),
        ("conf_b", 8), ("conf_g", 8), ("conf_bb", 8), ("gdn_cw", 72), ("gdn_g", 8), ("gdn_dtb", 1),
        ("gdn_alog", 1)]
COL_AT = {}
NCOLS = 0
for _name, _width in COLS:
    COL_AT[_name] = NCOLS
    NCOLS += _width

AB_GLA = [("small", 0)] + [("q", i) for i in range(4)] + [("k", i) for i in range(4)] \
    + [("v", i) for i in range(8)] + [("r", i) for i in range(8)]
AB_SSD = [("xs", i) for i in range(8)] + [("bm", 0), ("bm", 1), ("cm", 0), ("cm", 1)] + [("z", i) for i in range(8)]
CD_ALL = [("small", 0)] + [(k, i) for i in range(8) for k in ("gb", "ga", "k", "v", "og", "q")]
CONF_STEPS = [(0, 7), (7, 13), (13, 19), (19, 25), (25, 31)]


def weight_groups():
    g = [(f"mod0{r}", i, 4) for r in range(3) for i in range(2)]
    g += [("gla", 8 * i, 1) for i in range(4)]
    g += [("mod10", i, 4) for i in range(2)]
    g += [("ssd", 8 * i, 1) for i in range(3)]
    g += [(f"mod1{r}", i, 4) for r in range(1, 3) for i in range(2)]
    g += [("about", 4 * i, 1) for i in range(2)]
    g += [("moe0", i, 4) for i in range(12 * Q)]
    g += [("cd", 8 * i, 1) for i in range(7)]
    g += [("cdout", 4 * i, 1) for i in range(2)]
    g += [("moe1", i, 4) for i in range(12 * Q)]
    return g


RING = 3


class Ring:

    def __init__(self):
        self.groups = weight_groups()
        self.first, self.landed = {}, []
        total = [0] * RING
        for n, (stage, _, dmas) in enumerate(self.groups):
            self.first.setdefault(stage, n)
            total[n % RING] += 16 * dmas
            self.landed.append(total[n % RING])


def hybrid_backbone(nc, A, out):
    rg = Ring()
    with ExitStack() as ctx:
        def sem(name):
            return ctx.enter_context(nc.semaphore(name))

        def sb(name, shape, dt=F32, stack=ctx):
            return stack.enter_context(nc.sbuf_tensor(name, shape, dt))

        ps = [ctx.enter_context(nc.psum_tensor(f"bank{i}", [P, 512], F32)) for i in range(8)]

        ring = sb("ring", [P, RING, 4, 2048])
        x = sb("x", [P, KD, T])
        hT = sb("hT", [P, KD, T])
        cols = sb("cols", [P, NCOLS])
        modT = sb("modT", [P, 2, 12, 4, 2])
        afac = sb("afac", [P, 2, 2, KD, 2])
        ident = sb("ident", [P, P])
        ones = sb("ones", [P, P])
        m_gla = sb("m_gla", [P, 2, P], I32)
        m_inc = sb("m_inc", [P, 2, P])
        m_str = sb("m_str", [P, 2, P])
        rst64 = sb("rst64", [P, T])
        rst128 = sb("rst128", [P, T])
        small = sb("small", [P, T])
        rstd = sb("rstd", [P, T])
        iota1 = sb("iota1", [P, CAP])
        gbias = sb("gbias", [P, KD, 2])
        act_c = sb("act_c", [P, KD, 32])
        mrow = sb("mrow", [P, 512])
        dsk = sb("dsk", [P, SH])

        def col(name, i=0, n=1):
            return cols[:, COL_AT[name] + i:COL_AT[name] + i + n]

        def mod(layer, part, k, s):
            return modT[:, layer, 2 * part + k // 4, k % 4, s:s + 1]

        with ExitStack() as st:
            mixA = sb("mixA", [P, 8, T], F32, st)
            with ExitStack() as s2:
                g_q = sb("g_q", [P, GH, T], F32, s2)
                g_k = sb("g_k", [P, GH, T], F32, s2)
                g_v = sb("g_v", [P, 8, NT, P], F32, s2)
                w2p = sb("w2p", [P, 8, P], F32, s2)
                w2s = sb("w2s", [P, P], F32, s2)
                gcum = rstd
                e1 = sb("e1", [P, T], F32, s2)
                e3 = sb("e3", [P, T], F32, s2)
                qg = sb("qg", [P, T], F32, s2)
                attm = sb("attm", [P, 2, NT, P], F32, s2)
                egl = sb("egl", [P, NC], F32, s2)
                kk = x[:, 0:2, :]
                kdt = x[:, 2:4, :].rearrange("p a (b c d) -> p (a b) c d", b=2, c=2)
                sS = x[:, 4:8, :].rearrange("p a (b e) -> p (a b) e", b=2)
                ssq = sb("ssq", [P, NT], F32, s2)
                ssr = sb("ssr", [P, NT], F32, s2)
                sst = sb("sst", [P, NT], F32, s2)
            with ExitStack() as s2:
                zmix = sb("zmix", [P, 8, T], F32, s2)
                xs_t = sb("xs_t", [P, 8, NT, P], F32, s2)
                bmc = sb("bmc", [P, 2, T], F32, s2)
                cmc = sb("cmc", [P, 2, T], F32, s2)
                bm_t = sb("bm_t", [P, 2, NT, P], F32, s2)
                cpad = x[:, 0:3, :].rearrange("p a b -> p (a b)")[:, 0:4 * (SEQ + 2)].rearrange("p (a b c) -> p a b c", a=2, b=2)
                cacc = x[:, 4:6, :]
                s_in = sb("s_in", [P, 3, T], F32, s2)
                row1 = sb("row1", [P, T], F32, s2)
                dtT, acT, dtw, cdec, eal, albuf, nacT = [sb(f"ssd_g{i}", [P, NT, 64], F32, s2) for i in range(7)]
                alog_e = sb("alog_e", [P, 1], F32, s2)
                m_far = sb("m_far", [P, 2, P], BF16, s2)
                identb = sb("identb", [P, P], BF16, s2)
                dtc, ac, sp_w, sp_l, sp_z, sp_u = [x[:, i, :] for i in range(6)]
                row = [x[:, 2, :], row1[:, :]]
                seg = [x[:, 3, :], rstd[:, :]]
                mat = [x[:, 4, :], x[:, 0, :]]
                cbs = x[:, 5, :]
                wv = x[:, 7, :]
                ysb = hT[:, :, :].rearrange("p (t a) b -> p t (a b)", t=NT)

        with ExitStack() as st:
            xe = sb("xe", [P, 2, KD, E * CAP], F32, st)
            htok = sb("htok", [P, NT, D], F32, st)
            pick = sb("pick", [P, 2, 2, E * CAP], F32, st)
            pgate = sb("pgate", [P, 2, 2, E * CAP], F32, st)
            gateT = sb("gateT", [P, 2, Q, SEQ], F32, st)
            pickw = sb("pickw", [48, 2, SEQ], F32, st)
            router = sb("router", [P, KD, E], F32, st)
            aff = sb("aff", [P, NT, E], F32, st)
            affc = sb("affc", [P, 2, 48], F32, st)
            slotT = sb("slotT", [P, 2, 48], F32, st)
            top8 = sb("top8", [48, 8], F32, st)
            rowst = sb("rowst", [P, 3, NT], F32, st)
            affT, pickv = rstd[0:48, 0:SEQ], rstd[0:48, SEQ:T]
            hid = [hT[:, 2 * s:2 * s + 2, :].rearrange("p a b -> p (a b)") for s in range(2)]
            hidT = [hT[:, 4 + 2 * s:6 + 2 * s, :].rearrange("p a (b c) -> p (a b) c", c=P) for s in range(2)]
            xg = [htok[:, s, :].rearrange("p (k c) -> p k c", k=KD) for s in range(2)]
            yex = [pgate[:, s, :, :].rearrange("p a b -> p (a b)") for s in range(2)]
            sil = [pick[:, s, 0, :] for s in range(2)]
        with ExitStack() as st:
            gluR = sb("gluR", [P, KD, ROWS, PADW], F32, st)
            og = sb("og", [P, KD, SEQ], F32, st)
            k_t = sb("k_t", [P, KD, NT, P], F32, st)
            q_t = sb("q_t", [P, KD, 2, P], F32, st)
            v_t = sb("v_t", [P, KD, NT, P], F32, st)
            wk = sb("wk", [P, 5, T], F32, st)
            osb = mrow[:, 0:2 * P].rearrange("p (t c) -> p t c", t=2)
            gts = sb("gts", [P, 6, NT, 2, 8], F32, st)
            lvm = sb("lvm", [P, 7, P], F32, st)
            alogx = sb("alogx", [P, 1], F32, st)
            rkq = sb("rkq", [P, KD, 6], F32, st)
            onr = sb("onr", [P, 3, 2], F32, st)
            conf = x[:, :, 0:SEQ]
            wkf = wk[:, :, :].rearrange("p a b -> p (a b)")
            cpad2 = wkf[:, 0:4 * (SEQ + 2)].rearrange("p (a b c) -> p a b c", a=2, b=2)
            cacc2 = wk[:, 3:5, :]
            gsig = [rstd[:, 256 * i:256 * i + 256] for i in range(2)]
            gval = [rst64[:, 256 * i:256 * i + 256] for i in range(2)]
            csq = [wkf[:, 256 * i:256 * i + 256] for i in range(2)]
            gcb = rst64[:, :]
            albuf2 = wk[:, 0, 0:256].rearrange("p (t r) -> p t r", t=NT)
            gcT, btT, egc, ekd, egl2, beg = [gts[:, i, :, :, :] for i in range(6)]
            Lm = [hT[:, d, :] for d in range(2)]
            Um = [hT[:, 2 + d, :] for d in range(2)]
            Xm = [hT[:, 4 + d, :] for d in range(2)]
            Ym = [hT[:, 6 + d, :] for d in range(2)]
            glf = gluR[:, :, :, :].rearrange("p a b c -> p (a b c)")
            Zm = [glf[:, 512 * d:512 * d + 512] for d in range(2)]
            Bm = [glf[:, 1024 + 512 * d:1536 + 512 * d] for d in range(2)]
            kts = glf[:, 2048:2560]
            kc, dec = wk[:, 0, :], [wk[:, 2 + d, :] for d in range(2)]
            qc, qts = wk[:, 1, 0:256], wk[:, 1, 256:512]
            aqk = [wk[:, 4, 256 * d:256 * d + 256] for d in range(2)]
            kdm, vb, kbe, um, wT = Lm, Zm, Bm, Xm, Um
            grow = [rstd[:, :], small[:, :]]
            Sg = [rst128[:, P * d:P * d + P] for d in range(2)]
            vn = [rst128[:, 256 + P * d:384 + P * d] for d in range(2)]
        MOE_ORDER = [("w1", 0, 0), ("w1", 0, 1), ("w3", 0, 0), ("w3", 0, 1), ("w1", 1, 0), ("w1", 1, 1),
                     ("w3", 1, 0), ("w3", 1, 1), ("w2", 0, 0), ("w2", 1, 0), ("w2", 0, 1), ("w2", 1, 1)]

        landed = [sem(f"landed{i}") for i in range(RING)]
        w_used = sem("w_used")
        consts_in = sem("consts_in")
        consts_made = sem("consts_made")
        S = {}

        def sg(name):
            if name not in S:
                S[name] = sem(name)
            return S[name]

        block = ctx.enter_context(nc.Block())

        def prime(eng, name):
            for _ in range(2):
                eng.drain().then_inc(sg(name), 1)

        def slot(n):
            return ring[:, n % RING, :, :]

        def load_experts(sp, first, layer):
            with sp.Fori(0, Q) as q:
                for gi, (name, half, kh) in enumerate(MOE_ORDER):
                    s = (first + gi) % RING
                    sp.wait_ge(w_used, 12 * q + first + gi - RING + 1)
                    for j in range(4):
                        w = A[name][layer, bass.ds(4 * q + j, 1)].rearrange("e (k p) n -> p (e k) n", p=P)
                        sp.dma_start(ring[:, s, j, :].rearrange("p (k n) -> p k n", k=4),
                                     w[:, 4 * kh:4 * kh + 4, 512 * half:512 * half + 512]).then_inc(landed[s], 16)

        def load_group(sp, n, stage, i):
            s = n % RING
            if stage.startswith("mod"):
                layer, r = int(stage[3]), int(stage[4])
                w = A["mod_w"][layer].rearrange("(k p) n -> p k n", p=P)
                for g in range(4):
                    cb = 4 * r + g
                    sp.dma_start(ring[:, s, g, :].rearrange("p (k n) -> p k n", k=4),
                                 w[:, 4 * i:4 * i + 4, 512 * cb:512 * cb + 512]).then_inc(landed[s], 16)
            elif stage in ("gla", "ssd", "cd"):
                w = A["cd_w"] if stage == "cd" else A["ab_w"]
                base, count = {"gla": (0, 25), "ssd": (25, 20), "cd": (0, 49)}[stage]
                m = min(8, count - i)
                sp.dma_start(ring[:, s, :, :].rearrange("p a (b n) -> p (a b) n", b=2)[:, 0:m, :],
                             w[base + i:base + i + m].rearrange("c p n -> p c n")).then_inc(landed[s], 16)
            elif stage in ("about", "cdout"):
                w = A["ab_wo"] if stage == "about" else A["cd_wo"]
                sp.dma_start(ring[:, s, :, :], w[i:i + 4].rearrange("c p n -> p c n")).then_inc(landed[s], 16)

        def root_guess(act, v, y, cause, count, done):
            act.wait_ge(cause, count)
            nc.scalar.activation(y, v, ACT.Ln)
            act.drain()
            nc.scalar.activation(y, y, ACT.Exp, scale=-0.5).then_inc(done, 1)

        def root_refine(dve, y, v, t):
            nc.vector.tensor_tensor(t, y, y, ALU.mult)
            dve.drain()
            nc.vector.tensor_tensor(t, t, v, ALU.mult)
            dve.drain()
            nc.vector.tensor_scalar(t, t, -0.5, 1.5, ALU.mult, ALU.add)
            dve.drain()
            nc.vector.tensor_tensor(y, y, t, ALU.mult)
            dve.drain()

        GLA_KINDS = {"small": ("plain", False, True), "q": ("plain", False, True), "k": ("plain", False, True),
                     "v": ("plain", True, True), "r": ("silu", False, True)}
        SSD_KINDS = {"z": ("silu", False, True), "xs": ("conv", True, True), "bm": ("conv", True, True),
                     "cm": ("conv", False, True)}
        CD_KINDS = {"small": ("plain", False, True), "gb": ("gate", False, False), "ga": ("glu", False, False),
                    "og": ("silu", False, False), "q": ("conv", True, False), "k": ("conv", True, True), "v": ("conv", True, True)}
        counts = {"tile": 0, "turn": 0, "conv": 0}

        def plan(stage, tiles, kinds, bias, bias0):
            made = []
            for j, (kind, i) in enumerate(tiles):
                how, turn, both = kinds[kind]
                made.append(dict(group=rg.first[stage] + j // 8, place=j % 8, kind=kind, i=i, how=how,
                                 no=counts["tile"], last=j % 8 == 7 or j == len(tiles) - 1,
                                 turn=counts["turn"] if turn else None, conv=counts["conv"] if how == "conv" else None,
                                 c0=0 if both else SEQ, bias=col(bias, bias0 + j)))
                counts["tile"] += 1
                counts["turn"] += turn
                counts["conv"] += how == "conv"
            return made

        PLAN = {"gla": plan("gla", AB_GLA, GLA_KINDS, "ab_b", 0), "ssd": plan("ssd", AB_SSD, SSD_KINDS, "ab_b", len(AB_GLA)),
                "cd": plan("cd", CD_ALL, CD_KINDS, "cd_b", 0)}

        def conv_pad(p):
            return (cpad2 if p["group"] >= rg.first["cd"] else cpad)[:, p["conv"] % 2]

        def conv_sum(p):
            return (cacc2 if p["group"] >= rg.first["cd"] else cacc)[:, p["conv"] % 2, :]

        def turn_source(p):
            if p["kind"] == "bm":
                return bmc[:, p["i"], :]
            if p["how"] == "conv":
                return conv_sum(p)
            return e1[:, :] if p["turn"] % 2 == 0 else e3[:, :]

        conv_turn = [p["turn"] for made in PLAN.values() for p in made if p["conv"] is not None]

        def heads(ap):
            return ap.rearrange("p (c a b) -> p c a b", a=2, b=64)

        def edge(d):
            return P - 1 if d == 0 else 0

        @block.sync
        def _(sp):
            sp.dma_start(cols[:, :], A["cols"]).then_inc(consts_in, 16)
            sp.dma_start(x[:, :, :], A["xT"].rearrange("(k p) t -> p k t", p=P)).then_inc(consts_in, 16)
            for n, (stage, i, dmas) in enumerate(rg.groups):
                if stage in ("moe0", "moe1"):
                    if i == 0:
                        load_experts(sp, n, int(stage[3]))
                    continue
                if n >= RING:
                    sp.wait_ge(w_used, n - RING + 1)
                load_group(sp, n, stage, i)
            sp.wait_ge(sg("out_ready"), 1)
            sp.dma_start(out.rearrange("(k p) t -> p k t", p=P), hT[:, :, SEQ:T]).then_inc(sg("out_written"), 16)
            sp.wait_ge(sg("out_written"), 16)

        @block.tensor
        def _(pe):
            mm = nc.tensor.matmul

            def group_in(n):
                pe.wait_ge(landed[n % RING], rg.landed[n])

            def modulation(layer, r):
                first = rg.first[f"mod{layer}{r}"]
                if layer == 0 and r == 0:
                    pe.wait_ge(sg("cond_ready"), 1)
                elif (layer, r) != (1, 0):
                    pe.wait_ge(sg("mod_row_copied"), 3 * layer + r)
                for kh in range(2):
                    group_in(first + kh)
                    w = slot(first + kh).rearrange("p g (k n) -> p g k n", k=4)
                    for k in range(4):
                        for g in range(4):
                            last = mm(ps[6][32 * g:32 * g + 32, :], act_c[:, 4 * kh + k, :], w[:, g, k, :],
                                      start=(kh == 0 and k == 0), stop=(kh == 1 and k == 3),
                                      tile_position=(0, 32 * g))
                    last.then_inc(w_used, 1)
                pe.drain().then_inc(sg("mod_rows"), 1)
                pe.wait_ge(sg("mod_row_copied"), 3 * layer + r + 1)
                if layer == 0 and r == 0:
                    pe.wait_ge(sg("norm_ms"), 1)
                elif (layer, r) != (1, 0):
                    pe.wait_ge(sg("mod_added"), 3 * layer + r)
                for q in range(4):
                    nc.tensor.transpose(ps[7][:, q * P:(q + 1) * P], mrow[:, q * P:(q + 1) * P], ident[:, :])
                pe.drain().then_inc(sg("mod_turned"), 1)

            def norm(i, cw):
                pe.wait_ge(sg("norm_squares"), i + 1)
                for k in range(KD):
                    last = mm(ps[7][:, 0:cw], ones[:, :], hT[:, k, T - cw:T], start=(k == 0), stop=(k == KD - 1))
                last.then_inc(sg("norm_sums"), 1)

            def project(made, lag=2):
                for j in range(len(made) + lag):
                    if j < len(made):
                        p = made[j]
                        if p["place"] == 0:
                            group_in(p["group"])
                        if p["no"] >= 4:
                            pe.wait_ge(sg("proj_evacuated"), p["no"] - 3)
                        w = slot(p["group"]).rearrange("p a (b k c) -> p (a b) k c", b=2, k=KD)[:, p["place"]]
                        for k in range(KD):
                            last = mm(ps[p["no"] % 4][:, p["c0"]:T], w[:, k, :], hT[:, k, p["c0"]:T],
                                      start=(k == 0), stop=(k == KD - 1))
                        last.then_inc(sg("proj_done"), 1)
                        if p["last"]:
                            pe.drain().then_inc(w_used, 1)
                    if j >= lag and made[j - lag]["turn"] is not None:
                        p = made[j - lag]
                        m = p["turn"]
                        pe.wait_ge(sg("turn_ready"), m + 1)
                        if m >= 2:
                            pe.wait_ge(sg("turn_copied"), m - 1)
                        src = turn_source(p)
                        for t in range(p["c0"] // P, NT):
                            last = nc.tensor.transpose(ps[4 + m % 2][:, t * P:(t + 1) * P], src[:, t * P:(t + 1) * P], ident[:, :])
                        last.then_inc(sg("turn_done"), 1)

            def gla():
                with pe.Fori(0, GH) as h:
                    for d in range(2):
                        n = 2 * h + d
                        pe.wait_ge(sg("gla_w2"), n + 1)
                        pe.wait_ge(sg("gla_kdt"), n)
                        if d == 0:
                            pe.wait_ge(sg("head_mixed"), h)
                        mm(ps[0][:, :], w2s[:, :], small[:, :], start=True, stop=True).then_inc(sg("gla_gz"), 1)
                        pe.wait_ge(sg("gla_gated"), n + 1)
                        pe.wait_ge(sg("gla_masked"), n)
                        for t in range(NT):
                            nc.tensor.transpose(ps[0][:, t * P:(t + 1) * P], kk[:, 1, t * P:(t + 1) * P], ident[:, :])
                        for t in range(NT):
                            tt = slice(t * P, (t + 1) * P)
                            last = mm(ps[1][:, tt], kk[:, 0, tt], qg[:, tt], start=True, stop=True, skip_group_check=True)
                        last.then_inc(sg("gla_att"), 1)
                        pe.wait_ge(sg("gla_kdt"), n + 1)
                        pe.wait_ge(sg("gla_S"), n)
                        for c in range(NC):
                            last = mm(ps[2 + c // 2][:, 256 * (c % 2):256 * (c % 2) + 256], kdt[:, c // 2, c % 2, :],
                                      g_v[:, bass.ds(2 * h, 2), c // 2, :], start=True, stop=True, skip_group_check=True)
                        last.then_inc(sg("gla_kv"), 1)
                        pe.wait_ge(sg("gla_masked"), n + 1)
                        if d == 0:
                            pe.wait_ge(sg("head_normed"), h)
                        for t in range(NT):
                            mm(ps[6 + t // 2][:, 256 * (t % 2):256 * (t % 2) + 256], attm[:, d, t, :],
                               g_v[:, bass.ds(2 * h, 2), t, :], start=(d == 0 and t % 2 == 0), stop=False, skip_group_check=True)
                        pe.wait_ge(sg("gla_S"), n + 1)
                        for c in range(NC):
                            if c == (0 if d == 0 else 3):
                                continue
                            b = 64 * (c % 2)
                            last = mm(ps[6 + c // 4][b:b + 64, 256 * (c // 2 % 2):256 * (c // 2 % 2) + 256],
                                      qg[:, 64 * c:64 * c + 64], sS[:, c, :], start=False, stop=True, skip_group_check=True,
                                      tile_position=(0, b))
                        last.then_inc(sg("gla_o"), 1)
                    pe.wait_ge(sg("head_normed"), h + 1)
                    for e in range(2):
                        for t in range(NT):
                            last = nc.tensor.transpose(ps[e][:, t * P:(t + 1) * P],
                                                       kk[:, t // 2, (t % 2) * 256 + e * P:(t % 2) * 256 + e * P + P], ident[:, :])
                    last.then_inc(sg("head_turned"), 1)

            def ssd_gates():
                pe.wait_ge(sg("gate_cums"), 1)
                for t in range(NT):
                    nc.tensor.transpose(ps[0][:, t * P:(t + 1) * P], dtc[:, t * P:(t + 1) * P], ident[:, :])
                    nc.tensor.transpose(ps[1][:, t * P:(t + 1) * P], ac[:, t * P:(t + 1) * P], ident[:, :])
                mm(ps[2][:, 0:256], ones[:, :], albuf[:, :, :], start=True, stop=True).then_inc(sg("gate_cums_turned"), 1)

            def ssd():
                prime(pe, "ssd_bc")
                prime(pe, "ssd_y")
                for g in range(2):
                    if g:
                        pe.wait_ge(sg("ssd_cbm"), g)
                    for t in range(NT):
                        tt = slice(t * P, (t + 1) * P)
                        last = mm(ps[4][:, tt], bmc[:, g, tt], cmc[:, g, tt], start=True, stop=True, skip_group_check=True)
                    last.then_inc(sg("ssd_cb"), 1)
                    for d in range(2):
                        n = 2 * g + d
                        order = [0, 1, 2, 3] if d == 0 else [1, 0, 3, 2]
                        for i in range(3):
                            pe.wait_ge(sg("ssd_wv"), 3 * n + i + 1)
                            if 3 * n + i:
                                pe.wait_ge(sg("ssd_state"), 3 * n + i)
                            mm(ps[5][:, :], bm_t[:, g, order[i], :], wv[:, :], start=True, stop=True).then_inc(sg("ssd_kv"), 1)
                        for i in range(3):
                            t = order[i + 1]
                            pe.wait_ge(sg("ssd_state"), 3 * n + i + 1)
                            if 3 * n + i >= 2:
                                pe.wait_ge(sg("ssd_inter_added"), 3 * n + i - 1)
                            mm(ps[6 + i % 2][:, :], cmc[:, g, t * P:(t + 1) * P], s_in[:, i, :], start=True, stop=True).then_inc(sg("ssd_inter"), 1)
                        if n == 0:
                            pe.wait_ge(sg("gate_gap"), 1)
                        def decays(k, hp):
                            pe.wait_ge(sg("ssd_row"), k + 1)
                            pe.wait_ge(sg("ssd_decay"), k - 1)
                            mm(ps[hp][:, :], ones[:, :], row[hp], start=True, stop=False)
                            mm(ps[hp][:, :].rearrange("p (t i) -> p t i", t=NT), identb[:, :], m_far[:, d:d + 1, :].broadcast_to([P, NT, P]),
                               start=False, stop=True).then_inc(sg("ssd_bc"), 1)

                        def outputs(k, hp, tile):
                            pe.wait_ge(sg("ssd_mat"), k + 1)
                            pe.wait_ge(sg("ssd_y_added"), k - 1)
                            for t in range(NT):
                                last = mm(ps[2 + hp][:, P * t:P * t + P], mat[hp][:, t * P:(t + 1) * P], tile(t),
                                          start=True, stop=True, skip_group_check=True)
                            last.then_inc(sg("ssd_y"), 1)

                        k0 = 8 * n + 2
                        for hp in range(2):
                            decays(k0 + hp, hp)
                        with pe.Fori(0, 3) as pair:
                            for hp in range(2):
                                outputs(k0 + 2 * pair + hp, hp, lambda t: xs_t[:, bass.ds(pair + 4 * g, 1), t, :])
                                decays(k0 + 2 * pair + 2 + hp, hp)
                        for hp in range(2):
                            outputs(k0 + 6 + hp, hp, lambda t: xs_t[:, 4 * g + 3, t, :])
                pe.wait_ge(sg("ssd_pass"), 4)
                for c in range(8):
                    if c >= 4:
                        pe.wait_ge(sg("ssd_gated"), c - 3)
                    for t in range(NT):
                        last = nc.tensor.transpose(ps[c % 4][:, t * P:(t + 1) * P], ysb[:, t, c * P:(c + 1) * P], ident[:, :])
                    last.then_inc(sg("ssd_turned"), 1)
                for g in range(2):
                    pe.wait_ge(sg("ssd_squares"), g + 1)
                    for c in range(4):
                        last = mm(ps[4 + g][:, :], ones[:, :], x[:, c, :], start=(c == 0), stop=(c == 3))
                    last.then_inc(sg("ssd_sums"), 1)

            def conformer_norm():
                for r in range(2):
                    for k in range(KD):
                        if r == 0:
                            if k == 0:
                                pe.wait_ge(sg("conf_ready"), 1)
                            rhs = conf[:, k, :]
                        else:
                            pe.wait_ge(sg("conf_squares"), k + 1)
                            rhs = csq[k % 2]
                        last = mm(ps[6 + r][:, 0:SEQ], ones[:, :], rhs, start=(k == 0), stop=(k == KD - 1))
                        if r == 1:
                            last.then_inc(sg("conf_sq_used"), 1)
                    pe.drain().then_inc(sg("conf_sums"), 1)

            def gdn_gates():
                pe.wait_ge(sg("gate_cums"), 2)
                for t in range(NT):
                    nc.tensor.transpose(ps[0][:, t * P:(t + 1) * P], gcb[:, t * P:(t + 1) * P], ident[:, :])
                mm(ps[1][:, 0:256], ones[:, :], albuf2, start=True, stop=True).then_inc(sg("gate_cums_turned"), 1)

            def gdn():
                tiles = [slice(t * P, (t + 1) * P) for t in range(NT)]
                with pe.Fori(0, KD) as h:
                    pe.wait_ge(sg("gdn_ktq"), h + 1)
                    pe.wait_ge(sg("head_mixed"), GH + h)
                    for t in range(NT):
                        nc.tensor.transpose(ps[0][:, tiles[t]], kts[:, tiles[t]], ident[:, :])
                    for t in range(2):
                        last = nc.tensor.transpose(ps[1][:, tiles[t]], qts[:, tiles[t]], ident[:, :])
                    last.then_inc(sg("gdn_kT"), 1)
                    for d in range(2):
                        pe.wait_ge(sg("gdn_row"), 2 * h + d + 1)
                        mm(ps[4 + d][:, :], ones[:, :], grow[d], start=True, stop=True).then_inc(sg("gdn_bc"), 1)
                    pe.wait_ge(sg("gdn_kc"), h + 1)
                    for t in range(NT):
                        mm(ps[2][:, tiles[t]], kc[:, tiles[t]], kc[:, tiles[t]], start=True, stop=True, skip_group_check=True)
                    for t in range(2):
                        last = mm(ps[3][:, tiles[t]], kc[:, tiles[2 + t]], qc[:, tiles[t]], start=True, stop=True, skip_group_check=True)
                    last.then_inc(sg("gdn_kk"), 1)
                    for d in range(2):
                        pe.wait_ge(sg("gdn_L"), 2 * h + d + 1)
                        for t in range(NT):
                            last = nc.tensor.transpose(ps[6 + d][:, tiles[t]], Lm[d][:, tiles[t]], ident[:, :])
                        last.then_inc(sg("gdn_U"), 1)
                    for l in range(6):
                        for d in range(2):
                            pe.wait_ge(sg("gdn_xy"), 14 * h + 2 * l + d + 1)
                            pe.wait_ge(sg("gdn_bt"), 12 * h + 2 * l + d + 1)
                            for t in range(NT):
                                last = mm(ps[3 * d][:, tiles[t]], Bm[d][:, tiles[t]], Xm[d][:, tiles[t]], start=True, stop=True, skip_group_check=True)
                            last.then_inc(sg("gdn_z"), 1)
                        for d in range(2):
                            pe.wait_ge(sg("gdn_zc"), 12 * h + 2 * l + d + 1)
                            for t in range(NT):
                                last = mm(ps[3 * d + 2][:, tiles[t]], Zm[d][:, tiles[t]], Ym[d][:, tiles[t]], start=True, stop=True, skip_group_check=True)
                            if l < 5:
                                for t in range(NT):
                                    last = mm(ps[3 * d + 1][:, tiles[t]], Ym[d][:, tiles[t]], Zm[d][:, tiles[t]], start=True, stop=True, skip_group_check=True)
                            last.then_inc(sg("gdn_p"), 1)
                    for d in range(2):
                        pe.wait_ge(sg("gdn_xy"), 14 * h + 12 + d + 1)
                        pe.wait_ge(sg("gdn_rhs"), 2 * h + d + 1)
                        for t in range(NT):
                            mm(ps[3 * d][:, tiles[t]], Ym[d][:, tiles[t]], vb[d][:, tiles[t]], start=True, stop=True, skip_group_check=True)
                        for t in range(NT):
                            last = mm(ps[3 * d + 1][:, tiles[t]], kbe[d][:, tiles[t]], Ym[d][:, tiles[t]], start=True, stop=True, skip_group_check=True)
                        last.then_inc(sg("gdn_uw"), 1)
                    for i in range(NT):
                        for d in range(2):
                            t = (0, 1, 2, 3)[i] if d == 0 else (1, 0, 3, 2)[i]
                            bank = ps[3 * d + 2]
                            if i > 0:
                                pe.wait_ge(sg("gdn_S"), 6 * h + 2 * (i - 1) + d + 1)
                                if i == 1:
                                    pe.wait_ge(sg("gdn_uwc"), 2 * h + d + 1)
                                mm(bank[:, 0:P], wT[d][:, tiles[t]], Sg[d], start=True, stop=True, skip_group_check=True).then_inc(sg("gdn_ws"), 1)
                            if t >= 2:
                                mm(ps[7][:, (2 * d + t - 2) * P:(2 * d + t - 1) * P], qc[:, tiles[t - 2]], Sg[d], start=True, stop=True, skip_group_check=True)
                        for d in range(2):
                            t = (0, 1, 2, 3)[i] if d == 0 else (1, 0, 3, 2)[i]
                            bank = ps[3 * d + 2]
                            pe.wait_ge(sg("gdn_vn"), 8 * h + 2 * i + d + 1)
                            if i < 3:
                                mm(bank[:, P:2 * P], kdm[d][:, tiles[t]], vn[d], start=True, stop=True, skip_group_check=True).then_inc(sg("gdn_kv"), 1)
                            if t >= 2:
                                last = mm(ps[6][:, (t - 2) * P:(t - 1) * P], aqk[d][:, tiles[t - 2]], vn[d],
                                          start=(i == 2 and d == 0), stop=True, skip_group_check=True)
                    last.then_inc(sg("gdn_o"), 1)
                    pe.wait_ge(sg("head_normed"), GH + h + 1)
                    for t in range(2):
                        last = nc.tensor.transpose(ps[1][:, tiles[t]], osb[:, t, :], ident[:, :])
                    last.then_inc(sg("head_turned"), 1)

            def out_projection(stage, layer, mixed, c0):
                for c in range(8):
                    n = rg.first[stage] + c // 4
                    if c % 4 == 0:
                        group_in(n)
                    k0 = 8 * layer + c
                    if k0 >= 4:
                        pe.wait_ge(sg("out_scaled"), k0 - 3)
                    w = slot(n)[:, c % 4, :].rearrange("p (k c) -> p k c", k=16)
                    for k in range(16):
                        last = mm(ps[c % 4][:, c0:T], w[:, k, :], mixed(k), start=(k == 0), stop=(k == 15))
                    last.then_inc(sg("out_done"), 1)
                    if c % 4 == 3:
                        pe.drain().then_inc(w_used, 1)

            def route(layer, streams):
                tiles = [t for t in range(NT) if t // 2 in streams]
                pe.wait_ge(sg("router_in"), 16 * (layer + 1))
                for t in tiles:
                    for k in range(KD):
                        last = mm(ps[0][:, E * t:E * t + E], hT[:, k, t * P:(t + 1) * P], router[:, k, :],
                                  start=(k == 0), stop=(k == KD - 1), skip_group_check=True)
                last.then_inc(sg("logits"), 1)
                for i, t in enumerate(tiles):
                    for half in range(2):
                        m = 2 * i + half + 8 * layer
                        if i >= 1:
                            pe.wait_ge(sg("htok_copied"), m - 1)
                        for k in range(4):
                            last = nc.tensor.transpose(ps[1 + half][:, k * P:(k + 1) * P],
                                                       hT[:, 4 * half + k, t * P:(t + 1) * P], ident[:, :])
                        last.then_inc(sg("htok_turned"), 1)
                pe.wait_ge(sg("affinities"), 2 * layer + 1)
                for tt in range(2):
                    last = nc.tensor.transpose(ps[3][0:48, tt * P:(tt + 1) * P], affc[:, tt, :], ident[:, :])
                last.then_inc(sg("aff_turned"), 1)
                pe.wait_ge(sg("affinities"), 2 * layer + 2)
                for tt in range(2):
                    last = nc.tensor.transpose(ps[4][:, 48 * tt:48 * tt + 48], pickw[:, 1, tt * P:(tt + 1) * P], ident[0:48, 0:48])
                last.then_inc(sg("aff_turned"), 1)
                pe.wait_ge(sg("picks"), 2 * layer + 1)
                pe.wait_ge(sg("htok_copied"), 8 * layer + 2 * len(tiles))
                g = 16 * layer
                for s in streams:
                    for k in range(KD):
                        if g >= 4:
                            pe.wait_ge(sg("gathered_copied"), g - 3)
                        for tt in range(2):
                            last = mm(ps[4 + g % 4][:, :], htok[:, 2 * s + tt, k * P:(k + 1) * P], pick[:, s, tt, :],
                                      start=(tt == 0), stop=(tt == 1))
                        last.then_inc(sg("gathered"), 1)
                        g += 1
                pe.wait_ge(sg("picks"), 2 * layer + 2)
                for i, s in enumerate(streams):
                    for half in range(2):
                        for q in range(2):
                            for tt in range(2):
                                last = nc.tensor.transpose(ps[2 * (i % 2) + half][:, 256 * q + P * tt:256 * q + P * tt + P],
                                                           pgate[:, s, tt, (2 * half + q) * P:(2 * half + q + 1) * P], ident[:, :])
                        last.then_inc(sg("gates_turned"), 1)

            def experts(layer, streams):
                first = rg.first[f"moe{layer}"]
                q0 = Q * layer
                with pe.Fori(0, Q) as q:
                    pe.wait_ge(sg("moe_xg"), q + q0 + 1)

                    def weights(gi):
                        s = (first + gi) % RING
                        pe.wait_ge(landed[s], q * 256 + rg.landed[first + gi])
                        return ring[:, s, :, :].rearrange("p j (k n) -> p j k n", k=4)

                    def product(gi, kh, lhs, banks):
                        w = weights(gi)
                        for k in range(4):
                            for s in streams:
                                for j in range(4):
                                    last = mm(ps[banks + s][32 * j:32 * j + 32, :], lhs[s][:, 4 * kh + k, 32 * j:32 * j + 32],
                                              w[:, j, k, :], start=(kh == 0 and k == 0), stop=(kh == 1 and k == 3),
                                              tile_position=(0, 32 * j))
                        last.then_inc(w_used, 1)

                    def turn(hf, bank):
                        pe.wait_ge(sg("moe_hid"), 2 * q + 2 * q0 + hf + 1)
                        for s in streams:
                            for b in range(4):
                                last = nc.tensor.transpose(ps[bank + s][:, b * P:(b + 1) * P],
                                                           hid[s][:, 512 * hf + b * P:512 * hf + b * P + P], ident[:, :])
                        last.then_inc(sg("moe_turned"), 1)

                    for hf in range(2):
                        n = 2 * q + 2 * q0 + hf
                        if hf == 0:
                            pe.wait_ge(sg("moe_tcopied"), n)
                        pe.wait_ge(sg("moe_silu"), n)
                        product(4 * hf, 0, xg, 0)
                        product(4 * hf + 1, 1, xg, 0)
                        pe.drain().then_inc(sg("moe_h1"), 1)
                        if hf == 1:
                            turn(0, 5)
                        pe.wait_ge(sg("moe_ycopied"), 2 * q + 2 * q0)
                        pe.wait_ge(sg("moe_hid"), n)
                        product(4 * hf + 2, 0, xg, 2)
                        product(4 * hf + 3, 1, xg, 2)
                        pe.drain().then_inc(sg("moe_h3"), 1)
                    pe.wait_ge(sg("moe_tcopied"), 2 * q + 2 * q0 + 1)
                    product(8, 0, hidT, 5)
                    turn(1, 0)
                    product(9, 0, hidT, 2)
                    pe.wait_ge(sg("moe_tcopied"), 2 * q + 2 * q0 + 2)
                    product(10, 1, hidT, 5)
                    pe.drain().then_inc(sg("moe_y"), 1)
                    product(11, 1, hidT, 2)
                    pe.drain().then_inc(sg("moe_y"), 1)
                    for dt in range(KD):
                        if dt % 4 == 0:
                            pe.wait_ge(sg("moe_ycopied"), 2 * q + 2 * q0 + dt // 4 + 1)
                        if dt >= 2:
                            pe.wait_ge(sg("moe_added"), 8 * q + 8 * q0 + dt - 1)
                        for s in streams:
                            last = mm(ps[7 if dt % 2 else 4][:, 256 * s:256 * s + 256], yex[s][:, dt * P:(dt + 1) * P],
                                      gateT[:, s, bass.ds(q, 1), :], start=True, stop=True, skip_group_check=True)
                        last.then_inc(sg("moe_sum"), 1)

            pe.wait_ge(consts_made, 1)
            norm(0, T)
            for r in range(3):
                modulation(0, r)
            pe.wait_ge(sg("h_ready"), 1)
            project(PLAN["gla"])
            pe.wait_ge(sg("gla_zeroed"), 1)
            gla()
            pe.wait_ge(sg("head_mixed"), GH)
            modulation(1, 0)
            project(PLAN["ssd"])
            modulation(1, 1)
            modulation(1, 2)
            ssd_gates()
            ssd()
            pe.wait_ge(sg("ssd_mixed"), 2)
            out_projection("about", 0, lambda k: (mixA if k < 8 else zmix)[:, k % 8, :], 0)
            norm(1, T)
            pe.wait_ge(sg("h_ready"), 2)
            route(0, (0, 1))
            pe.wait_ge(sg("routed"), 1)
            experts(0, (0, 1))
            pe.wait_ge(sg("x_ready"), 2)
            norm(2, T)
            pe.wait_ge(sg("h_ready"), 3)
            project(PLAN["cd"])
            conformer_norm()
            gdn_gates()
            gdn()
            pe.wait_ge(sg("head_mixed"), GH + KD)
            pe.wait_ge(sg("conf_done"), 1)
            out_projection("cdout", 1, lambda k: conf[:, k, :] if k < 8 else og[:, k - 8, :], SEQ)
            norm(3, SEQ)
            pe.wait_ge(sg("h_ready"), 4)
            route(1, (1,))
            pe.wait_ge(sg("routed"), 2)
            experts(1, (1,))
            norm(4, SEQ)

        @block.scalar
        def _(act):
            A_ = nc.scalar.activation

            def conditioning():
                act.wait_ge(sg("cond_zeroed"), 1)
                A_(act_c[:, :, 0:2], col("cvec", 0, 16).rearrange("p (s k) -> p k s", s=2), ACT.Silu).then_inc(sg("cond_ready"), 1)

            def modulation(layer, r):
                act.wait_ge(sg("mod_rows"), 3 * layer + r + 1)
                if 3 * layer + r:
                    act.wait_ge(sg("mod_turned"), 3 * layer + r)
                A_(mrow[:, :], ps[6][:, :], ACT.Copy).then_inc(sg("mod_row_copied"), 1)

            def norm(i, layer, which, cw):
                if i == 0:
                    act.wait_ge(consts_in, 64)
                else:
                    act.wait_ge(sg("x_ready"), i)
                A_(hT[:, :, T - cw:T], x[:, :, T - cw:T], ACT.Square).then_inc(sg("norm_squares"), 1)
                act.wait_ge(sg("norm_ms"), i + 1)
                A_(rstd[:, T - cw:T], rstd[:, T - cw:T], ACT.Sqrt).then_inc(sg("norm_root"), 1)
                if i == 0:
                    for r in range(3):
                        modulation(0, r)
                if layer is None:
                    return
                act.wait_ge(sg("afac_ready"), layer + 1)
                for k in range(KD):
                    act.wait_ge(sg("norm_scaled"), 8 * i + k + 1)
                    for s in range(2):
                        if s == 0 and cw < T:
                            continue
                        cc = slice(s * SEQ, (s + 1) * SEQ)
                        last = A_(hT[:, k, cc], hT[:, k, cc], ACT.Identity, bias=mod(layer, 3 * which, k, s),
                                  scale=afac[:, layer, which, k, s:s + 1])
                last.then_inc(sg("h_ready"), 1)

            def project(made, dest, conv_bias=None):
                def finish_conv(p):
                    c = p["conv"]
                    act.wait_ge(sg("conv_done"), c + 1)
                    to = conv_sum(p)[:, p["c0"]:T] if dest(p) is None else dest(p)
                    A_(to, conv_sum(p)[:, p["c0"]:T], ACT.Silu, bias=conv_bias(p)).then_inc(sg("conv_silu"), 1)
                    if p["turn"] is not None:
                        act.drain().then_inc(sg("turn_ready"), 1)

                waiting = None
                for p in made:
                    bank, c0 = ps[p["no"] % 4], p["c0"]
                    act.wait_ge(sg("proj_done"), p["no"] + 1)
                    if p["how"] == "conv":
                        c = p["conv"]
                        if c >= 2:
                            act.wait_ge(sg("conv_done"), c - 1)
                        s0 = c0 // SEQ
                        if p["group"] >= rg.first["cd"]:
                            act.wait_ge(sg("conv_pads"), 2)
                        A_(conv_pad(p)[:, s0:2, 1:SEQ + 1], bank[:, c0:T].rearrange("p (s t) -> p s t", t=SEQ), ACT.Identity,
                           bias=p["bias"]).then_inc(sg("proj_evacuated"), 1)
                        act.drain().then_inc(sg("conv_in"), 1)
                    elif p["how"] in ("gate", "glu"):
                        i = p["i"]
                        if i >= 2:
                            act.wait_ge(sg("glu_done"), i - 1)
                        A_(gsig[i % 2] if p["how"] == "gate" else gval[i % 2], bank[:, SEQ:T],
                           ACT.Sigmoid if p["how"] == "gate" else ACT.Identity, bias=p["bias"]).then_inc(sg("proj_evacuated"), 1)
                        if p["how"] == "glu":
                            act.drain().then_inc(sg("glu_in"), 1)
                    elif p["turn"] is not None:
                        if p["turn"] >= 2:
                            act.wait_ge(sg("turn_done"), p["turn"] - 1)
                        A_(turn_source(p), bank[:, :], ACT.Identity, bias=p["bias"]).then_inc(sg("proj_evacuated"), 1)
                        act.drain().then_inc(sg("turn_ready"), 1)
                    else:
                        A_(dest(p), bank[:, c0:T], ACT.Silu if p["how"] == "silu" else ACT.Identity,
                           bias=p["bias"]).then_inc(sg("proj_evacuated"), 1)
                    if waiting is not None:
                        finish_conv(waiting)
                    waiting = p if p["how"] == "conv" else None
                if waiting is not None:
                    finish_conv(waiting)

            def conformer_norm():
                for k in range(KD):
                    act.wait_ge(sg("conf_centered"), k + 1)
                    if k >= 2:
                        act.wait_ge(sg("conf_sq_used"), k - 1)
                    A_(csq[k % 2], conf[:, k, :], ACT.Square).then_inc(sg("conf_squares"), 1)
                act.wait_ge(sg("root_in"), 3)
                A_(rstd[:, 0:SEQ], rstd[:, 0:SEQ], ACT.Sqrt).then_inc(sg("root_out"), 1)
                for k in range(KD):
                    act.wait_ge(sg("conf_scaled"), k + 1)
                    A_(conf[:, k, :], conf[:, k, :], ACT.Silu, bias=col("conf_bb", k), scale=col("conf_g", k))
                act.drain().then_inc(sg("conf_done"), 1)

            def gdn_gates():
                act.wait_ge(sg("root_in"), 4)
                A_(rkq[:, :, :], rkq[:, :, :], ACT.Sqrt).then_inc(sg("root_out"), 1)
                act.wait_ge(sg("sp_abs"), 2)
                A_(gcb[64:128, :], small[64:128, :], ACT.Sigmoid)
                A_(Um[0][0:64, :], Um[0][0:64, :], ACT.Exp, scale=-1.0).then_inc(sg("sp_u"), 1)
                A_(alogx[0:64, :], cols[0:64, COL_AT["gdn_alog"]:COL_AT["gdn_alog"] + 1], ACT.Exp)
                act.wait_ge(sg("sp_w"), 2)
                A_(Xm[0][0:64, :], Ym[0][0:64, :], ACT.Ln).then_inc(sg("sp_ln"), 1)
                act.wait_ge(sg("gate_gap"), 2)
                A_(egl2, egl2, ACT.Exp)
                A_(egc, gcT, ACT.Exp)
                A_(ekd, ekd, ACT.Exp).then_inc(sg("gate_exps"), 1)

            def gdn():
                with act.Fori(0, KD) as h:
                    act.wait_ge(sg("gdn_kT"), h + 1)
                    act.wait_ge(sg("gdn_o"), h)
                    A_(kc, ps[0][:, :], ACT.Copy)
                    A_(qc, ps[1][:, 0:SEQ], ACT.Copy).then_inc(sg("gdn_kc"), 1)
                    for d in range(2):
                        act.wait_ge(sg("gdn_gaps"), 2 * h + d + 1)
                        A_(dec[d], dec[d], ACT.Exp, scale=-1.0)
                        A_(aqk[d], aqk[d], ACT.Exp).then_inc(sg("gdn_decay"), 1)
                    for d in range(2):
                        act.wait_ge(sg("gdn_U"), 2 * h + d + 1)
                        A_(Um[d], ps[6 + d][:, :], ACT.Copy).then_inc(sg("gdn_Uc"), 1)
                    for l in range(6):
                        for d in range(2):
                            act.wait_ge(sg("gdn_z"), 12 * h + 2 * l + d + 1)
                            A_(Zm[d], ps[3 * d][:, :], ACT.Copy).then_inc(sg("gdn_zc"), 1)
                    for d in range(2):
                        act.wait_ge(sg("gdn_uw"), 2 * h + d + 1)
                        A_(um[d], ps[3 * d][:, :], ACT.Copy)
                        A_(wT[d], ps[3 * d + 1][:, :], ACT.Copy).then_inc(sg("gdn_uwc"), 1)
                    act.wait_ge(sg("gdn_osum"), h + 1)
                    for t in range(2):
                        last = A_(dec[0][:, t * P:(t + 1) * P], osb[:, t, :], ACT.Square, accum_out=onr[:, 0, t:t + 1])
                    last.then_inc(sg("head_squares"), 1)
                    root_guess(act, onr[:, 0, :], onr[:, 1, :], sg("head_ms"), GH + h + 1, sg("head_guess"))

            def out_projection(layer, streams):
                act.wait_ge(sg("out_bias"), layer + 1)
                for c in range(8):
                    act.wait_ge(sg("out_done"), 8 * layer + c + 1)
                    if 8 * layer + c >= 2:
                        act.wait_ge(sg("out_added"), 8 * layer + c - 1)
                    for s in streams:
                        cc = slice(s * SEQ, (s + 1) * SEQ)
                        last = A_(hT[:, c % 2, cc], ps[c % 4][:, cc], ACT.Identity, bias=gbias[:, c, s:s + 1], scale=mod(layer, 2, c, s))
                    last.then_inc(sg("out_scaled"), 1)

            def route(layer, streams):
                n = 2 * len(streams)
                for m in range(2 * n):
                    t = (NT - n) + m // 2
                    act.wait_ge(sg("htok_turned"), 8 * layer + m + 1)
                    A_(htok[:, t, 512 * (m % 2):512 * (m % 2) + 512], ps[1 + m % 2][:, :], ACT.Copy).then_inc(sg("htok_copied"), 1)
                    if m == 1:
                        act.wait_ge(sg("logits_shifted"), layer + 1)
                        A_(aff[:, NT - n:NT, :], aff[:, NT - n:NT, :], ACT.Exp).then_inc(sg("aff_exp"), 1)
                g = 16 * layer
                for s in streams:
                    for k in range(KD):
                        act.wait_ge(sg("gathered"), g + 1)
                        A_(xe[:, s, k, :], ps[4 + g % 4][:, :], ACT.Copy).then_inc(sg("gathered_copied"), 1)
                        g += 1
                act.drain().then_inc(sg("xe_ready"), 1)

            def experts(layer, streams):
                q0 = Q * layer
                with act.Fori(0, Q) as q:
                    n = 2 * q + 2 * q0
                    for hf in range(2):
                        act.wait_ge(sg("moe_h1"), n + hf + 1)
                        act.wait_ge(sg("moe_hid"), n + hf)
                        for s in streams:
                            last = A_(sil[s], ps[s][:, :], ACT.Silu)
                        last.then_inc(sg("moe_silu"), 1)
                    for hf in range(2):
                        act.wait_ge(sg("moe_turned"), n + hf + 1)
                        for s in streams:
                            last = A_(hidT[s][:, 4 * hf:4 * hf + 4, :], ps[(5 if hf == 0 else 0) + s][:, :].rearrange("p (b c) -> p b c", b=4), ACT.Copy)
                        last.then_inc(sg("moe_tcopied"), 1)
                    for hd in range(2):
                        act.wait_ge(sg("moe_y"), n + hd + 1)
                        act.wait_ge(sg("moe_sum"), 8 * q + 8 * q0)
                        for s in streams:
                            last = A_(yex[s][:, 512 * hd:512 * hd + 512], ps[(5 if hd == 0 else 2) + s][:, :], ACT.Copy)
                        last.then_inc(sg("moe_ycopied"), 1)

            def ssd_gates():
                act.wait_ge(sg("sp_abs"), 1)
                A_(sp_u[64:128, :], sp_u[64:128, :], ACT.Exp, scale=-1.0).then_inc(sg("sp_u"), 1)
                A_(alog_e[64:128, :], cols[64:128, COL_AT["ssd_alog"]:COL_AT["ssd_alog"] + 1], ACT.Exp)
                act.wait_ge(sg("sp_w"), 1)
                A_(sp_l[64:128, :], sp_w[64:128, :], ACT.Ln).then_inc(sg("sp_ln"), 1)
                modulation(1, 1)
                modulation(1, 2)
                act.wait_ge(sg("gate_gap"), 1)
                A_(eal[:, :, :], ps[2][:, 0:256].rearrange("p (t r) -> p t r", t=NT), ACT.Exp)
                A_(cdec[:, :, :], acT[:, :, :], ACT.Exp)
                A_(dtw[:, :, :], dtw[:, :, :], ACT.Exp).then_inc(sg("gate_exps"), 1)

            def ssd():
                prime(act, "ssd_decay")
                for g in range(2):
                    for d in range(2):
                        n = 2 * g + d
                        with act.Fori(0, 4) as pair:
                            for hp in range(2):
                                k = 8 * n + 2 + 2 * pair + hp
                                act.wait_ge(sg("ssd_bc"), k + 1)
                                act.wait_ge(sg("ssd_mat"), k - 1)
                                for t in range(NT):
                                    last = A_(seg[hp][:, t * P:t * P + P], ps[hp][:, t * P:t * P + P], ACT.Exp,
                                              bias=nacT[:, t, bass.ds(2 * pair + 32 * d + 8 * g + hp, 1)])
                                last.then_inc(sg("ssd_decay"), 1)
                for g in range(2):
                    act.wait_ge(sg("ssd_gated"), 4 * g + 4)
                    A_(x[:, 0:4, :], zmix[:, 4 * g:4 * g + 4, :], ACT.Square).then_inc(sg("ssd_squares"), 1)
                    act.wait_ge(sg("root_in"), g + 1)
                    A_(rstd[:, :], rstd[:, :], ACT.Sqrt).then_inc(sg("root_out"), 1)

            def gla():
                with act.Fori(0, GH) as h:
                    for d in range(2):
                        n = 2 * h + d
                        w = w2p[:, bass.ds(h + 4 * d, 1), :].rearrange("p a c -> p (a c)")
                        act.wait_ge(sg("gla_gz"), n)
                        A_(w2s[:, :], w, ACT.Copy).then_inc(sg("gla_w2"), 1)
                        act.wait_ge(sg("gla_gz"), n + 1)
                        act.wait_ge(sg("gla_gated"), n)
                        A_(e1[:, :], ps[0][:, :], ACT.Identity, bias=cols[:, bass.ds(h + COL_AT["gla_bg"] + 4 * d, 1)]).then_inc(sg("gla_z"), 1)
                        act.wait_ge(sg("gla_absz"), n + 1)
                        A_(gcum[:, :], gcum[:, :], ACT.Exp, scale=-1.0)
                        act.drain()
                        A_(e1[:, :], gcum[:, :], ACT.Ln, bias=1.0).then_inc(sg("gla_lnz"), 1)
                        act.wait_ge(sg("gla_scanned"), n + 1)
                        A_(e1[:, :], gcum[:, :], ACT.Exp, scale=1.0 / 16)
                        A_(kk[:, 0, :], gcum[:, :], ACT.Exp, scale=-1.0 / 16).then_inc(sg("gla_exps"), 1)
                        act.wait_ge(sg("gla_gap"), n + 1)
                        A_(e3[:, :], e3[:, :], ACT.Exp, scale=1.0 / 16)
                        g3 = gcum[:, :].rearrange("p (c j) -> p c j", j=CH)
                        A_(egl[:, :], g3[:, :, CH - 1 if d == 0 else 0], ACT.Exp, scale=1.0 / 16).then_inc(sg("gla_e3"), 1)
                        act.wait_ge(sg("gla_att"), n + 1)
                        src = ps[0][:, :].rearrange("p (t d) -> p t d", t=NT)
                        A_(kdt[0:64, :, 0, :], src[0:64], ACT.Copy)
                        A_(kdt[64:128, :, 1, :], src[64:128], ACT.Copy).then_inc(sg("gla_kdt"), 1)
                    act.wait_ge(sg("gla_o"), 2 * h + 2)
                    for t in range(NT):
                        last = A_(sS[:, t, :], ps[6 + t // 2][:, 256 * (t % 2):256 * (t % 2) + 256], ACT.Square,
                                  accum_out=ssq[:, t:t + 1])
                    last.then_inc(sg("head_squares"), 1)
                    root_guess(act, ssq[:, :], ssr[:, :], sg("head_ms"), h + 1, sg("head_guess"))

            def dest(p):
                if p["kind"] == "small":
                    return small[:, :]
                if p["kind"] == "og":
                    return og[:, p["i"], :]
                if p["how"] == "conv" and (p["kind"] == "xs" or p["group"] >= rg.first["cd"]):
                    return None
                return {"q": g_q, "k": g_k, "r": mixA, "z": zmix, "bm": bmc, "cm": cmc}[p["kind"]][:, p["i"], :]

            def ssd_conv_bias(p):
                return col("ssd_cb", {"xs": 0, "bm": 8, "cm": 10}[p["kind"]] + p["i"])

            act.dma_start(w2p[:, :, :], A["w2p"]).then_inc(consts_in, 16)
            act.dma_start(dsk[:, :], A["ssd_d"].broadcast_to([P, SH])).then_inc(consts_in, 16)
            act.wait_ge(consts_in, 64)
            conditioning()
            norm(0, 0, 0, T)
            project(PLAN["gla"], dest)
            gla()
            modulation(1, 0)
            act.wait_ge(sg("conv_pads"), 1)
            project(PLAN["ssd"], dest, ssd_conv_bias)
            ssd_gates()
            ssd()
            act.wait_ge(sg("ssd_mixed"), 2)
            act.dma_start(x[:, :, :], A["xT"].rearrange("(k p) t -> p k t", p=P)).then_inc(sg("x_again"), 16)
            out_projection(0, (0, 1))
            act.wait_ge(sg("x_ready"), 1)
            act.dma_start(router[:, :, :], A["router"][0]).then_inc(sg("router_in"), 16)
            norm(1, 0, 1, T)
            route(0, (0, 1))
            experts(0, (0, 1))
            norm(2, 1, 0, T)
            act.wait_ge(sg("cd_consts"), 1)
            project(PLAN["cd"], dest, lambda p: 0.0)
            conformer_norm()
            gdn_gates()
            gdn()
            out_projection(1, (1,))
            act.wait_ge(sg("x_ready"), 3)
            act.dma_start(router[:, :, :], A["router"][1]).then_inc(sg("router_in"), 16)
            norm(3, 1, 1, SEQ)
            route(1, (1,))
            experts(1, (1,))
            norm(4, None, None, SEQ)

        @block.vector
        def _(dve):
            V = nc.vector

            def modulation(layer, r):
                dve.wait_ge(sg("mod_turned"), 3 * layer + r + 1)
                src = ps[7][:, :].rearrange("p (q g s) -> p g q s", q=4, g=4)[:, :, :, 0:2]
                bias = col(f"mod_b{layer}", 16 * r, 16).rearrange("p (g q) -> p g q", g=4).unsqueeze(3).broadcast_to([P, 4, 4, 2])
                V.tensor_tensor(modT[:, layer, 4 * r:4 * r + 4, :, :], src, bias, ALU.add)
                dve.drain().then_inc(sg("mod_added"), 1)
                if r == 2:
                    for w in range(2):
                        sc = modT[:, layer, 6 * w + 2:6 * w + 4, :, :].rearrange("p a b s -> p (a b) s")
                        g = col("norm1" if w == 0 else "norm2", 8 * layer, 8).unsqueeze(2).broadcast_to([P, KD, 2])
                        last = V.scalar_tensor_tensor(afac[:, layer, w, :, :], sc, 1.0, g, ALU.add, ALU.mult)
                    last.then_inc(sg("afac_ready"), 1)

            def norm(i, cw):
                c0 = T - cw
                dve.wait_ge(sg("norm_sums"), i + 1)
                V.tensor_scalar(rstd[:, c0:T], ps[7][:, 0:cw], 1.0 / D, 1e-6, ALU.mult, ALU.add).then_inc(sg("norm_ms"), 1)
                dve.wait_ge(sg("norm_root"), i + 1)
                V.reciprocal(rstd[:, c0:T], rstd[:, c0:T])
                dve.drain()
                for k in range(KD):
                    V.tensor_tensor(hT[:, k, c0:T], x[:, k, c0:T], rstd[:, c0:T], ALU.mult).then_inc(sg("norm_scaled"), 1)

            def project(made, dest, taps=None):
                def conformer_taps(i, lo, hi):
                    y = conf[:, i, :].rearrange("p (r c) -> p r c", r=ROWS)
                    for w in range(lo, hi):
                        if w == 0:
                            V.tensor_scalar(y, gluR[:, i, :, 0:GW], col("conf_w", i), col("conf_b", i), ALU.mult, ALU.add)
                        else:
                            V.scalar_tensor_tensor(y, gluR[:, i, :, w:w + GW], col("conf_w", 8 * w + i), y, ALU.mult, ALU.add)
                        dve.drain()

                glu_at = {j + n: (p["i"], lo, hi) for j, p in enumerate(made) if p["how"] == "glu" for n, (lo, hi) in enumerate(CONF_STEPS)}
                for j in range(len(made) + 2):
                    if j < len(made) and made[j]["how"] == "glu":
                        i = made[j]["i"]
                        dve.wait_ge(sg("glu_in"), i + 1)
                        V.tensor_tensor(gluR[:, i, :, CK // 2:CK // 2 + GW], gsig[i % 2].rearrange("p (r c) -> p r c", r=ROWS),
                                        gval[i % 2].rearrange("p (r c) -> p r c", r=ROWS), ALU.mult)
                        dve.drain().then_inc(sg("glu_done"), 1)
                    if j < len(made) and made[j]["how"] == "conv":
                        p = made[j]
                        c, s0 = p["conv"], p["c0"] // SEQ
                        if p["kind"] == "k" and p["i"] == 0 and p["group"] >= rg.first["cd"]:
                            dve.wait_ge(sg("conv_silu"), c)
                            dve.drain()
                            V.memset(cpad2[:, :, :, 0:1], 0.0)
                            V.memset(cpad2[:, :, :, SEQ + 1:SEQ + 2], 0.0)
                            dve.drain().then_inc(sg("conv_pads"), 1)
                        dve.wait_ge(sg("conv_in"), c + 1)
                        if c >= 2:
                            dve.wait_ge(sg("conv_silu"), c - 1)
                            before = conv_turn[c - 2]
                            if before is not None:
                                dve.wait_ge(sg("turn_done"), before + 1)
                        to = conv_sum(p)[:, p["c0"]:T].rearrange("p (s t) -> p s t", t=SEQ)
                        w, pad = taps(p), conv_pad(p)
                        V.tensor_scalar(to, pad[:, s0:2, 1:SEQ + 1], w[1], None, ALU.mult)
                        dve.drain()
                        V.scalar_tensor_tensor(to, pad[:, s0:2, 0:SEQ], w[0], to, ALU.mult, ALU.add)
                        dve.drain()
                        V.scalar_tensor_tensor(to, pad[:, s0:2, 2:SEQ + 2], w[2], to, ALU.mult, ALU.add).then_inc(sg("conv_done"), 1)
                    if j >= 2 and made[j - 2]["turn"] is not None:
                        p = made[j - 2]
                        dve.wait_ge(sg("turn_done"), p["turn"] + 1)
                        V.tensor_copy(dest(p), ps[4 + p["turn"] % 2][:, p["c0"]:T].rearrange("p (t c) -> p t c", c=P)).then_inc(sg("turn_copied"), 1)
                    if j in glu_at:
                        conformer_taps(*glu_at[j])

            def conformer_norm():
                dve.drain().then_inc(sg("conf_ready"), 1)
                dve.wait_ge(sg("conf_sums"), 1)
                V.tensor_scalar(rstd[:, 0:SEQ], ps[6][:, 0:SEQ], 1.0 / D, None, ALU.mult)
                dve.drain()
                for k in range(KD):
                    V.tensor_tensor(conf[:, k, :], conf[:, k, :], rstd[:, 0:SEQ], ALU.subtract).then_inc(sg("conf_centered"), 1)
                dve.wait_ge(sg("conf_sums"), 2)
                dve.drain()
                V.tensor_scalar(rstd[:, 0:SEQ], ps[7][:, 0:SEQ], 1.0 / D, 1e-5, ALU.mult, ALU.add).then_inc(sg("root_in"), 1)
                dve.wait_ge(sg("root_out"), 3)
                V.reciprocal(rstd[:, 0:SEQ], rstd[:, 0:SEQ])
                dve.drain()
                for k in range(KD):
                    V.tensor_tensor(conf[:, k, :], conf[:, k, :], rstd[:, 0:SEQ], ALU.mult).then_inc(sg("conf_scaled"), 1)

            def gdn_gates():
                sq = hT[:, 0:4, :].rearrange("p a b -> p (a b)")
                for half in range(2):
                    kh = k_t[:, 4 * half:4 * half + 4, :, :]
                    V.tensor_tensor(sq.rearrange("p (h t c) -> p h t c", h=4, t=NT), kh, kh, ALU.mult)
                    dve.drain()
                    V.tensor_reduce(rkq[:, 4 * half:4 * half + 4, 0:4], sq.rearrange("p (h t c) -> p h t c", h=4, t=NT), AX.X, ALU.add)
                    dve.drain()
                V.tensor_tensor(sq.rearrange("p (h t c) -> p h t c", h=8, t=2), q_t[:, :, :, :], q_t[:, :, :, :], ALU.mult)
                dve.drain()
                V.tensor_reduce(rkq[:, :, 4:6], sq.rearrange("p (h t c) -> p h t c", h=8, t=2), AX.X, ALU.add)
                dve.drain()
                V.tensor_scalar(rkq[:, :, :], rkq[:, :, :], 1e-6, None, ALU.add).then_inc(sg("root_in"), 1)
                dve.wait_ge(sg("root_out"), 4)
                V.reciprocal(rkq[:, :, :], rkq[:, :, :])
                dve.drain()
                V.tensor_scalar(rkq[:, :, 4:6], rkq[:, :, 4:6], float(P) ** -0.5, None, ALU.mult)
                rows = slice(0, 64)
                z, u, w, l, sp = Lm[0], Um[0], Ym[0], Xm[0], Lm[1]
                V.tensor_scalar(z[rows], small[rows, :], cols[rows, COL_AT["gdn_dtb"]:COL_AT["gdn_dtb"] + 1], None, ALU.add)
                dve.drain()
                V.scalar_tensor_tensor(u[rows], z[rows], -1.0, z[rows], ALU.mult, ALU.max).then_inc(sg("sp_abs"), 1)
                softplus_tail(rows, z, u, w, l, sp)
                V.tensor_scalar(w[rows], sp[rows], alogx[rows, :], -1.0, ALU.mult, ALU.mult)
                dve.drain()
                V.tensor_tensor_scan(gcb[0:32, :], rst128[0:32, :], w[0:32, :], 0.0, ALU.mult, ALU.add)
                V.tensor_tensor_scan(gcb[32:64, ::-1], rst128[32:64, :], w[32:64, ::-1], 0.0, ALU.mult, ALU.add)
                dve.drain()
                V.memset(albuf2, 0.0)
                dve.drain()
                for t in range(NT):
                    for d in range(2):
                        e = t * P + edge(d)
                        last = V.tensor_scalar(albuf2[0:64, t, 32 * d:32 * d + 32], ident[0:64, 32 * d:32 * d + 32], gcb[0:64, e:e + 1], None, ALU.mult)
                last.then_inc(sg("gate_cums"), 1)
                dve.wait_ge(sg("gate_cums_turned"), 2)
                tm = ps[0][:, :].rearrange("p (t d r) -> p t d r", t=NT, d=4)
                V.tensor_copy(gcT, tm[:, :, 0:2, 0:8])
                V.tensor_copy(btT, tm[:, :, 2:4, 0:8])
                V.tensor_copy(egl2, ps[1][:, 0:256].rearrange("p (t d r) -> p t d r", t=NT, d=2)[:, :, :, 0:8])
                dve.drain()
                V.tensor_tensor(ekd, egl2, gcT, ALU.subtract).then_inc(sg("gate_gap"), 1)
                dve.wait_ge(sg("gate_exps"), 2)
                V.tensor_tensor(beg, btT, egc, ALU.mult)
                dve.drain()

            def gdn():
                dve.wait_ge(sg("cd_consts"), 2)
                tiles = [slice(t * P, (t + 1) * P) for t in range(NT)]

                def t4(ap):
                    return ap.rearrange("p (t c) -> p t c", c=P)

                V.memset(osb[:, :, :], 0.0)
                with dve.Fori(0, KD) as h:
                    def gate(v, t, d):
                        return v[:, t, d, bass.ds(h, 1)]

                    def head(v):
                        return v[:, bass.ds(h, 1)].rearrange("p a t c -> p (a t) c")

                    V.tensor_tensor(t4(kts), head(k_t), rkq[:, bass.ds(h, 1), 0:4].rearrange("p a t -> p (a t)").unsqueeze(2).broadcast_to([P, NT, P]), ALU.mult)
                    V.tensor_tensor(t4(qts), head(q_t), rkq[:, bass.ds(h, 1), 4:6].rearrange("p a t -> p (a t)").unsqueeze(2).broadcast_to([P, 2, P]), ALU.mult).then_inc(sg("gdn_ktq"), 1)
                    for d in range(2):
                        V.tensor_scalar(grow[d], gcb, ident[:, bass.ds(h + 32 * d, 1)], None, ALU.mult).then_inc(sg("gdn_row"), 1)
                    for d in range(2):
                        dve.wait_ge(sg("gdn_bc"), 2 * h + d + 1)
                        for t in range(NT):
                            V.tensor_scalar(dec[d][:, tiles[t]], ps[4 + d][:, tiles[t]], gate(gcT, t, d), 0.0, ALU.subtract, ALU.max)
                        for t in range(2):
                            last = V.tensor_scalar(aqk[d][:, tiles[t]], ps[4 + d][:, tiles[2 + t]], gate(gcT, 2 + t, d), 0.0, ALU.subtract, ALU.min)
                        last.then_inc(sg("gdn_gaps"), 1)
                    dve.wait_ge(sg("gdn_kk"), h + 1)
                    for d in range(2):
                        dve.wait_ge(sg("gdn_decay"), 2 * h + d + 1)
                        for t in range(NT):
                            V.scalar_tensor_tensor(dec[d][:, tiles[t]], ps[2][:, tiles[t]], gate(btT, t, d), dec[d][:, tiles[t]], ALU.mult, ALU.mult)
                        V.tensor_tensor(aqk[d], ps[3][:, 0:SEQ], aqk[d], ALU.mult)
                        dve.drain()
                        V.tensor_tensor(t4(Lm[d]), t4(dec[d]), m_str[:, d:d + 1, :].broadcast_to([P, NT, P]), ALU.mult).then_inc(sg("gdn_L"), 1)
                        V.tensor_tensor(t4(aqk[d]), t4(aqk[d]), m_inc[:, d:d + 1, :].broadcast_to([P, 2, P]), ALU.mult)
                    idb = ident[:, :].unsqueeze(1).broadcast_to([P, NT, P])
                    m1 = lvm[:, 0:1, :].broadcast_to([P, NT, P])
                    for d in range(2):
                        dve.drain()
                        V.tensor_tensor(t4(Xm[d]), t4(Lm[d]), m1, ALU.mult)
                        dve.wait_ge(sg("gdn_Uc"), 2 * h + d + 1)
                        V.tensor_tensor(t4(Ym[d]), t4(Um[d]), m1, ALU.mult)
                        dve.drain()
                        V.tensor_tensor(t4(Xm[d]), idb, t4(Xm[d]), ALU.subtract)
                        V.tensor_tensor(t4(Ym[d]), idb, t4(Ym[d]), ALU.subtract).then_inc(sg("gdn_xy"), 1)
                    for d in range(2):
                        for t in range(NT):
                            V.tensor_scalar(kdm[d][:, tiles[t]], kts[:, tiles[t]], gate(ekd, t, d), None, ALU.mult)
                    for l in range(6):
                        for d in range(2):
                            dve.wait_ge(sg("gdn_p"), 12 * h + 2 * l + d + 1)
                            last = V.tensor_tensor(Ym[d], Ym[d], ps[3 * d + 2][:, :], ALU.subtract)
                            if l < 5:
                                last = V.tensor_tensor(Xm[d], Xm[d], ps[3 * d + 1][:, :], ALU.subtract)
                            last.then_inc(sg("gdn_xy"), 1)
                    for d in range(2):
                        for t in range(NT):
                            V.tensor_scalar(vb[d][:, tiles[t]], v_t[:, bass.ds(h, 1), t, :].rearrange("p a c -> p (a c)"), gate(btT, t, d), None, ALU.mult)
                            last = V.tensor_scalar(kbe[d][:, tiles[t]], kts[:, tiles[t]], gate(beg, t, d), None, ALU.mult)
                        last.then_inc(sg("gdn_rhs"), 1)
                    for i in range(NT):
                        for d in range(2):
                            t = (0, 1, 2, 3)[i] if d == 0 else (1, 0, 3, 2)[i]
                            if i == 0:
                                dve.wait_ge(sg("gdn_uwc"), 2 * h + d + 1)
                                V.tensor_copy(vn[d], um[d][:, tiles[t]]).then_inc(sg("gdn_vn"), 1)
                            else:
                                dve.wait_ge(sg("gdn_ws"), 6 * h + 2 * (i - 1) + d + 1)
                                V.tensor_tensor(vn[d], um[d][:, tiles[t]], ps[3 * d + 2][:, 0:P], ALU.subtract).then_inc(sg("gdn_vn"), 1)
                        if i < 3:
                            for d in range(2):
                                t = (0, 1, 2, 3)[i] if d == 0 else (1, 0, 3, 2)[i]
                                dve.wait_ge(sg("gdn_kv"), 6 * h + 2 * i + d + 1)
                                if i == 0:
                                    V.tensor_copy(Sg[d], ps[3 * d + 2][:, P:2 * P]).then_inc(sg("gdn_S"), 1)
                                else:
                                    V.scalar_tensor_tensor(Sg[d], Sg[d], gate(egl2, t, d), ps[3 * d + 2][:, P:2 * P], ALU.mult, ALU.add).then_inc(sg("gdn_S"), 1)
                    dve.wait_ge(sg("gdn_o"), h + 1)
                    V.tensor_copy(osb[:, :, :], ps[6][:, 0:256].rearrange("p (t c) -> p t c", t=2))
                    for d in range(2):
                        dve.drain()
                        for t in range(2):
                            V.scalar_tensor_tensor(osb[:, t, :], ps[7][:, (2 * d + t) * P:(2 * d + t + 1) * P], gate(egc, 2 + t, d), osb[:, t, :], ALU.mult, ALU.add)
                    dve.drain().then_inc(sg("gdn_osum"), 1)
                    dve.wait_ge(sg("head_squares"), GH + h + 1)
                    V.tensor_scalar(onr[:, 0, :], onr[:, 0, :], 1.0 / P, 1e-6, ALU.mult, ALU.add).then_inc(sg("head_ms"), 1)
                    dve.wait_ge(sg("head_guess"), GH + h + 1)
                    root_refine(dve, onr[:, 1, :], onr[:, 0, :], onr[:, 2, :])
                    for t in range(2):
                        last = V.tensor_scalar(osb[:, t, :], osb[:, t, :], onr[:, 1, t:t + 1], None, ALU.mult)
                    last.then_inc(sg("head_normed"), 1)
                    dve.wait_ge(sg("head_turned"), GH + h + 1)
                    oh = og[:, bass.ds(h, 1), :].rearrange("p a c -> p (a c)")
                    V.scalar_tensor_tensor(oh, ps[1][:, 0:SEQ], cols[:, bass.ds(h + COL_AT["gdn_g"], 1)], oh, ALU.mult, ALU.mult).then_inc(sg("head_mixed"), 1)

            def final():
                dve.wait_ge(sg("norm_sums"), 5)
                V.tensor_scalar(rstd[:, SEQ:T], ps[7][:, 0:SEQ], 1.0 / D, 1e-6, ALU.mult, ALU.add).then_inc(sg("norm_ms"), 1)
                dve.wait_ge(sg("norm_root"), 5)
                V.reciprocal(rstd[:, SEQ:T], rstd[:, SEQ:T])
                dve.drain()
                for k in range(KD):
                    V.scalar_tensor_tensor(hT[:, k, SEQ:T], x[:, k, SEQ:T], col("final", k), rstd[:, SEQ:T], ALU.mult, ALU.mult)
                dve.drain().then_inc(sg("out_ready"), 1)

            def out_projection(layer, streams, bias):
                for s in streams:
                    for h in range(2):
                        last = V.tensor_tensor(gbias[:, 4 * h:4 * h + 4, s], modT[:, layer, 4 + h, :, s], col(bias, 4 * h, 4), ALU.mult)
                last.then_inc(sg("out_bias"), 1)
                if layer == 0:
                    dve.wait_ge(sg("x_again"), 16)
                for c in range(8):
                    dve.wait_ge(sg("out_scaled"), 8 * layer + c + 1)
                    cc = slice(0 if 0 in streams else SEQ, T)
                    last = V.tensor_tensor(x[:, c, cc], x[:, c, cc], hT[:, c % 2, cc], ALU.add).then_inc(sg("out_added"), 1)
                dve.drain().then_inc(sg("x_ready"), 1)

            def route(layer, streams):
                n = 2 * len(streams)
                tl = slice(NT - n, NT)

                def over_experts(v):
                    return v.unsqueeze(2).broadcast_to([P, n, E])

                V.memset(affc[:, :, :], 0.0)
                dve.wait_ge(sg("logits"), layer + 1)
                lg = ps[0][:, 0:NT * E].rearrange("p (t e) -> p t e", t=NT)[:, tl, :]
                V.tensor_reduce(rowst[:, 0, tl], lg, AX.X, ALU.max)
                dve.drain()
                V.tensor_tensor(aff[:, tl, :], lg, over_experts(rowst[:, 0, tl]), ALU.subtract).then_inc(sg("logits_shifted"), 1)
                dve.wait_ge(sg("aff_exp"), layer + 1)
                V.tensor_reduce(rowst[:, 1, tl], aff[:, tl, :], AX.X, ALU.add)
                dve.drain()
                V.reciprocal(rowst[:, 2, tl], rowst[:, 1, tl])
                dve.drain()
                V.tensor_tensor(aff[:, tl, :], aff[:, tl, :], over_experts(rowst[:, 2, tl]), ALU.mult)
                dve.drain()
                for s in streams:
                    V.tensor_copy(affc[:, :, 32 * s:32 * s + E], aff[:, 2 * s:2 * s + 2, :])
                dve.drain().then_inc(sg("affinities"), 1)
                dve.wait_ge(sg("aff_turned"), 2 * layer + 1)
                V.tensor_copy(affT, ps[3][0:48, 0:SEQ])
                dve.drain()
                bufs = [affT, pickw[:, 0, :], pickw[:, 1, :], pickw[:, 0, :], pickw[:, 1, :]]
                for r in range(4):
                    V.max(top8[:, :], bufs[r])
                    dve.drain()
                    V.match_replace(bufs[r + 1], top8[:, :], bufs[r], -1.0)
                    dve.drain()
                V.tensor_scalar(pickv, pickw[:, 1, :], 0.0, None, ALU.is_lt)
                V.memset(affT, 1.0)
                dve.drain()
                V.tensor_tensor_scan(pickw[:, 0, :], affT, pickv, 0.0, ALU.mult, ALU.add)
                dve.drain()
                V.tensor_tensor(pickw[:, 1, :], pickw[:, 0, :], pickv, ALU.mult)
                dve.drain().then_inc(sg("affinities"), 1)
                dve.wait_ge(sg("aff_turned"), 2 * layer + 2)
                V.tensor_copy(slotT[:, :, :], ps[4][:, 0:96].rearrange("p (a b) -> p a b", a=2))
                dve.drain()
                for s in streams:
                    for tt in range(2):
                        pv = pick[:, s, tt, :].rearrange("p (e c) -> p e c", e=E)
                        V.tensor_tensor(pv, slotT[:, tt, 32 * s:32 * s + E].unsqueeze(2).broadcast_to([P, E, CAP]),
                                        iota1[:, :].unsqueeze(1).broadcast_to([P, E, CAP]), ALU.is_equal)
                dve.drain().then_inc(sg("picks"), 1)
                for s in streams:
                    for tt in range(2):
                        V.tensor_tensor(pgate[:, s, tt, :].rearrange("p (e c) -> p e c", e=E), pick[:, s, tt, :].rearrange("p (e c) -> p e c", e=E),
                                        aff[:, 2 * s + tt, :].unsqueeze(2).broadcast_to([P, E, CAP]), ALU.mult)
                dve.drain().then_inc(sg("picks"), 1)
                for i, s in enumerate(streams):
                    for half in range(2):
                        dve.wait_ge(sg("gates_turned"), 4 * layer + 2 * i + half + 1)
                        V.tensor_copy(gateT[:, s, 2 * half:2 * half + 2, :], ps[2 * i + half][:, :].rearrange("p (q t) -> p q t", q=2))
                dve.drain()
                dve.wait_ge(sg("xe_ready"), layer + 1)
                dve.drain().then_inc(sg("routed"), 1)

            def experts(layer, streams):
                q0 = Q * layer
                with dve.Fori(0, Q) as q:
                    n = 2 * q + 2 * q0
                    for hf in range(2):
                        dve.wait_ge(sg("moe_h3"), n + hf + 1)
                        dve.wait_ge(sg("moe_silu"), n + hf + 1)
                        for s in streams:
                            last = V.tensor_tensor(hid[s][:, 512 * hf:512 * hf + 512], sil[s], ps[2 + s][:, :], ALU.mult)
                        last.then_inc(sg("moe_hid"), 1)
                    for dt in range(KD):
                        dve.wait_ge(sg("moe_sum"), 8 * q + 8 * q0 + dt + 1)
                        for s in streams:
                            cc = slice(s * SEQ, (s + 1) * SEQ)
                            last = V.scalar_tensor_tensor(x[:, dt, cc], ps[7 if dt % 2 else 4][:, cc], mod(layer, 5, dt, s),
                                                          x[:, dt, cc], ALU.mult, ALU.add)
                        last.then_inc(sg("moe_added"), 1)
                dve.drain().then_inc(sg("x_ready"), 1)

            def softplus_tail(rows, z, u, w, l, to):
                dve.wait_ge(sg("sp_u"), 1 if rows.start else 2)
                V.tensor_scalar(w[rows], u[rows], 1.0, None, ALU.add).then_inc(sg("sp_w"), 1)
                dve.drain()
                V.tensor_scalar(to[rows], w[rows], -1.0, TINY, ALU.add, ALU.add)
                dve.drain()
                V.reciprocal(to[rows], to[rows])
                dve.drain()
                V.tensor_tensor(to[rows], to[rows], u[rows], ALU.mult)
                dve.wait_ge(sg("sp_ln"), 1 if rows.start else 2)
                dve.drain()
                V.scalar_tensor_tensor(to[rows], l[rows], TINY, to[rows], ALU.add, ALU.mult)
                dve.drain()
                V.scalar_tensor_tensor(to[rows], z[rows], 0.0, to[rows], ALU.max, ALU.add)
                dve.drain()

            def ssd_gates():
                rows = slice(64, 128)
                dve.wait_ge(sg("conv_silu"), 12)
                dve.drain()
                V.memset(dtc[:, :], 0.0)
                V.memset(ac[:, :], 0.0)
                V.tensor_scalar(sp_z[rows, :], small[rows, :], cols[rows, COL_AT["ssd_dtb"]:COL_AT["ssd_dtb"] + 1], None, ALU.add)
                dve.drain()
                V.scalar_tensor_tensor(sp_u[rows, :], sp_z[rows, :], -1.0, sp_z[rows, :], ALU.mult, ALU.max).then_inc(sg("sp_abs"), 1)
                softplus_tail(rows, sp_z, sp_u, sp_w, sp_l, dtc)
                V.tensor_scalar(sp_w[rows, :], dtc[rows, :], alog_e[rows, :], -1.0, ALU.mult, ALU.mult)
                dve.drain()
                V.tensor_tensor_scan(ac[64:96, :], rst128[64:96, :], sp_w[64:96, :], 0.0, ALU.mult, ALU.add)
                V.tensor_tensor_scan(ac[96:128, ::-1], rst128[96:128, :], sp_w[96:128, ::-1], 0.0, ALU.mult, ALU.add)
                dve.drain()
                for t in range(NT):
                    for d in range(2):
                        e = t * P + edge(d)
                        last = V.tensor_scalar(albuf[:, t, 32 * d:32 * d + 32], ident[:, 64 + 32 * d:96 + 32 * d], ac[:, e:e + 1], None, ALU.mult)
                last.then_inc(sg("gate_cums"), 1)
                modulation(1, 1)
                modulation(1, 2)
                dve.wait_ge(sg("gate_cums_turned"), 1)
                V.tensor_copy(dtT[:, :, :], ps[0][:, :].rearrange("p (t r) -> p t r", t=NT)[:, :, 64:128])
                V.tensor_copy(acT[:, :, :], ps[1][:, :].rearrange("p (t r) -> p t r", t=NT)[:, :, 64:128])
                V.tensor_scalar(nacT[:, :, :], ps[1][:, :].rearrange("p (t r) -> p t r", t=NT)[:, :, 64:128], -1.0, None, ALU.mult)
                dve.drain()
                V.tensor_tensor(dtw[:, :, :], ps[2][:, 0:256].rearrange("p (t r) -> p t r", t=NT), acT[:, :, :], ALU.subtract).then_inc(sg("gate_gap"), 1)
                dve.wait_ge(sg("gate_exps"), 1)
                V.tensor_tensor(dtw[:, :, :], dtw[:, :, :], dtT[:, :, :], ALU.mult)
                for t in range(NT):
                    V.tensor_tensor(heads(ysb[:, t, :]), xs_t[:, :, t, :].rearrange("p c (a b) -> p c a b", a=2),
                                    dsk[:, :].rearrange("p (c a) -> p c a", a=2).unsqueeze(3).broadcast_to([P, 8, 2, 64]), ALU.mult)
                dve.drain()

            def ssd():
                prime(dve, "ssd_mat")
                prime(dve, "ssd_y_added")
                for g in range(2):
                    dve.wait_ge(sg("ssd_cb"), g + 1)
                    V.tensor_copy(cbs, ps[4][:, :])
                    dve.drain().then_inc(sg("ssd_cbm"), 1)
                    for d in range(2):
                        n = 2 * g + d
                        order = [0, 1, 2, 3] if d == 0 else [1, 0, 3, 2]
                        r0 = 32 * d + 8 * g

                        def spread(v, t):
                            return v[:, t, r0:r0 + 8].rearrange("p (c a) -> p c a", a=2).unsqueeze(3).broadcast_to([P, 4, 2, 64])

                        for i in range(3):
                            t = order[i]
                            if 3 * n + i >= 1:
                                dve.wait_ge(sg("ssd_kv"), 3 * n + i)
                            V.tensor_tensor(heads(wv[:, :]), xs_t[:, 4 * g:4 * g + 4, t, :].rearrange("p c (a b) -> p c a b", a=2),
                                            spread(dtw, t), ALU.mult).then_inc(sg("ssd_wv"), 1)
                            if i > 0:
                                V.tensor_tensor(heads(s_in[:, i, :]), heads(s_in[:, i - 1, :]), spread(eal, t), ALU.mult)
                            dve.wait_ge(sg("ssd_kv"), 3 * n + i + 1)
                            dve.drain()
                            if i == 0:
                                if n >= 1:
                                    dve.wait_ge(sg("ssd_inter"), 3 * n)
                                V.tensor_copy(s_in[:, 0, :], ps[5][:, :])
                            else:
                                V.tensor_tensor(s_in[:, i, :], s_in[:, i, :], ps[5][:, :], ALU.add)
                            dve.drain().then_inc(sg("ssd_state"), 1)
                        for i in range(3):
                            t = order[i + 1]
                            dve.wait_ge(sg("ssd_inter"), 3 * n + i + 1)
                            V.tensor_tensor(heads(wv[:, :]), heads(ps[6 + i % 2][:, :]), spread(cdec, t), ALU.mult)
                            dve.drain()
                            yt = ysb[:, t, 512 * g:512 * g + 512]
                            V.tensor_tensor(yt, yt, wv[:, :], ALU.add)
                            dve.drain().then_inc(sg("ssd_inter_added"), 1)
                        with dve.Fori(0, 4) as pair:
                            for hp in range(2):
                                k = 8 * n + 2 + 2 * pair + hp
                                dve.wait_ge(sg("ssd_decay"), k + 1)
                                dve.wait_ge(sg("ssd_y"), k - 1)
                                for t in range(NT):
                                    last = V.scalar_tensor_tensor(mat[hp][:, t * P:t * P + P], seg[hp][:, t * P:t * P + P],
                                                                  dtT[:, t, bass.ds(2 * pair + r0 + hp, 1)], cbs[:, t * P:t * P + P],
                                                                  ALU.mult, ALU.mult)
                                last.then_inc(sg("ssd_mat"), 1)
                            for hp in range(2):
                                k = 8 * n + 2 + 2 * pair + hp
                                dve.wait_ge(sg("ssd_y"), k + 1)
                                yh = ysb[:, :, bass.ds(128 * pair + 512 * g + 64 * hp, 64)]
                                V.tensor_tensor(yh, yh, ps[2 + hp][:, :].rearrange("p (t c) -> p t c", t=NT)[:, :, 64 * hp:64 * hp + 64],
                                                ALU.add).then_inc(sg("ssd_y_added"), 1)
                        dve.drain().then_inc(sg("ssd_pass"), 1)
                for c in range(8):
                    dve.wait_ge(sg("ssd_turned"), c + 1)
                    V.tensor_tensor(zmix[:, c, :], zmix[:, c, :], ps[c % 4][:, :], ALU.mult).then_inc(sg("ssd_gated"), 1)
                for g in range(2):
                    dve.wait_ge(sg("ssd_sums"), g + 1)
                    V.tensor_scalar(rstd[:, :], ps[4 + g][:, :], 1.0 / 512, 1e-6, ALU.mult, ALU.add).then_inc(sg("root_in"), 1)
                    dve.wait_ge(sg("root_out"), g + 1)
                    V.reciprocal(rstd[:, :], rstd[:, :])
                    dve.drain()
                    for c in range(4 * g, 4 * g + 4):
                        V.scalar_tensor_tensor(zmix[:, c, :], zmix[:, c, :], col("ssd_g", c), rstd[:, :], ALU.mult, ALU.mult)
                    dve.drain().then_inc(sg("ssd_mixed"), 1)

            def gla():
                V.memset(kdt[:, :, :, :], 0.0)
                V.memset(sS[:, :, :], 0.0)
                V.memset(attm[:, :, :, :], 0.0)
                dve.drain().then_inc(sg("gla_zeroed"), 1)
                with dve.Fori(0, GH) as h:
                    q_h = g_q[:, bass.ds(h, 1), :].rearrange("p a c -> p (a c)")
                    k_h = g_k[:, bass.ds(h, 1), :].rearrange("p a c -> p (a c)")
                    for d in range(2):
                        n = 2 * h + d
                        dve.wait_ge(sg("gla_z"), n + 1)
                        V.tensor_scalar(e3[:, :], e1[:, :], 0.0, None, ALU.min)
                        V.scalar_tensor_tensor(gcum[:, :], e1[:, :], -1.0, e1[:, :], ALU.mult, ALU.max).then_inc(sg("gla_absz"), 1)
                        dve.drain()
                        dve.wait_ge(sg("gla_lnz"), n + 1)
                        V.tensor_tensor(e3[:, :], e3[:, :], e1[:, :], ALU.subtract)
                        dve.drain()
                        rev = (lambda a: a) if d == 0 else (lambda a: a[:, ::-1])
                        V.tensor_tensor_scan(rev(gcum[:, :]), rst64[:, :], rev(e3[:, :]), 0.0, ALU.mult, ALU.add).then_inc(sg("gla_scanned"), 1)
                        dve.drain()
                        g3 = gcum[:, :].rearrange("p (c j) -> p c j", j=CH)
                        edge = CH - 1 if d == 0 else 0
                        V.tensor_tensor(e3[:, :].rearrange("p (c j) -> p c j", j=CH), g3[:, :, edge:edge + 1].broadcast_to([P, NC, CH]),
                                        g3, ALU.subtract).then_inc(sg("gla_gap"), 1)
                        dve.wait_ge(sg("gla_exps"), n + 1)
                        dve.wait_ge(sg("gla_o"), n)
                        V.scalar_tensor_tensor(qg[:, :], q_h, float(P) ** -0.5, e1[:, :], ALU.mult, ALU.mult)
                        V.tensor_tensor(kk[:, 0, :], k_h, kk[:, 0, :], ALU.mult)
                        dve.wait_ge(sg("gla_e3"), n + 1)
                        V.tensor_tensor(kk[:, 1, :], k_h, e3[:, :], ALU.mult).then_inc(sg("gla_gated"), 1)
                        dve.wait_ge(sg("gla_att"), n + 1)
                        V.tensor_copy(ssq[:, 0:1], egl[:, 0:1])
                        V.copy_predicated(attm[:, d, :, :], m_gla[:, d:d + 1, :].broadcast_to([P, NT, P]),
                                          ps[1][:, :].rearrange("p (t i) -> p t i", t=NT)).then_inc(sg("gla_masked"), 1)
                        dve.wait_ge(sg("gla_kv"), n + 1)
                        order = [0, 1, 2, 3, 4, 5, 6, 7] if d == 0 else [3, 2, 1, 0, 7, 6, 5, 4]
                        for a, b in zip(order, order[1:]):
                            kv = ps[2 + a // 2][:, 256 * (a % 2):256 * (a % 2) + 256]
                            if a == order[0]:
                                last = V.tensor_copy(sS[:, b, :], kv)
                            else:
                                last = V.scalar_tensor_tensor(sS[:, b, :], sS[:, a, :], egl[:, a:a + 1], kv, ALU.mult, ALU.add)
                            if b != order[-1]:
                                dve.drain()
                        last.then_inc(sg("gla_S"), 1)
                    dve.wait_ge(sg("head_squares"), h + 1)
                    V.tensor_scalar(ssq[:, :], ssq[:, :], 1.0 / GDV, 1e-6, ALU.mult, ALU.add).then_inc(sg("head_ms"), 1)
                    dve.wait_ge(sg("head_guess"), h + 1)
                    root_refine(dve, ssr[:, :], ssq[:, :], sst[:, :])
                    for b in range(2):
                        last = V.tensor_tensor(kk[:, b, :].rearrange("p (t e) -> p t e", t=2), ps[6 + b][:, :].rearrange("p (t e) -> p t e", t=2),
                                               ssr[:, 2 * b:2 * b + 2].unsqueeze(2).broadcast_to([P, 2, GDV]), ALU.mult)
                    last.then_inc(sg("head_normed"), 1)
                    dve.wait_ge(sg("head_turned"), h + 1)
                    for e in range(2):
                        r = mixA[:, bass.ds(2 * h + e, 1), :].rearrange("p a c -> p (a c)")
                        last = V.scalar_tensor_tensor(r, ps[e][:, :], cols[:, bass.ds(2 * h + e + COL_AT["gla_g"], 1)], r, ALU.mult, ALU.mult)
                    last.then_inc(sg("head_mixed"), 1)

            def dest(p):
                if p["group"] >= rg.first["cd"]:
                    return {"v": v_t, "q": q_t, "k": k_t}[p["kind"]][:, p["i"], :, :]
                return {"v": g_v, "xs": xs_t, "bm": bm_t}[p["kind"]][:, p["i"], :, :]

            def cd_taps(p):
                return [col("gdn_cw", 24 * w + 8 * "qkv".index(p["kind"]) + p["i"]) for w in range(3)]

            def ssd_taps(p):
                return [col("ssd_cw", 12 * w + {"xs": 0, "bm": 8, "cm": 10}[p["kind"]] + p["i"]) for w in range(3)]

            dve.wait_ge(consts_in, 64)
            V.memset(act_c[:, :, :], 0.0).then_inc(sg("cond_zeroed"), 1)
            norm(0, T)
            for r in range(3):
                modulation(0, r)
            project(PLAN["gla"], dest)
            gla()
            modulation(1, 0)
            V.memset(cpad[:, :, :, 0:1], 0.0)
            V.memset(cpad[:, :, :, SEQ + 1:SEQ + 2], 0.0)
            dve.drain().then_inc(sg("conv_pads"), 1)
            project(PLAN["ssd"], dest, ssd_taps)
            ssd_gates()
            ssd()
            out_projection(0, (0, 1), "ab_bout")
            norm(1, T)
            route(0, (0, 1))
            experts(0, (0, 1))
            norm(2, T)
            dve.wait_ge(sg("cd_consts"), 1)
            project(PLAN["cd"], dest, cd_taps)
            conformer_norm()
            gdn_gates()
            gdn()
            out_projection(1, (1,), "cd_bout")
            norm(3, SEQ)
            route(1, (1,))
            experts(1, (1,))
            final()

        @block.gpsimd
        def _(pool):
            G = nc.gpsimd
            G.memset(ident[:, :], 0.0)
            G.memset(ones[:, :], 1.0)
            G.memset(m_inc[:, :, :], 1.0)
            G.memset(m_str[:, :, :], 1.0)
            G.memset(m_gla[:, :, :], 1)
            G.memset(rst64[:, :], 1.0)
            G.memset(rst128[:, :], 1.0)
            G.iota(iota1[:, :], [[1, CAP]], base=1, channel_multiplier=0, allow_small_or_imprecise_dtypes=True)
            pool.drain()
            G.memset(rst64[:, :].rearrange("p (c j) -> p c j", j=CH)[:, :, 0:1], 0.0)
            G.memset(rst128[:, :].rearrange("p (c j) -> p c j", j=P)[:, :, 0:1], 0.0)
            G.affine_select(out=ident[:, :], in_=ident[:, :], compare_op=ALU.not_equal, fill=1.0, base=0,
                            pattern=[[-1, P]], channel_multiplier=1)
            for d in range(2):
                sign = 1 - 2 * d
                G.affine_select(out=m_inc[:, d, :], in_=m_inc[:, d, :], compare_op=ALU.is_ge, fill=0.0, base=0,
                                pattern=[[sign, P]], channel_multiplier=-sign)
                G.affine_select(out=m_gla[:, d, :], in_=m_gla[:, d, :], compare_op=ALU.is_ge, fill=0, base=0,
                                pattern=[[sign, P]], channel_multiplier=-sign)
                G.affine_select(out=m_str[:, d, :], in_=m_str[:, d, :], compare_op=ALU.is_gt, fill=0.0, base=0,
                                pattern=[[-sign, P]], channel_multiplier=sign)
            pool.drain()
            G.memset(m_gla[0:64, :, 64:128], 0)
            G.memset(m_gla[64:128, :, 0:64], 0)
            pool.drain().then_inc(consts_made, 1)

            def experts(layer, streams):
                q0 = Q * layer
                with pool.Fori(0, Q) as q:
                    pool.wait_ge(sg("routed"), layer + 1)
                    pool.wait_ge(sg("moe_h3"), 2 * q + 2 * q0)
                    for s in streams:
                        last = G.tensor_copy(xg[s], xe[:, s, :, bass.ds(P * q, P)])
                    last.then_inc(sg("moe_xg"), 1)

            def ssd():
                pool.wait_ge(sg("gate_cums"), 1)
                pool.wait_ge(sg("gate_gap"), 1)
                G.memset(identb[:, :], 0.0)
                G.memset(m_far[:, :, :], 0.0)
                pool.drain()
                G.affine_select(out=identb[:, :], in_=identb[:, :], compare_op=ALU.not_equal, fill=1.0, base=0,
                                pattern=[[-1, P]], channel_multiplier=1)
                for d in range(2):
                    sign = 1 - 2 * d
                    G.affine_select(out=m_far[:, d, :], in_=m_far[:, d, :], compare_op=ALU.is_ge, fill=-1e30, base=0,
                                    pattern=[[sign, P]], channel_multiplier=-sign)
                prime(pool, "ssd_row")
                for g in range(2):
                    for d in range(2):
                        with pool.Fori(0, 4) as pair:
                            for hp in range(2):
                                k = 16 * g + 8 * d + 2 + 2 * pair + hp
                                pool.wait_ge(sg("ssd_bc"), k - 1)
                                G.tensor_tensor(row[hp], ac[:, :], ident[:, bass.ds(2 * pair + 64 + 32 * d + 8 * g + hp, 1)].broadcast_to([P, T]),
                                                ALU.mult).then_inc(sg("ssd_row"), 1)

            def gdn():
                pool.wait_ge(sg("x_ready"), 2)
                G.memset(gluR[:, :, :, :], 0.0)
                pool.drain().then_inc(sg("cd_consts"), 1)
                G.memset(lvm[:, :, :], 1.0)
                for l in range(7):
                    pool.drain()
                    b = 2 << l
                    v = lvm[:, l, :].rearrange("p (n c) -> p n c", c=b)
                    G.affine_select(out=v, in_=v, compare_op=ALU.is_ge, fill=0.0, base=0, pattern=[[-b, P // b], [0, b]], channel_multiplier=1)
                    pool.drain()
                    G.affine_select(out=v, in_=v, compare_op=ALU.is_ge, fill=0.0, base=b - 1, pattern=[[b, P // b], [0, b]], channel_multiplier=-1)
                pool.drain()
                for l in range(6, 0, -1):
                    G.tensor_tensor(lvm[:, l, :], lvm[:, l, :], lvm[:, l - 1, :], ALU.subtract)
                    pool.drain()
                G.tensor_tensor(lvm[:, 0, :], lvm[:, 0, :], ident[:, :], ALU.subtract)
                pool.drain().then_inc(sg("cd_consts"), 1)
                with pool.Fori(0, KD) as h:
                    for l in range(6):
                        for d in range(2):
                            if l == 0:
                                pool.wait_ge(sg("gdn_Uc"), 2 * h + d + 1)
                                pool.wait_ge(sg("gdn_uw"), 2 * h)
                            else:
                                pool.wait_ge(sg("gdn_z"), 12 * h + 2 * l + d - 1)
                            G.tensor_tensor(Bm[d].rearrange("p (t c) -> p t c", c=P), Um[d].rearrange("p (t c) -> p t c", c=P),
                                            lvm[:, l + 1:l + 2, :].broadcast_to([P, NT, P]), ALU.mult).then_inc(sg("gdn_bt"), 1)

            ssd()
            experts(0, (0, 1))
            gdn()
            experts(1, (1,))


def pack_columns(np, a):
    got = np.zeros((P, NCOLS), np.float32)

    def put(name, vec, at=0):
        v = np.asarray(vec).reshape(-1, P).T
        got[:, COL_AT[name] + at:COL_AT[name] + at + v.shape[1]] = v

    def tiles(vec, order, place):
        for j, (kind, i) in enumerate(order):
            if kind != "small":
                o = place[kind] + i * P
                got[:, at0 + j] = vec[o:o + P]

    put("mod_b0", a["mod_b"][0])
    put("mod_b1", a["mod_b"][1])
    put("norm1", a["norm1_g"])
    put("norm2", a["norm2_g"])
    put("final", a["final_norm_g"])
    put("cvec", a["c_ctx"])
    put("cvec", a["c"][0], 8)
    b = a["ab_b_in"][0]
    at0 = COL_AT["ab_b"]
    tiles(b, AB_GLA + AB_SSD, AB_PLACE)
    for dst, src, n in AB_SMALL:
        got[dst:dst + n, at0] = b[src:src + n]
    put("ab_bout", a["ab_b_out"][0])
    put("gla_bg", a["gla_b_gate2"][0])
    put("gla_g", a["gla_norm_g"][0])
    put("ssd_cw", a["ssd_conv_w"][0])
    put("ssd_cb", a["ssd_conv_b"][0])
    put("ssd_g", a["ssd_norm_g"][0])
    for d in range(2):
        got[64 + 32 * d:80 + 32 * d, COL_AT["ssd_dtb"]] = a["ssd_dt_bias"][0, d]
        got[64 + 32 * d:80 + 32 * d, COL_AT["ssd_alog"]] = a["ssd_a_log"][0, d]
        got[32 * d:32 * d + 8, COL_AT["gdn_dtb"]] = a["gdn_dt_bias"][0, d]
        got[32 * d:32 * d + 8, COL_AT["gdn_alog"]] = a["gdn_a_log"][0, d]
    b = a["cd_b_in"][0]
    at0 = COL_AT["cd_b"]
    tiles(b, CD_ALL, CD_PLACE)
    for dst, src, n in CD_SMALL:
        got[dst:dst + n, at0] = b[src:src + n]
    put("cd_bout", a["cd_b_out"][0])
    put("conf_w", a["conf_dw_w"][0])
    put("conf_b", a["conf_dw_b"][0])
    put("conf_g", a["conf_ln_g"][0])
    put("conf_bb", a["conf_ln_b"][0])
    put("gdn_cw", a["gdn_conv_w"][0])
    put("gdn_g", a["gdn_norm_g"][0])
    return got


AB_PLACE = {"q": 0, "k": 512, "v": 1024, "r": 2048, "z": 3104, "xs": 4128, "bm": 5152, "cm": 5408}
AB_SMALL = [(0, 3072, 16), (32, 3088, 16), (64, 5664, 16), (96, 5680, 16)]
CD_PLACE = {"ga": 0, "gb": 1024, "q": 2048, "k": 3072, "v": 4096, "og": 5120}
CD_SMALL = [(0, 6144, 8), (32, 6152, 8), (64, 6160, 8), (96, 6168, 8)]


def pack_projection(np, w, order, place, gates):
    got = np.zeros((len(order), P, KD, P), np.float32)
    for j, (kind, i) in enumerate(order):
        if kind == "small":
            for dst, src, n in gates:
                got[j, :, :, dst:dst + n] = w[:, src:src + n].reshape(KD, P, n).transpose(1, 0, 2)
        else:
            o = place[kind] + i * P
            got[j] = w[:, o:o + P].reshape(KD, P, P).transpose(1, 0, 2)
    return got.reshape(len(order), P, KD * P)


def pack_out(np, w):
    return np.ascontiguousarray(w.reshape(16, P, KD, P).transpose(2, 1, 0, 3)).reshape(KD, P, 16 * P)


def lay_out(np, a):
    w2p = np.zeros((P, 8, P), np.float32)
    for d in range(2):
        w2p[32 * d:32 * d + 16, 4 * d:4 * d + 4] = a["gla_w_gate2"][0, d].reshape(16, GH, P)
    return {
        "xT": np.ascontiguousarray(np.concatenate([a["ctx"][0].T, a["x"][0].T], axis=1)),
        "cols": pack_columns(np, a),
        "mod_w": a["mod_w"],
        "ab_w": pack_projection(np, a["ab_w_in"][0], AB_GLA + AB_SSD, AB_PLACE, AB_SMALL),
        "ab_wo": pack_out(np, a["ab_w_out"][0]),
        "cd_w": pack_projection(np, a["cd_w_in"][0], CD_ALL, CD_PLACE, CD_SMALL),
        "cd_wo": pack_out(np, a["cd_w_out"][0]),
        "w2p": w2p,
        "ssd_d": a["ssd_d"],
        "router": np.ascontiguousarray(a["moe_router"].reshape(2, KD, P, E).transpose(0, 2, 1, 3)),
        "w1": a["moe_w1"], "w3": a["moe_w3"], "w2": a["moe_w2"],
    }


def kernel(**inputs):
    import numpy as np
    import concourse.bacc as bacc
    from concourse import mybir as _mybir
    from concourse.bass_utils import run_bass_kernel_spmd as run

    nc = bacc.Bacc("TRN2", target_bir_lowering=False, num_devices=1, dynamic_dma_scratch_size=1024)
    arrays, args = {}, {}
    for name, a in lay_out(np, {k: np.asarray(v) for k, v in inputs.items()}).items():
        arrays[f"in_{name}"] = a
        args[name] = nc.dram_tensor(f"in_{name}", a.shape, _mybir.dt.from_np(a.dtype), kind="ExternalInput").ap()
    out = nc.dram_tensor("out_t", (D, SEQ), F32, kind="ExternalOutput").ap()
    hybrid_backbone(nc, args, out)
    r = run(nc, [arrays], core_ids=[0])
    return np.ascontiguousarray(r.results[0]["out_t"].T)[None]
```

```python
from contextlib import ExitStack

import concourse.bass as bass
from concourse import mybir

ALU = mybir.AluOpType
ACT = mybir.ActivationFunctionType
F32 = mybir.dt.float32
I32 = mybir.dt.int32
BF16 = mybir.dt.bfloat16
AX = mybir.AxisListType

P = 128
D = 1024
KD = D // P
SEQ = 256
T = 2 * SEQ
NT = T // P
CH = 64
NC = T // CH
GH, GDV = 4, 256
SH = 16
CK = 31
GW, ROWS = 64, SEQ // 64
PADW = GW + CK - 1
E, CAP = 16, 32
Q = E // 4
TINY = 1e-30

COLS = [("mod_b0", 48), ("mod_b1", 48), ("norm1", 16), ("norm2", 16), ("final", 8), ("cvec", 16),
        ("ab_b", 45), ("ab_bout", 8), ("gla_bg", 8), ("gla_g", 8), ("ssd_cw", 36), ("ssd_cb", 12),
        ("ssd_g", 8), ("ssd_dtb", 1), ("ssd_alog", 1), ("cd_b", 49), ("cd_bout", 8), ("conf_w", 248),
        ("conf_b", 8), ("conf_g", 8), ("conf_bb", 8), ("gdn_cw", 72), ("gdn_g", 8), ("gdn_dtb", 1),
        ("gdn_alog", 1)]
COL_AT = {}
NCOLS = 0
for _name, _width in COLS:
    COL_AT[_name] = NCOLS
    NCOLS += _width

AB_GLA = [("small", 0)] + [("q", i) for i in range(4)] + [("k", i) for i in range(4)] \
    + [("v", i) for i in range(8)] + [("r", i) for i in range(8)]
AB_SSD = [("xs", i) for i in range(8)] + [("bm", 0), ("bm", 1), ("cm", 0), ("cm", 1)] + [("z", i) for i in range(8)]
CD_ALL = [("small", 0)] + [(k, i) for i in range(8) for k in ("gb", "ga", "k", "v", "og", "q")]
CONF_STEPS = [(0, 7), (7, 13), (13, 19), (19, 25), (25, 31)]


def weight_groups():
    g = [(f"mod0{r}", i, 4) for r in range(3) for i in range(2)]
    g += [("gla", 8 * i, 1) for i in range(4)]
    g += [("mod10", i, 4) for i in range(2)]
    g += [("ssd", 8 * i, 1) for i in range(3)]
    g += [(f"mod1{r}", i, 4) for r in range(1, 3) for i in range(2)]
    g += [("about", 4 * i, 1) for i in range(2)]
    g += [("moe0", i, 4) for i in range(12 * Q)]
    g += [("cd", 8 * i, 1) for i in range(7)]
    g += [("cdout", 4 * i, 1) for i in range(2)]
    g += [("moe1", i, 4) for i in range(12 * Q)]
    return g


RING = 3


class Ring:

    def __init__(self):
        self.groups = weight_groups()
        self.first, self.landed = {}, []
        total = [0] * RING
        for n, (stage, _, dmas) in enumerate(self.groups):
            self.first.setdefault(stage, n)
            total[n % RING] += 16 * dmas
            self.landed.append(total[n % RING])


def hybrid_backbone(nc, A, out):
    rg = Ring()
    with ExitStack() as ctx:
        def sem(name):
            return ctx.enter_context(nc.semaphore(name))

        def sb(name, shape, dt=F32, stack=ctx):
            return stack.enter_context(nc.sbuf_tensor(name, shape, dt))

        ps = [ctx.enter_context(nc.psum_tensor(f"bank{i}", [P, 512], F32)) for i in range(8)]

        ring = sb("ring", [P, RING, 4, 2048])
        x = sb("x", [P, KD, T])
        hT = sb("hT", [P, KD, T])
        cols = sb("cols", [P, NCOLS])
        modT = sb("modT", [P, 2, 12, 4, 2])
        afac = sb("afac", [P, 2, 2, KD, 2])
        ident = sb("ident", [P, P])
        ones = sb("ones", [P, P])
        m_gla = sb("m_gla", [P, 2, P], I32)
        m_far = sb("m_far", [P, 2, P], BF16)
        m_near = sb("m_near", [P, 2, P], BF16)
        identb = sb("identb", [P, P], BF16)
        rst64 = sb("rst64", [P, T])
        rst128 = sb("rst128", [P, T])
        small = sb("small", [P, T])
        rstd = sb("rstd", [P, T])
        iota1 = sb("iota1", [P, CAP])
        gbias = sb("gbias", [P, KD, 2])
        act_c = sb("act_c", [P, KD, 32])
        mrow = sb("mrow", [P, 512])
        dsk = sb("dsk", [P, SH])

        def col(name, i=0, n=1):
            return cols[:, COL_AT[name] + i:COL_AT[name] + i + n]

        def mod(layer, part, k, s):
            return modT[:, layer, 2 * part + k // 4, k % 4, s:s + 1]

        with ExitStack() as st:
            mixA = sb("mixA", [P, 8, T], F32, st)
            with ExitStack() as s2:
                g_q = sb("g_q", [P, GH, T], F32, s2)
                g_k = sb("g_k", [P, GH, T], F32, s2)
                g_v = sb("g_v", [P, 8, NT, P], F32, s2)
                gcum = sb("gcum", [P, 8, T], F32, s2)
                ex = rstd
                e1 = sb("e1", [P, T], F32, s2)
                e3 = sb("e3", [P, T], F32, s2)
                qg = sb("qg", [P, T], F32, s2)
                attm = sb("attm", [P, 2, NT, P], F32, s2)
                egl = sb("egl", [P, 2, NC], F32, s2)
                kk = x[:, 0:2, :]
                kdt = x[:, 2:4, :].rearrange("p a (b c d) -> p (a b) c d", b=2, c=2)
                sS = x[:, 4:8, :].rearrange("p a (b e) -> p (a b) e", b=2)
                ssq = sb("ssq", [P, 2, GH, 2], F32, s2)
                w2p = kk.rearrange("p a (b c) -> p (a b) c", c=P)
                QG, K0, K1 = [qg[:, :], e1[:, :]], [kk[:, 0, :], e3[:, :]], [kk[:, 1, :], ex[:, :]]
                gz, gm, gu, gl = qg[:, :], attm[:, 0, :, :].rearrange("p t i -> p (t i)"), attm[:, 1, :, :].rearrange("p t i -> p (t i)"), ex[:, :]
            with ExitStack() as s2:
                zmix = sb("zmix", [P, 8, T], F32, s2)
                xs_t = sb("xs_t", [P, 8, NT, P], F32, s2)
                bmc = sb("bmc", [P, 2, T], F32, s2)
                cmc = sb("cmc", [P, 2, T], F32, s2)
                bm_t = sb("bm_t", [P, 2, NT, P], F32, s2)
                cpad = x[:, 0:3, :].rearrange("p a b -> p (a b)")[:, 0:4 * (SEQ + 2)].rearrange("p (a b c) -> p a b c", a=2, b=2)
                cacc = x[:, 4:6, :]
                s_in = sb("s_in", [P, 3, T], F32, s2)
                row1 = sb("row1", [P, T], F32, s2)
                dtT, acT, dtw, cdec, eal, albuf, nacT = [sb(f"ssd_g{i}", [P, NT, 64], F32, s2) for i in range(7)]
                alog_e = sb("alog_e", [P, 1], F32, s2)
                dtc, ac, sp_w, sp_l, sp_z, sp_u = [x[:, i, :] for i in range(6)]
                row = [x[:, 2, :], row1[:, :]]
                seg = [x[:, 3, :], rstd[:, :]]
                mat = [x[:, 4, :], x[:, 0, :]]
                cbs = x[:, 5, :]
                wv = [x[:, 7, :], x[:, 6, :]]
                ysb = hT[:, :, :].rearrange("p (t a) b -> p t (a b)", t=NT)

        with ExitStack() as st:
            xgs = sb("xgs", [P, 2, KD, P], F32, st)
            sils = sb("sils", [P, 2, 512], F32, st)
            htok = sb("htok", [P, NT, D], F32, st)
            pick = sb("pick", [P, 2, 2, E * CAP], F32, st)
            pgate = sb("pgate", [P, 2, 2, E * CAP], F32, st)
            gateT = sb("gateT", [P, 2, Q, SEQ], F32, st)
            pickw = sb("pickw", [48, 2, SEQ], F32, st)
            router = sb("router", [P, KD, E], F32, st)
            aff = sb("aff", [P, NT, E], F32, st)
            affc = sb("affc", [P, 2, 48], F32, st)
            slotT = sb("slotT", [P, 2, 48], F32, st)
            top8 = sb("top8", [48, 8], F32, st)
            rowst = sb("rowst", [P, 3, NT], F32, st)
            affT, pickv = rstd[0:48, 0:SEQ], rstd[0:48, SEQ:T]
            hid = [hT[:, 2 * s:2 * s + 2, :].rearrange("p a b -> p (a b)") for s in range(2)]
            hidT = [hT[:, 4 + 2 * s:6 + 2 * s, :].rearrange("p a (b c) -> p (a b) c", c=P) for s in range(2)]
            xg = [xgs[:, s, :, :] for s in range(2)]
            yex = [pgate[:, s, :, :].rearrange("p a b -> p (a b)") for s in range(2)]
            sil = [sils[:, s, :] for s in range(2)]
        with ExitStack() as st:
            gluR = sb("gluR", [P, KD, ROWS, PADW], F32, st)
            og = sb("og", [P, KD, SEQ], F32, st)
            k_t = sb("k_t", [P, KD, NT, P], F32, st)
            q_t = sb("q_t", [P, KD, 2, P], F32, st)
            v_t = sb("v_t", [P, KD, NT, P], F32, st)
            wk = sb("wk", [P, 5, T], F32, st)
            gts = sb("gts", [P, 7, NT, 2, 8], F32, st)
            lvm = sb("lvm", [P, 7, P], F32, st)
            alogx = sb("alogx", [P, 1], F32, st)
            rkq = sb("rkq", [P, KD, 6], F32, st)
            onr = sb("onr", [P, KD, 2], F32, st)
            conf = x[:, :, 0:SEQ]
            wkf = wk[:, :, :].rearrange("p a b -> p (a b)")
            cpad2 = wkf[:, 0:4 * (SEQ + 2)].rearrange("p (a b c) -> p a b c", a=2, b=2)
            cacc2 = wk[:, 3:5, :]
            gsig = [rstd[:, 256 * i:256 * i + 256] for i in range(2)]
            gval = [rst64[:, 256 * i:256 * i + 256] for i in range(2)]
            csq = [wkf[:, 256 * i:256 * i + 256] for i in range(2)]
            gcb = rst64[:, :]
            albuf2 = wk[:, 0, 0:256].rearrange("p (t r) -> p t r", t=NT)
            gcT, btT, egc, ekd, egl2, beg, ngcT = [gts[:, i, :, :, :] for i in range(7)]
            Lm = [hT[:, d, :] for d in range(2)]
            Um = [hT[:, 2 + d, :] for d in range(2)]
            Xm = [hT[:, 4 + d, :] for d in range(2)]
            Ym = [hT[:, 6 + d, :] for d in range(2)]
            glf = gluR[:, :, :, :].rearrange("p a b c -> p (a b c)")
            Zm = [glf[:, 512 * d:512 * d + 512] for d in range(2)]
            Bm = [glf[:, 1024 + 512 * d:1536 + 512 * d] for d in range(2)]
            kts = glf[:, 2048:2560]
            kc, dec = wk[:, 0, :], [wk[:, 2 + d, :] for d in range(2)]
            qc, qts = wk[:, 1, 0:256], wk[:, 1, 256:512]
            aqk = [wk[:, 4, 256 * d:256 * d + 256] for d in range(2)]
            kdm, kbe, um, wT = Lm, dec, Xm, Um
            vb = [kc, mrow[:, :]]
            grow = [rstd[:, :], small[:, :]]
            Sg = [rst128[:, P * d:P * d + P] for d in range(2)]
            vn = [rst128[:, 256 + P * d:384 + P * d] for d in range(2)]
        MOE_ORDER = [("w1", 0, 0), ("w1", 0, 1), ("w3", 0, 0), ("w3", 0, 1), ("w1", 1, 0), ("w1", 1, 1),
                     ("w3", 1, 0), ("w3", 1, 1), ("w2", 0, 0), ("w2", 1, 0), ("w2", 0, 1), ("w2", 1, 1)]

        landed = [sem(f"landed{i}") for i in range(RING)]
        w_used = sem("w_used")
        consts_in = sem("consts_in")
        consts_made = sem("consts_made")
        S = {}

        def sg(name):
            if name not in S:
                S[name] = sem(name)
            return S[name]

        block = ctx.enter_context(nc.Block())

        def prime(eng, name):
            for _ in range(2):
                eng.drain().then_inc(sg(name), 1)

        def slot(n):
            return ring[:, n % RING, :, :]

        def load_experts(sp, first, layer):
            with sp.Fori(0, Q) as q:
                for gi, (name, half, kh) in enumerate(MOE_ORDER):
                    s = (first + gi) % RING
                    sp.wait_ge(w_used, 12 * q + first + gi - RING + 1)
                    for j in range(4):
                        w = A[name][layer, bass.ds(4 * q + j, 1)].rearrange("e (k p) n -> p (e k) n", p=P)
                        sp.dma_start(ring[:, s, j, :].rearrange("p (k n) -> p k n", k=4),
                                     w[:, 4 * kh:4 * kh + 4, 512 * half:512 * half + 512]).then_inc(landed[s], 16)

        def load_group(sp, n, stage, i):
            s = n % RING
            if stage.startswith("mod"):
                layer, r = int(stage[3]), int(stage[4])
                w = A["mod_w"][layer].rearrange("(k p) n -> p k n", p=P)
                for g in range(4):
                    cb = 4 * r + g
                    sp.dma_start(ring[:, s, g, :].rearrange("p (k n) -> p k n", k=4),
                                 w[:, 4 * i:4 * i + 4, 512 * cb:512 * cb + 512]).then_inc(landed[s], 16)
            elif stage in ("gla", "ssd", "cd"):
                w = A["cd_w"] if stage == "cd" else A["ab_w"]
                base, count = {"gla": (0, 25), "ssd": (25, 20), "cd": (0, 49)}[stage]
                m = min(8, count - i)
                sp.dma_start(ring[:, s, :, :].rearrange("p a (b n) -> p (a b) n", b=2)[:, 0:m, :],
                             w[base + i:base + i + m].rearrange("c p n -> p c n")).then_inc(landed[s], 16)
            elif stage in ("about", "cdout"):
                w = A["ab_wo"] if stage == "about" else A["cd_wo"]
                sp.dma_start(ring[:, s, :, :], w[i:i + 4].rearrange("c p n -> p c n")).then_inc(landed[s], 16)

        GLA_KINDS = {"small": ("plain", False, True), "q": ("plain", False, True), "k": ("plain", False, True),
                     "v": ("plain", True, True), "r": ("silu", False, True)}
        SSD_KINDS = {"z": ("silu", False, True), "xs": ("conv", True, True), "bm": ("conv", True, True),
                     "cm": ("conv", False, True)}
        CD_KINDS = {"small": ("plain", False, True), "gb": ("gate", False, False), "ga": ("glu", False, False),
                    "og": ("silu", False, False), "q": ("conv", True, False), "k": ("conv", True, True), "v": ("conv", True, True)}
        counts = {"tile": 0, "turn": 0, "conv": 0}

        def plan(stage, tiles, kinds, bias, bias0):
            made = []
            for j, (kind, i) in enumerate(tiles):
                how, turn, both = kinds[kind]
                made.append(dict(group=rg.first[stage] + j // 8, place=j % 8, kind=kind, i=i, how=how,
                                 no=counts["tile"], last=j % 8 == 7 or j == len(tiles) - 1,
                                 turn=counts["turn"] if turn else None, conv=counts["conv"] if how == "conv" else None,
                                 c0=0 if both else SEQ, bias=col(bias, bias0 + j)))
                counts["tile"] += 1
                counts["turn"] += turn
                counts["conv"] += how == "conv"
            return made

        PLAN = {"gla": plan("gla", AB_GLA, GLA_KINDS, "ab_b", 0), "ssd": plan("ssd", AB_SSD, SSD_KINDS, "ab_b", len(AB_GLA)),
                "cd": plan("cd", CD_ALL, CD_KINDS, "cd_b", 0)}

        def conv_pad(p):
            return (cpad2 if p["group"] >= rg.first["cd"] else cpad)[:, p["conv"] % 2]

        def conv_sum(p):
            return (cacc2 if p["group"] >= rg.first["cd"] else cacc)[:, p["conv"] % 2, :]

        def turn_source(p):
            if p["kind"] == "bm":
                return bmc[:, p["i"], :]
            if p["how"] == "conv":
                return conv_sum(p)
            return e1[:, :] if p["turn"] % 2 == 0 else e3[:, :]

        conv_turn = [p["turn"] for made in PLAN.values() for p in made if p["conv"] is not None]

        def heads(ap):
            return ap.rearrange("p (c a b) -> p c a b", a=2, b=64)

        def edge(d):
            return P - 1 if d == 0 else 0

        @block.sync
        def _(sp):
            sp.dma_start(cols[:, :], A["cols"]).then_inc(consts_in, 16)
            sp.dma_start(x[:, :, :], A["xT"].rearrange("(k p) t -> p k t", p=P)).then_inc(consts_in, 16)
            for n, (stage, i, dmas) in enumerate(rg.groups):
                if stage in ("moe0", "moe1"):
                    if i == 0:
                        load_experts(sp, n, int(stage[3]))
                    continue
                if n >= RING:
                    sp.wait_ge(w_used, n - RING + 1)
                load_group(sp, n, stage, i)
            sp.wait_ge(sg("out_ready"), 1)
            sp.dma_start(out.rearrange("(k p) t -> p k t", p=P), hT[:, :, SEQ:T]).then_inc(sg("out_written"), 16)
            sp.wait_ge(sg("out_written"), 16)

        @block.tensor
        def _(pe):
            mm = nc.tensor.matmul

            def group_in(n):
                pe.wait_ge(landed[n % RING], rg.landed[n])

            def modulation(layer, r):
                first = rg.first[f"mod{layer}{r}"]
                if layer == 0 and r == 0:
                    pe.wait_ge(sg("cond_ready"), 1)
                elif (layer, r) != (1, 0):
                    pe.wait_ge(sg("mod_row_copied"), 3 * layer + r)
                for kh in range(2):
                    group_in(first + kh)
                    w = slot(first + kh).rearrange("p g (k n) -> p g k n", k=4)
                    for k in range(4):
                        for g in range(4):
                            last = mm(ps[6][32 * g:32 * g + 32, :], act_c[:, 4 * kh + k, :], w[:, g, k, :],
                                      start=(kh == 0 and k == 0), stop=(kh == 1 and k == 3),
                                      tile_position=(0, 32 * g))
                    last.then_inc(w_used, 1)
                pe.drain().then_inc(sg("mod_rows"), 1)
                pe.wait_ge(sg("mod_row_copied"), 3 * layer + r + 1)
                if layer == 0 and r == 0:
                    pe.wait_ge(sg("norm_ms"), 1)
                elif (layer, r) != (1, 0):
                    pe.wait_ge(sg("mod_added"), 3 * layer + r)
                for q in range(4):
                    nc.tensor.transpose(ps[7][:, q * P:(q + 1) * P], mrow[:, q * P:(q + 1) * P], ident[:, :])
                pe.drain().then_inc(sg("mod_turned"), 1)

            def norm(i, cw):
                for j in range(KD):
                    k = j // 2 + (KD // 2 if j % 2 else 0)
                    pe.wait_ge(sg("norm_squares2" if j % 2 else "norm_squares"), 4 * i + j // 2 + 1)
                    last = mm(ps[7][:, 0:cw], ones[:, :], hT[:, k, T - cw:T], start=(j == 0), stop=(j == KD - 1))
                last.then_inc(sg("norm_sums"), 1)

            def gla_gate(n):
                h, d = n // 2, n % 2
                if n == 0:
                    pe.wait_ge(consts_in, 64)
                    pe.wait_ge(sg("proj_evacuated"), 1)
                if n >= 2:
                    pe.wait_ge(sg("gla_z"), n - 1)
                mm(ps[6 + n % 2][:, :], w2p[:, 4 * d + h, :], small[:, :], start=True, stop=True).then_inc(sg("gla_gz"), 1)

            def project(made, lag=2, gates=None, ready=None):
                for j in range(len(made) + lag):
                    if j < len(made):
                        p = made[j]
                        if p["place"] == 0:
                            group_in(p["group"])
                        if p["no"] >= 4:
                            pe.wait_ge(sg("proj_evacuated"), p["no"] - 3)
                        w = slot(p["group"]).rearrange("p a (b k c) -> p (a b) k c", b=2, k=KD)[:, p["place"]]
                        for k in range(KD):
                            if j == 0 and ready is not None:
                                pe.wait_ge(sg("h_ready"), ready + k + 1)
                            last = mm(ps[p["no"] % 4][:, p["c0"]:T], w[:, k, :], hT[:, k, p["c0"]:T],
                                      start=(k == 0), stop=(k == KD - 1))
                        last.then_inc(sg("proj_done"), 1)
                        if p["last"]:
                            pe.drain().then_inc(w_used, 1)
                    if gates and j % 3 == 1 and j < 24:
                        gates(j // 3)
                    if j >= lag and made[j - lag]["turn"] is not None:
                        p = made[j - lag]
                        m = p["turn"]
                        pe.wait_ge(sg("turn_ready"), m + 1)
                        if m >= 2:
                            pe.wait_ge(sg("turn_copied"), m - 1)
                        src = turn_source(p)
                        for t in range(p["c0"] // P, NT):
                            last = nc.tensor.transpose(ps[4 + m % 2][:, t * P:(t + 1) * P], src[:, t * P:(t + 1) * P], ident[:, :])
                        last.then_inc(sg("turn_done"), 1)

            def gla():
                def turn_and_match(n, d):
                    pe.wait_ge(sg("gla_gated"), n + 1)
                    for t in range(NT):
                        nc.tensor.transpose(ps[0][:, t * P:(t + 1) * P], K1[d][:, t * P:(t + 1) * P], ident[:, :])
                    for t in range(NT):
                        tt = slice(t * P, (t + 1) * P)
                        last = mm(ps[1][:, tt], K0[d][:, tt], QG[d][:, tt], start=True, stop=True, skip_group_check=True)
                    last.then_inc(sg("gla_att"), 1)

                def direction(h, d, more):
                    n = 2 * h + d
                    pe.wait_ge(sg("gla_kdt"), n + 1)
                    pe.wait_ge(sg("gla_S"), n)
                    for c in range(NC):
                        last = mm(ps[2 + c // 2][:, 256 * (c % 2):256 * (c % 2) + 256], kdt[:, c // 2, c % 2, :],
                                  g_v[:, bass.ds(2 * h, 2), c // 2, :], start=True, stop=True, skip_group_check=True)
                    last.then_inc(sg("gla_kv"), 1)
                    pe.wait_ge(sg("gla_masked"), n + 1)
                    if d == 0:
                        pe.wait_ge(sg("gla_saved"), h)
                    for t in range(NT):
                        mm(ps[6 + t // 2][:, 256 * (t % 2):256 * (t % 2) + 256], attm[:, d, t, :],
                           g_v[:, bass.ds(2 * h, 2), t, :], start=(d == 0 and t % 2 == 0), stop=False, skip_group_check=True)
                    if more:
                        turn_and_match(n + 1, 1 - d)
                    pe.wait_ge(sg("gla_S"), n + 1)
                    for c in range(NC):
                        if c == (0 if d == 0 else 3):
                            continue
                        b = 64 * (c % 2)
                        last = mm(ps[6 + c // 4][b:b + 64, 256 * (c // 2 % 2):256 * (c // 2 % 2) + 256],
                                  QG[d][:, 64 * c:64 * c + 64], sS[:, c, :], start=False, stop=True, skip_group_check=True,
                                  tile_position=(0, b))
                    last.then_inc(sg("gla_o"), 1)

                turn_and_match(0, 0)
                with pe.Fori(0, GH - 1) as h:
                    direction(h, 0, True)
                    direction(h, 1, True)
                direction(GH - 1, 0, True)
                direction(GH - 1, 1, False)
                for h in range(GH):
                    pe.wait_ge(sg("head_normed"), h + 1)
                    if h >= 2:
                        pe.wait_ge(sg("head_mixed"), h - 1)
                    for e in range(2):
                        for t in range(NT):
                            src = (g_q if t < 2 else g_k)[:, h, (t % 2) * 256 + e * P:(t % 2) * 256 + e * P + P]
                            last = nc.tensor.transpose(ps[2 * (h % 2) + e][:, t * P:(t + 1) * P], src, ident[:, :])
                    last.then_inc(sg("head_turned"), 1)

            def ssd_gates():
                pe.wait_ge(sg("gate_cums"), 1)
                for t in range(NT):
                    nc.tensor.transpose(ps[0][:, t * P:(t + 1) * P], dtc[:, t * P:(t + 1) * P], ident[:, :])
                    nc.tensor.transpose(ps[1][:, t * P:(t + 1) * P], ac[:, t * P:(t + 1) * P], ident[:, :])
                mm(ps[2][:, 0:256], ones[:, :], albuf[:, :, :], start=True, stop=True).then_inc(sg("gate_cums_turned"), 1)

            def ssd():
                prime(pe, "ssd_bc")
                prime(pe, "ssd_y")
                for g in range(2):
                    if g:
                        pe.wait_ge(sg("ssd_cbm"), g)
                    for t in range(NT):
                        tt = slice(t * P, (t + 1) * P)
                        last = mm(ps[4][:, tt], bmc[:, g, tt], cmc[:, g, tt], start=True, stop=True, skip_group_check=True)
                    last.then_inc(sg("ssd_cb"), 1)
                    for d in range(2):
                        n = 2 * g + d
                        order = [0, 1, 2, 3] if d == 0 else [1, 0, 3, 2]
                        def decays(k, hp):
                            pe.wait_ge(sg("ssd_row"), k + 1)
                            pe.wait_ge(sg("ssd_decay"), k - 1)
                            mm(ps[hp][:, :], ones[:, :], row[hp], start=True, stop=False)
                            mm(ps[hp][:, :].rearrange("p (t i) -> p t i", t=NT), identb[:, :], m_far[:, d:d + 1, :].broadcast_to([P, NT, P]),
                               start=False, stop=True).then_inc(sg("ssd_bc"), 1)

                        def outputs(k, hp, tile):
                            pe.wait_ge(sg("ssd_mat"), k + 1)
                            pe.wait_ge(sg("ssd_y_added"), k - 1)
                            for t in range(NT):
                                last = mm(ps[2 + hp][:, P * t:P * t + P], mat[hp][:, t * P:(t + 1) * P], tile(t),
                                          start=True, stop=True, skip_group_check=True)
                            last.then_inc(sg("ssd_y"), 1)

                        k0 = 8 * n + 2
                        pe.wait_ge(sg("ssd_y_added"), k0)
                        for i in range(3):
                            pe.wait_ge(sg("ssd_wv"), 3 * n + i + 1)
                            if n and i == 0:
                                pe.wait_ge(sg("ssd_state"), 3 * n)
                            mm(ps[(5, 2, 3)[i]][:, :], bm_t[:, g, order[i], :], wv[i % 2], start=True, stop=True).then_inc(sg("ssd_kv"), 1)
                        if n == 0:
                            pe.wait_ge(sg("gate_gap"), 1)
                        for hp in range(2):
                            decays(k0 + hp, hp)
                        for i in range(3):
                            t = order[i + 1]
                            pe.wait_ge(sg("ssd_state"), 3 * n + i + 1)
                            if 3 * n + i >= 2:
                                pe.wait_ge(sg("ssd_inter_read"), 3 * n + i - 1)
                            mm(ps[6 + i % 2][:, :], cmc[:, g, t * P:(t + 1) * P], s_in[:, i, :], start=True, stop=True).then_inc(sg("ssd_inter"), 1)
                        with pe.Fori(0, 3) as pair:
                            for hp in range(2):
                                decays(k0 + 2 * pair + 2 + hp, hp)
                            for hp in range(2):
                                outputs(k0 + 2 * pair + hp, hp, lambda t: xs_t[:, bass.ds(pair + 4 * g, 1), t, :])
                        for hp in range(2):
                            outputs(k0 + 6 + hp, hp, lambda t: xs_t[:, 4 * g + 3, t, :])
                pe.wait_ge(sg("ssd_pass"), 4)
                for c in range(8):
                    if c >= 4:
                        pe.wait_ge(sg("ssd_gated"), c - 3)
                    for t in range(NT):
                        last = nc.tensor.transpose(ps[c % 4][:, t * P:(t + 1) * P], ysb[:, t, c * P:(c + 1) * P], ident[:, :])
                    last.then_inc(sg("ssd_turned"), 1)
                for g in range(2):
                    pe.wait_ge(sg("ssd_squares"), g + 1)
                    for c in range(4):
                        last = mm(ps[4 + g][:, :], ones[:, :], x[:, c, :], start=(c == 0), stop=(c == 3))
                    last.then_inc(sg("ssd_sums"), 1)

            def conformer_norm():
                for r in range(2):
                    for k in range(KD):
                        if r == 0:
                            if k == 0:
                                pe.wait_ge(sg("conf_ready"), 1)
                            rhs = conf[:, k, :]
                        else:
                            pe.wait_ge(sg("conf_squares"), k + 1)
                            rhs = csq[k % 2]
                        last = mm(ps[6 + r][:, 0:SEQ], ones[:, :], rhs, start=(k == 0), stop=(k == KD - 1))
                        if r == 1:
                            last.then_inc(sg("conf_sq_used"), 1)
                    pe.drain().then_inc(sg("conf_sums"), 1)

            def gdn_gates():
                pe.wait_ge(sg("gate_cums"), 2)
                for t in range(NT):
                    nc.tensor.transpose(ps[0][:, t * P:(t + 1) * P], gcb[:, t * P:(t + 1) * P], ident[:, :])
                mm(ps[1][:, 0:256], ones[:, :], albuf2, start=True, stop=True).then_inc(sg("gate_cums_turned"), 1)

            def gdn():
                tiles = [slice(t * P, (t + 1) * P) for t in range(NT)]

                def turn_kq(h):
                    pe.wait_ge(sg("gdn_ktq"), h + 1)
                    for t in range(NT):
                        nc.tensor.transpose(ps[0][:, tiles[t]], kts[:, tiles[t]], ident[:, :])
                    for t in range(2):
                        last = nc.tensor.transpose(ps[1][:, tiles[t]], qts[:, tiles[t]], ident[:, :])
                    last.then_inc(sg("gdn_kT"), 1)

                def spread(h, d):
                    pe.wait_ge(sg("gdn_row"), 2 * h + d + 1)
                    mm(ps[4 - d][:, :], ones[:, :], grow[d], start=True, stop=False)
                    mm(ps[4 - d][:, :].rearrange("p (t i) -> p t i", t=NT), identb[:, :], m_near[:, d:d + 1, :].broadcast_to([P, NT, P]),
                       start=False, stop=True).then_inc(sg("gdn_bc"), 1)

                def head(h, more):
                    pe.wait_ge(sg("gdn_decay"), 2 * h + 1)
                    for t in range(NT):
                        last = mm(ps[2][:, tiles[t]], kc[:, tiles[t]], kc[:, tiles[t]], start=True, stop=True, skip_group_check=True)
                    last.then_inc(sg("gdn_kk"), 1)
                    pe.wait_ge(sg("gdn_kc"), h + 1)
                    for t in range(2):
                        mm(ps[5][:, tiles[t]], kc[:, tiles[2 + t]], qc[:, tiles[t]], start=True, stop=True, skip_group_check=True)
                    pe.wait_ge(sg("gdn_osum"), h)
                    for d in range(2):
                        mm(ps[6 + d][:, 0:SEQ], ones[:, :], grow[d][:, SEQ:T], start=True, stop=False)
                        mm(ps[6 + d][:, 0:SEQ].rearrange("p (t i) -> p t i", t=2), identb[:, :], m_far[:, d:d + 1, :].broadcast_to([P, 2, P]),
                           start=False, stop=True).then_inc(sg("gdn_bc"), 1)
                    for d in range(2):
                        pe.wait_ge(sg("gdn_L"), 2 * h + d + 1)
                        for t in range(NT):
                            last = nc.tensor.transpose(ps[d][:, tiles[t]], Lm[d][:, tiles[t]], ident[:, :])
                        last.then_inc(sg("gdn_U"), 1)
                    for l in range(6):
                        for d in range(2):
                            pe.wait_ge(sg("gdn_x"), 12 * h + 2 * l + d + 1)
                            pe.wait_ge(sg("gdn_bt"), 12 * h + 2 * l + d + 1)
                            for t in range(NT):
                                last = mm(ps[3 * d][:, tiles[t]], Bm[d][:, tiles[t]], Xm[d][:, tiles[t]], start=True, stop=True, skip_group_check=True)
                            last.then_inc(sg("gdn_z"), 1)
                        for d in range(2):
                            pe.wait_ge(sg("gdn_zc"), 12 * h + 2 * l + d + 1)
                            pe.wait_ge(sg("gdn_y"), 14 * h + 2 * l + d + 1)
                            if l < 5:
                                for t in range(NT):
                                    last = mm(ps[3 * d + 1][:, tiles[t]], Ym[d][:, tiles[t]], Zm[d][:, tiles[t]], start=True, stop=True, skip_group_check=True)
                                last.then_inc(sg("gdn_px"), 1)
                            for t in range(NT):
                                last = mm(ps[3 * d + 2][:, tiles[t]], Zm[d][:, tiles[t]], Ym[d][:, tiles[t]], start=True, stop=True, skip_group_check=True)
                            last.then_inc(sg("gdn_py"), 1)
                    for d in range(2):
                        pe.wait_ge(sg("gdn_y"), 14 * h + 12 + d + 1)
                        pe.wait_ge(sg("gdn_rhs"), 2 * h + d + 1)
                        for t in range(NT):
                            mm(ps[3 * d][:, tiles[t]], Ym[d][:, tiles[t]], vb[d][:, tiles[t]], start=True, stop=True, skip_group_check=True)
                        for t in range(NT):
                            last = mm(ps[3 * d + 1][:, tiles[t]], kbe[d][:, tiles[t]], Ym[d][:, tiles[t]], start=True, stop=True, skip_group_check=True)
                        last.then_inc(sg("gdn_uw"), 1)
                    for i in range(NT):
                        for d in range(2):
                            t = (0, 1, 2, 3)[i] if d == 0 else (1, 0, 3, 2)[i]
                            bank = ps[3 * d + 2]
                            if i > 0:
                                pe.wait_ge(sg("gdn_S"), 6 * h + 2 * (i - 1) + d + 1)
                                if i == 1:
                                    pe.wait_ge(sg("gdn_uwc"), 2 * h + d + 1)
                                mm(bank[:, 0:P], wT[d][:, tiles[t]], Sg[d], start=True, stop=True, skip_group_check=True).then_inc(sg("gdn_ws"), 1)
                            if t >= 2:
                                mm(ps[7][:, (2 * d + t - 2) * P:(2 * d + t - 1) * P], qc[:, tiles[t - 2]], Sg[d], start=True, stop=True, skip_group_check=True)
                        if more and i > 0:
                            [turn_kq, lambda g: spread(g, 0), lambda g: spread(g, 1)][i - 1](h + 1)
                        for d in range(2):
                            t = (0, 1, 2, 3)[i] if d == 0 else (1, 0, 3, 2)[i]
                            bank = ps[3 * d + 2]
                            pe.wait_ge(sg("gdn_vn"), 8 * h + 2 * i + d + 1)
                            if i < 3:
                                mm(bank[:, P:2 * P], kdm[d][:, tiles[t]], vn[d], start=True, stop=True, skip_group_check=True).then_inc(sg("gdn_kv"), 1)
                            if t >= 2:
                                last = mm(ps[6][:, (t - 2) * P:(t - 1) * P], aqk[d][:, tiles[t - 2]], vn[d],
                                          start=(i == 2 and d == 0), stop=True, skip_group_check=True)
                    last.then_inc(sg("gdn_o"), 1)

                turn_kq(0)
                spread(0, 0)
                spread(0, 1)
                with pe.Fori(0, KD - 1) as h:
                    head(h, True)
                head(KD - 1, False)
                for g in range(4):
                    pe.wait_ge(sg("head_normed"), GH + g + 1)
                    for t in range(4):
                        last = nc.tensor.transpose(ps[g][:, tiles[t]], q_t[:, 2 * g + t // 2, t % 2, :], ident[:, :])
                    last.then_inc(sg("head_turned"), 1)

            def out_projection(stage, layer, mixed, c0):
                for c in range(8):
                    n = rg.first[stage] + c // 4
                    if c % 4 == 0:
                        group_in(n)
                    k0 = 8 * layer + c
                    if k0 >= 4:
                        pe.wait_ge(sg("out_scaled"), k0 - 3)
                    w = slot(n)[:, c % 4, :].rearrange("p (k c) -> p k c", k=16)
                    for k in range(16):
                        last = mm(ps[c % 4][:, c0:T], w[:, k, :], mixed(k), start=(k == 0), stop=(k == 15))
                    last.then_inc(sg("out_done"), 1)
                    if c % 4 == 3:
                        pe.drain().then_inc(w_used, 1)

            def route(layer, streams):
                tiles = [t for t in range(NT) if t // 2 in streams]
                pe.wait_ge(sg("router_in"), 16 * (layer + 1))
                for t in tiles:
                    for k in range(KD):
                        last = mm(ps[0][:, E * t:E * t + E], hT[:, k, t * P:(t + 1) * P], router[:, k, :],
                                  start=(k == 0), stop=(k == KD - 1), skip_group_check=True)
                last.then_inc(sg("logits"), 1)
                for i, t in enumerate(tiles):
                    for half in range(2):
                        m = 2 * i + half + 8 * layer
                        if i >= 1:
                            pe.wait_ge(sg("htok_copied"), m - 1)
                        for k in range(4):
                            last = nc.tensor.transpose(ps[1 + half][:, k * P:(k + 1) * P],
                                                       hT[:, 4 * half + k, t * P:(t + 1) * P], ident[:, :])
                        last.then_inc(sg("htok_turned"), 1)
                pe.wait_ge(sg("affinities"), 2 * layer + 1)
                for tt in range(2):
                    last = nc.tensor.transpose(ps[3][0:48, tt * P:(tt + 1) * P], affc[:, tt, :], ident[:, :])
                last.then_inc(sg("aff_turned"), 1)
                pe.wait_ge(sg("affinities"), 2 * layer + 2)
                for tt in range(2):
                    last = nc.tensor.transpose(ps[4][:, 48 * tt:48 * tt + 48], pickw[:, 1, tt * P:(tt + 1) * P], ident[0:48, 0:48])
                last.then_inc(sg("aff_turned"), 1)
                pe.wait_ge(sg("htok_copied"), 8 * layer + 2 * len(tiles))
                pe.wait_ge(sg("picks"), 2 * layer + 2)
                for i, s in enumerate(streams):
                    for half in range(2):
                        for q in range(2):
                            for tt in range(2):
                                last = nc.tensor.transpose(ps[2 * (i % 2) + half][:, 256 * q + P * tt:256 * q + P * tt + P],
                                                           pgate[:, s, tt, (2 * half + q) * P:(2 * half + q + 1) * P], ident[:, :])
                        last.then_inc(sg("gates_turned"), 1)

            def experts(layer, streams):
                first = rg.first[f"moe{layer}"]
                q0 = Q * layer
                with pe.Fori(0, Q) as q:
                    pe.wait_ge(sg("moe_added"), 8 * q + 8 * q0)
                    if 0 in streams:
                        pe.wait_ge(sg("moe_tcopied"), 2 * q + 2 * q0)
                        pe.wait_ge(sg("moe_silu"), 2 * q + 2 * q0)
                    for i, s in enumerate(streams):
                        for half in range(2):
                            bank = ps[(4, 7, 0, 1)[2 * i + half]]
                            for k in range(4):
                                ch = (4 * half + k) * P
                                for tt in range(2):
                                    last = mm(bank[:, k * P:(k + 1) * P], htok[:, 2 * s + tt, ch:ch + P], pick[:, s, tt, bass.ds(P * q, P)],
                                              start=(tt == 0), stop=(tt == 1), skip_group_check=True)
                            last.then_inc(sg("gathered"), 1)
                    pe.wait_ge(sg("moe_xg"), q + q0 + 1)

                    def weights(gi):
                        s = (first + gi) % RING
                        pe.wait_ge(landed[s], q * 256 + rg.landed[first + gi])
                        return ring[:, s, :, :].rearrange("p j (k n) -> p j k n", k=4)

                    def product(gi, kh, lhs, banks):
                        w = weights(gi)
                        for k in range(4):
                            for s in streams:
                                for j in range(4):
                                    last = mm(ps[banks + s][32 * j:32 * j + 32, :], lhs[s][:, 4 * kh + k, 32 * j:32 * j + 32],
                                              w[:, j, k, :], start=(kh == 0 and k == 0), stop=(kh == 1 and k == 3),
                                              tile_position=(0, 32 * j))
                        last.then_inc(w_used, 1)

                    def turn(hf, bank):
                        pe.wait_ge(sg("moe_hid"), 2 * q + 2 * q0 + hf + 1)
                        for s in streams:
                            for b in range(4):
                                last = nc.tensor.transpose(ps[bank + s][:, b * P:(b + 1) * P],
                                                           hid[s][:, 512 * hf + b * P:512 * hf + b * P + P], ident[:, :])
                        last.then_inc(sg("moe_turned"), 1)

                    for hf in range(2):
                        n = 2 * q + 2 * q0 + hf
                        if hf == 0:
                            pe.wait_ge(sg("moe_tcopied"), n)
                        pe.wait_ge(sg("moe_silu"), n)
                        product(4 * hf, 0, xg, 0)
                        product(4 * hf + 1, 1, xg, 0)
                        pe.drain().then_inc(sg("moe_h1"), 1)
                        if hf == 1:
                            turn(0, 5)
                        pe.wait_ge(sg("moe_ycopied"), 2 * q + 2 * q0)
                        pe.wait_ge(sg("moe_hid"), n)
                        product(4 * hf + 2, 0, xg, 2)
                        product(4 * hf + 3, 1, xg, 2)
                        pe.drain().then_inc(sg("moe_h3"), 1)
                    pe.wait_ge(sg("moe_tcopied"), 2 * q + 2 * q0 + 1)
                    product(8, 0, hidT, 5)
                    turn(1, 0)
                    product(9, 0, hidT, 2)
                    pe.wait_ge(sg("moe_tcopied"), 2 * q + 2 * q0 + 2)
                    product(10, 1, hidT, 5)
                    pe.drain().then_inc(sg("moe_y"), 1)
                    product(11, 1, hidT, 2)
                    pe.drain().then_inc(sg("moe_y"), 1)
                    for dt in range(KD):
                        if dt % 4 == 0:
                            pe.wait_ge(sg("moe_ycopied"), 2 * q + 2 * q0 + dt // 4 + 1)
                        if dt >= 2:
                            pe.wait_ge(sg("moe_added"), 8 * q + 8 * q0 + dt - 1)
                        for s in streams:
                            last = mm(ps[7 if dt % 2 else 4][:, 256 * s:256 * s + 256], yex[s][:, dt * P:(dt + 1) * P],
                                      gateT[:, s, bass.ds(q, 1), :], start=True, stop=True, skip_group_check=True)
                        last.then_inc(sg("moe_sum"), 1)

            pe.wait_ge(consts_made, 1)
            norm(0, T)
            for r in range(3):
                modulation(0, r)
            project(PLAN["gla"], gates=gla_gate, ready=0)
            pe.wait_ge(sg("gla_zeroed"), 1)
            gla()
            pe.wait_ge(sg("head_mixed"), GH)
            modulation(1, 0)
            project(PLAN["ssd"])
            modulation(1, 1)
            ssd_gates()
            ssd()
            modulation(1, 2)
            pe.wait_ge(sg("ssd_mixed"), 2)
            out_projection("about", 0, lambda k: (mixA if k < 8 else zmix)[:, k % 8, :], 0)
            norm(1, T)
            pe.wait_ge(sg("h_ready"), 2 * KD)
            route(0, (0, 1))
            pe.wait_ge(sg("routed"), 1)
            experts(0, (0, 1))
            pe.wait_ge(sg("x_ready"), 2)
            norm(2, T)
            project(PLAN["cd"], ready=2 * KD)
            conformer_norm()
            gdn_gates()
            gdn()
            pe.wait_ge(sg("head_mixed"), GH + 1)
            pe.wait_ge(sg("conf_done"), 1)
            out_projection("cdout", 1, lambda k: conf[:, k, :] if k < 8 else og[:, k - 8, :], SEQ)
            norm(3, SEQ)
            pe.wait_ge(sg("h_ready"), 4 * KD)
            route(1, (1,))
            pe.wait_ge(sg("routed"), 2)
            experts(1, (1,))
            norm(4, SEQ)

        @block.scalar
        def _(act):
            A_ = nc.scalar.activation

            def conditioning():
                act.wait_ge(sg("cond_zeroed"), 1)
                A_(act_c[:, :, 0:2], col("cvec", 0, 16).rearrange("p (s k) -> p k s", s=2), ACT.Silu).then_inc(sg("cond_ready"), 1)

            def modulation(layer, r):
                act.wait_ge(sg("mod_rows"), 3 * layer + r + 1)
                if 3 * layer + r:
                    act.wait_ge(sg("mod_turned"), 3 * layer + r)
                A_(mrow[:, :], ps[6][:, :], ACT.Copy).then_inc(sg("mod_row_copied"), 1)

            def norm(i, layer, which, cw):
                if i == 0:
                    act.wait_ge(consts_in, 48)
                else:
                    act.wait_ge(sg("x_ready"), i)
                for k in range(KD // 2):
                    A_(hT[:, k, T - cw:T], x[:, k, T - cw:T], ACT.Square).then_inc(sg("norm_squares"), 1)
                act.wait_ge(sg("norm_ms"), i + 1)
                A_(rstd[:, T - cw:T], rstd[:, T - cw:T], ACT.Sqrt).then_inc(sg("norm_root"), 1)
                if i == 0:
                    for r in range(3):
                        modulation(0, r)
                if layer is None:
                    return
                act.wait_ge(sg("afac_ready"), layer + 1)
                for k in range(KD):
                    act.wait_ge(sg("norm_scaled"), 8 * i + k + 1)
                    for s in range(2):
                        if s == 0 and cw < T:
                            continue
                        cc = slice(s * SEQ, (s + 1) * SEQ)
                        last = A_(hT[:, k, cc], hT[:, k, cc], ACT.Identity, bias=mod(layer, 3 * which, k, s),
                                  scale=afac[:, layer, which, k, s:s + 1])
                    last.then_inc(sg("h_ready"), 1)

            def gla_logits(n):
                h, d = n // 2, n % 2
                act.wait_ge(sg("gla_gz"), n + 1)
                A_(gz, ps[6 + n % 2][:, :], ACT.Identity, bias=col("gla_bg", 4 * d + h)).then_inc(sg("gla_z"), 1)

            def gla_softplus(n):
                act.wait_ge(sg("gla_absz"), n + 1)
                A_(gu, gu, ACT.Exp, scale=-1.0)
                if n:
                    act.wait_ge(sg("gla_scanned"), n)
                act.drain()
                A_(gl, gu, ACT.Ln, bias=1.0).then_inc(sg("gla_lnz"), 1)

            def project(made, dest, conv_bias=None, gates=False):
                def kq_squares(p):
                    act.wait_ge(sg("turn_copied"), p["turn"] + 1)
                    first, v = (0, k_t) if p["kind"] == "k" else (4, q_t)
                    act.drain()
                    for t in range(NT if first == 0 else 2):
                        A_(mrow[:, t * P:t * P + P], v[:, p["i"], t, :], ACT.Square, accum_out=rkq[:, p["i"], first + t:first + t + 1])

                def finish_conv(p):
                    c = p["conv"]
                    act.wait_ge(sg("conv_done"), c + 1)
                    to = conv_sum(p)[:, p["c0"]:T] if dest(p) is None else dest(p)
                    A_(to, conv_sum(p)[:, p["c0"]:T], ACT.Silu, bias=conv_bias(p)).then_inc(sg("conv_silu"), 1)
                    if p["turn"] is not None:
                        act.drain().then_inc(sg("turn_ready"), 1)

                waiting = None
                for j, p in enumerate(made):
                    bank, c0 = ps[p["no"] % 4], p["c0"]
                    act.wait_ge(sg("proj_done"), p["no"] + 1)
                    if p["how"] == "conv":
                        c = p["conv"]
                        if c >= 2:
                            act.wait_ge(sg("conv_done"), c - 1)
                        s0 = c0 // SEQ
                        if p["group"] >= rg.first["cd"]:
                            act.wait_ge(sg("conv_pads"), 2)
                        A_(conv_pad(p)[:, s0:2, 1:SEQ + 1], bank[:, c0:T].rearrange("p (s t) -> p s t", t=SEQ), ACT.Identity,
                           bias=p["bias"]).then_inc(sg("proj_evacuated"), 1)
                        act.drain().then_inc(sg("conv_in"), 1)
                    elif p["how"] in ("gate", "glu"):
                        i = p["i"]
                        if i >= 2:
                            act.wait_ge(sg("glu_done"), i - 1)
                        A_(gsig[i % 2] if p["how"] == "gate" else gval[i % 2], bank[:, SEQ:T],
                           ACT.Sigmoid if p["how"] == "gate" else ACT.Identity, bias=p["bias"]).then_inc(sg("proj_evacuated"), 1)
                        if p["how"] == "glu":
                            act.drain().then_inc(sg("glu_in"), 1)
                    elif p["turn"] is not None:
                        if p["turn"] >= 2:
                            act.wait_ge(sg("turn_done"), p["turn"] - 1)
                        A_(turn_source(p), bank[:, :], ACT.Identity, bias=p["bias"]).then_inc(sg("proj_evacuated"), 1)
                        act.drain().then_inc(sg("turn_ready"), 1)
                    else:
                        A_(dest(p), bank[:, c0:T], ACT.Silu if p["how"] == "silu" else ACT.Identity,
                           bias=p["bias"]).then_inc(sg("proj_evacuated"), 1)
                    if gates and j % 3 == 1:
                        gla_logits(j // 3)
                    if gates and j % 3 == 2:
                        gla_softplus(j // 3)
                    if waiting is not None:
                        finish_conv(waiting)
                    waiting = p if p["how"] == "conv" else None
                    if j >= 4 and made[j - 4]["kind"] in ("k", "q") and made[j - 4]["turn"] is not None:
                        kq_squares(made[j - 4])
                if waiting is not None:
                    finish_conv(waiting)
                for p in made[-4:]:
                    if p["kind"] in ("k", "q") and p["turn"] is not None:
                        kq_squares(p)

            def conformer_norm():
                for k in range(KD):
                    act.wait_ge(sg("conf_centered"), k + 1)
                    if k >= 2:
                        act.wait_ge(sg("conf_sq_used"), k - 1)
                    A_(csq[k % 2], conf[:, k, :], ACT.Square).then_inc(sg("conf_squares"), 1)
                act.wait_ge(sg("root_in"), 4)
                A_(rstd[:, 0:SEQ], rstd[:, 0:SEQ], ACT.Sqrt).then_inc(sg("root_out"), 1)
                for k in range(KD):
                    act.wait_ge(sg("conf_scaled"), k + 1)
                    A_(conf[:, k, :], conf[:, k, :], ACT.Silu, bias=col("conf_bb", k), scale=col("conf_g", k))
                act.drain().then_inc(sg("conf_done"), 1)

            def gdn_gates():
                act.wait_ge(sg("root_in"), 5)
                A_(rkq[:, :, :], rkq[:, :, :], ACT.Sqrt).then_inc(sg("root_out"), 1)
                act.wait_ge(sg("sp_abs"), 2)
                A_(gcb[64:128, :], small[64:128, :], ACT.Sigmoid)
                A_(Um[0][0:64, :], Um[0][0:64, :], ACT.Exp, scale=-1.0).then_inc(sg("sp_u"), 1)
                A_(alogx[0:64, :], cols[0:64, COL_AT["gdn_alog"]:COL_AT["gdn_alog"] + 1], ACT.Exp)
                act.wait_ge(sg("sp_w"), 2)
                A_(Xm[0][0:64, :], Ym[0][0:64, :], ACT.Ln).then_inc(sg("sp_ln"), 1)
                act.wait_ge(sg("gate_gap"), 2)
                A_(egl2, egl2, ACT.Exp)
                A_(egc, gcT, ACT.Exp)
                A_(ekd, ekd, ACT.Exp).then_inc(sg("gate_exps"), 1)

            def gdn():
                def decays(h):
                    act.wait_ge(sg("gdn_kT"), h + 1)
                    A_(kc, ps[0][:, :], ACT.Copy)
                    for d in range(2):
                        act.wait_ge(sg("gdn_bc"), 4 * h + d + 1)
                        for t in range(NT):
                            last = A_(dec[d][:, t * P:t * P + P], ps[4 - d][:, t * P:t * P + P], ACT.Exp, bias=gcT[:, t, d, bass.ds(h, 1)], scale=-1.0)
                        last.then_inc(sg("gdn_decay"), 1)

                def head(h, more):
                    act.wait_ge(sg("gdn_o"), h)
                    A_(qc, ps[1][:, 0:SEQ], ACT.Copy).then_inc(sg("gdn_kc"), 1)
                    for d in range(2):
                        act.wait_ge(sg("gdn_bc"), 4 * h + d + 3)
                        for t in range(2):
                            last = A_(aqk[d][:, t * P:t * P + P], ps[6 + d][:, t * P:t * P + P], ACT.Exp, bias=ngcT[:, 2 + t, d, bass.ds(h, 1)])
                        last.then_inc(sg("gdn_qdecay"), 1)
                    for d in range(2):
                        act.wait_ge(sg("gdn_U"), 2 * h + d + 1)
                        A_(Um[d], ps[d][:, :], ACT.Copy).then_inc(sg("gdn_Uc"), 1)
                    for l in range(6):
                        for d in range(2):
                            act.wait_ge(sg("gdn_z"), 12 * h + 2 * l + d + 1)
                            A_(Zm[d], ps[3 * d][:, :], ACT.Copy).then_inc(sg("gdn_zc"), 1)
                    for d in range(2):
                        act.wait_ge(sg("gdn_uw"), 2 * h + d + 1)
                        A_(um[d], ps[3 * d][:, :], ACT.Copy)
                        A_(wT[d], ps[3 * d + 1][:, :], ACT.Copy).then_inc(sg("gdn_uwc"), 1)
                    if more:
                        decays(h + 1)

                decays(0)
                with act.Fori(0, KD - 1) as h:
                    head(h, True)
                head(KD - 1, False)
                act.wait_ge(sg("root_in"), 6)
                A_(onr[:, :, :], onr[:, :, :], ACT.Sqrt).then_inc(sg("root_out"), 1)

            def out_projection(layer, streams):
                act.wait_ge(sg("out_bias"), layer + 1)
                for c in range(8):
                    act.wait_ge(sg("out_done"), 8 * layer + c + 1)
                    if 8 * layer + c >= 2:
                        act.wait_ge(sg("out_added"), 8 * layer + c - 1)
                    for s in streams:
                        cc = slice(s * SEQ, (s + 1) * SEQ)
                        last = A_(hT[:, c % 2, cc], ps[c % 4][:, cc], ACT.Identity, bias=gbias[:, c, s:s + 1], scale=mod(layer, 2, c, s))
                    last.then_inc(sg("out_scaled"), 1)

            def route(layer, streams):
                n = 2 * len(streams)
                for m in range(2 * n):
                    t = (NT - n) + m // 2
                    act.wait_ge(sg("htok_turned"), 8 * layer + m + 1)
                    A_(htok[:, t, 512 * (m % 2):512 * (m % 2) + 512], ps[1 + m % 2][:, :], ACT.Copy).then_inc(sg("htok_copied"), 1)
                    if m == 1:
                        act.wait_ge(sg("logits_shifted"), layer + 1)
                        A_(aff[:, NT - n:NT, :], aff[:, NT - n:NT, :], ACT.Exp).then_inc(sg("aff_exp"), 1)
            def experts(layer, streams):
                q0 = Q * layer
                with act.Fori(0, Q) as q:
                    n = 2 * q + 2 * q0
                    for i, s in enumerate(streams):
                        for half in range(2):
                            b = 2 * i + half
                            act.wait_ge(sg("gathered"), 2 * len(streams) * q + 16 * layer + b + 1)
                            last = A_(xg[s][:, 4 * half:4 * half + 4, :], ps[(4, 7, 0, 1)[b]][:, :].rearrange("p (k c) -> p k c", k=4), ACT.Copy)
                    last.then_inc(sg("moe_xg"), 1)
                    for hf in range(2):
                        act.wait_ge(sg("moe_h1"), n + hf + 1)
                        act.wait_ge(sg("moe_hid"), n + hf)
                        for s in streams:
                            last = A_(sil[s], ps[s][:, :], ACT.Silu)
                        last.then_inc(sg("moe_silu"), 1)
                    for hf in range(2):
                        act.wait_ge(sg("moe_turned"), n + hf + 1)
                        for s in streams:
                            last = A_(hidT[s][:, 4 * hf:4 * hf + 4, :], ps[(5 if hf == 0 else 0) + s][:, :].rearrange("p (b c) -> p b c", b=4), ACT.Copy)
                        last.then_inc(sg("moe_tcopied"), 1)
                    for hd in range(2):
                        act.wait_ge(sg("moe_y"), n + hd + 1)
                        act.wait_ge(sg("moe_sum"), 8 * q + 8 * q0)
                        for s in streams:
                            last = A_(yex[s][:, 512 * hd:512 * hd + 512], ps[(5 if hd == 0 else 2) + s][:, :], ACT.Copy)
                        last.then_inc(sg("moe_ycopied"), 1)

            def ssd_gates():
                act.wait_ge(sg("sp_abs"), 1)
                A_(sp_u[64:128, :], sp_u[64:128, :], ACT.Exp, scale=-1.0).then_inc(sg("sp_u"), 1)
                A_(alog_e[64:128, :], cols[64:128, COL_AT["ssd_alog"]:COL_AT["ssd_alog"] + 1], ACT.Exp)
                act.wait_ge(sg("sp_w"), 1)
                A_(sp_l[64:128, :], sp_w[64:128, :], ACT.Ln).then_inc(sg("sp_ln"), 1)
                modulation(1, 1)
                act.wait_ge(sg("gate_gap"), 1)
                A_(eal[:, :, :], ps[2][:, 0:256].rearrange("p (t r) -> p t r", t=NT), ACT.Exp)
                A_(cdec[:, :, :], acT[:, :, :], ACT.Exp)
                A_(dtw[:, :, :], dtw[:, :, :], ACT.Exp).then_inc(sg("gate_exps"), 1)

            def ssd():
                prime(act, "ssd_decay")
                for g in range(2):
                    for d in range(2):
                        n = 2 * g + d
                        with act.Fori(0, 4) as pair:
                            for hp in range(2):
                                k = 8 * n + 2 + 2 * pair + hp
                                act.wait_ge(sg("ssd_bc"), k + 1)
                                act.wait_ge(sg("ssd_mat"), k - 1)
                                for t in range(NT):
                                    last = A_(seg[hp][:, t * P:t * P + P], ps[hp][:, t * P:t * P + P], ACT.Exp,
                                              bias=nacT[:, t, bass.ds(2 * pair + 32 * d + 8 * g + hp, 1)])
                                last.then_inc(sg("ssd_decay"), 1)
                for g in range(2):
                    act.wait_ge(sg("ssd_gated"), 4 * g + 4)
                    A_(x[:, 0:4, :], zmix[:, 4 * g:4 * g + 4, :], ACT.Square).then_inc(sg("ssd_squares"), 1)
                    act.wait_ge(sg("root_in"), g + 2)
                    A_(rstd[:, :], rstd[:, :], ACT.Sqrt).then_inc(sg("root_out"), 1)

            def gla():
                def exps(n, d):
                    g = gcum[:, bass.ds(n, 1), :].rearrange("p a c -> p (a c)")
                    act.wait_ge(sg("gla_gap"), n + 1)
                    A_(QG[d], g, ACT.Exp, scale=1.0 / 16)
                    A_(K0[d], g, ACT.Exp, scale=-1.0 / 16)
                    A_(egl[:, d, :], g.rearrange("p (c j) -> p c j", j=CH)[:, :, CH - 1 if d == 0 else 0], ACT.Exp, scale=1.0 / 16)
                    A_(K1[d], K1[d], ACT.Exp, scale=1.0 / 16).then_inc(sg("gla_exps"), 1)

                def save(h):
                    A_(g_q[:, bass.ds(h, 1), :].rearrange("p a c -> p (a c)"), ps[6][:, :], ACT.Copy)
                    A_(g_k[:, bass.ds(h, 1), :].rearrange("p a c -> p (a c)"), ps[7][:, :], ACT.Copy).then_inc(sg("gla_saved"), 1)

                def turned(n):
                    act.wait_ge(sg("gla_att"), n + 1)
                    src = ps[0][:, :].rearrange("p (t d) -> p t d", t=NT)
                    A_(kdt[0:64, :, 0, :], src[0:64], ACT.Copy)
                    A_(kdt[64:128, :, 1, :], src[64:128], ACT.Copy).then_inc(sg("gla_kdt"), 1)

                act.wait_ge(sg("turn_done"), 8)
                exps(0, 0)
                turned(0)
                exps(1, 1)
                turned(1)
                with act.Fori(1, GH) as h:
                    act.wait_ge(sg("gla_o"), 2 * h - 1)
                    exps(2 * h, 0)
                    turned(2 * h)
                    act.wait_ge(sg("gla_o"), 2 * h)
                    save(h - 1)
                    exps(2 * h + 1, 1)
                    turned(2 * h + 1)
                act.wait_ge(sg("gla_o"), 2 * GH)
                save(GH - 1)
                act.drain()
                A_(x[:, 0:4, :], g_q[:, :, :], ACT.Square)
                A_(x[:, 4:8, :], g_k[:, :, :], ACT.Square).then_inc(sg("head_squares"), 1)
                act.wait_ge(sg("root_in"), 1)
                A_(ssq[:, :, :, :], ssq[:, :, :, :], ACT.Sqrt).then_inc(sg("root_out"), 1)

            def dest(p):
                if p["kind"] == "small":
                    return small[:, :]
                if p["kind"] == "og":
                    return og[:, p["i"], :]
                if p["how"] == "conv" and (p["kind"] == "xs" or p["group"] >= rg.first["cd"]):
                    return None
                return {"q": g_q, "k": g_k, "r": mixA, "z": zmix, "bm": bmc, "cm": cmc}[p["kind"]][:, p["i"], :]

            def ssd_conv_bias(p):
                return col("ssd_cb", {"xs": 0, "bm": 8, "cm": 10}[p["kind"]] + p["i"])

            act.dma_start(dsk[:, :], A["ssd_d"].broadcast_to([P, SH])).then_inc(consts_in, 16)
            act.wait_ge(consts_in, 48)
            conditioning()
            norm(0, 0, 0, T)
            act.dma_start(w2p[:, :, :], A["w2p"]).then_inc(consts_in, 16)
            project(PLAN["gla"], dest, gates=True)
            gla()
            modulation(1, 0)
            act.wait_ge(sg("conv_pads"), 1)
            project(PLAN["ssd"], dest, ssd_conv_bias)
            ssd_gates()
            ssd()
            modulation(1, 2)
            act.wait_ge(sg("ssd_mixed"), 2)
            act.dma_start(x[:, :, :], A["xT"].rearrange("(k p) t -> p k t", p=P)).then_inc(sg("x_again"), 16)
            out_projection(0, (0, 1))
            act.wait_ge(sg("x_ready"), 1)
            act.dma_start(router[:, :, :], A["router"][0]).then_inc(sg("router_in"), 16)
            norm(1, 0, 1, T)
            route(0, (0, 1))
            experts(0, (0, 1))
            norm(2, 1, 0, T)
            act.wait_ge(sg("cd_consts"), 1)
            project(PLAN["cd"], dest, lambda p: 0.0)
            conformer_norm()
            gdn_gates()
            gdn()
            out_projection(1, (1,))
            act.wait_ge(sg("x_ready"), 3)
            act.dma_start(router[:, :, :], A["router"][1]).then_inc(sg("router_in"), 16)
            norm(3, 1, 1, SEQ)
            route(1, (1,))
            experts(1, (1,))
            norm(4, None, None, SEQ)

        @block.vector
        def _(dve):
            V = nc.vector

            def modulation(layer, r):
                dve.wait_ge(sg("mod_turned"), 3 * layer + r + 1)
                src = ps[7][:, :].rearrange("p (q g s) -> p g q s", q=4, g=4)[:, :, :, 0:2]
                bias = col(f"mod_b{layer}", 16 * r, 16).rearrange("p (g q) -> p g q", g=4).unsqueeze(3).broadcast_to([P, 4, 4, 2])
                V.tensor_tensor(modT[:, layer, 4 * r:4 * r + 4, :, :], src, bias, ALU.add)
                dve.drain().then_inc(sg("mod_added"), 1)
                if r == 2:
                    for w in range(2):
                        sc = modT[:, layer, 6 * w + 2:6 * w + 4, :, :].rearrange("p a b s -> p (a b) s")
                        g = col("norm1" if w == 0 else "norm2", 8 * layer, 8).unsqueeze(2).broadcast_to([P, KD, 2])
                        last = V.scalar_tensor_tensor(afac[:, layer, w, :, :], sc, 1.0, g, ALU.add, ALU.mult)
                    last.then_inc(sg("afac_ready"), 1)

            def squares(cw):
                for k in range(KD // 2, KD):
                    xk = x[:, k, T - cw:T]
                    V.tensor_tensor(hT[:, k, T - cw:T], xk, xk, ALU.mult).then_inc(sg("norm_squares2"), 1)

            def norm(i, cw):
                c0 = T - cw
                squares(cw)
                dve.wait_ge(sg("norm_sums"), i + 1)
                V.tensor_scalar(rstd[:, c0:T], ps[7][:, 0:cw], 1.0 / D, 1e-6, ALU.mult, ALU.add).then_inc(sg("norm_ms"), 1)
                dve.wait_ge(sg("norm_root"), i + 1)
                V.reciprocal(rstd[:, c0:T], rstd[:, c0:T])
                dve.drain()
                for k in range(KD):
                    V.tensor_tensor(hT[:, k, c0:T], x[:, k, c0:T], rstd[:, c0:T], ALU.mult).then_inc(sg("norm_scaled"), 1)

            def gla_magnitude(n):
                dve.drain()
                dve.wait_ge(sg("gla_z"), n + 1)
                V.tensor_scalar(gm, gz, 0.0, None, ALU.min)
                V.scalar_tensor_tensor(gu, gz, -1.0, gz, ALU.mult, ALU.max).then_inc(sg("gla_absz"), 1)

            def gla_sums(n):
                dve.wait_ge(sg("gla_lnz"), n + 1)
                V.tensor_tensor(gm, gm, gl, ALU.subtract)
                dve.drain()
                rev = (lambda a: a) if n % 2 == 0 else (lambda a: a[:, ::-1])
                V.tensor_tensor_scan(rev(gcum[:, n, :]), rst64[:, :], rev(gm), 0.0, ALU.mult, ALU.add).then_inc(sg("gla_scanned"), 1)

            def project(made, dest, taps=None, gates=False):
                def conformer_taps(i, lo, hi):
                    y = conf[:, i, :].rearrange("p (r c) -> p r c", r=ROWS)
                    for w in range(lo, hi):
                        if w == 0:
                            V.tensor_scalar(y, gluR[:, i, :, 0:GW], col("conf_w", i), col("conf_b", i), ALU.mult, ALU.add)
                        else:
                            V.scalar_tensor_tensor(y, gluR[:, i, :, w:w + GW], col("conf_w", 8 * w + i), y, ALU.mult, ALU.add)
                        dve.drain()

                glu_at = {j + n: (p["i"], lo, hi) for j, p in enumerate(made) if p["how"] == "glu" for n, (lo, hi) in enumerate(CONF_STEPS)}
                for j in range(len(made) + 2):
                    if j < len(made) and made[j]["how"] == "glu":
                        i = made[j]["i"]
                        dve.wait_ge(sg("glu_in"), i + 1)
                        V.tensor_tensor(gluR[:, i, :, CK // 2:CK // 2 + GW], gsig[i % 2].rearrange("p (r c) -> p r c", r=ROWS),
                                        gval[i % 2].rearrange("p (r c) -> p r c", r=ROWS), ALU.mult)
                        dve.drain().then_inc(sg("glu_done"), 1)
                    if j < len(made) and made[j]["how"] == "conv":
                        p = made[j]
                        c, s0 = p["conv"], p["c0"] // SEQ
                        if p["kind"] == "k" and p["i"] == 0 and p["group"] >= rg.first["cd"]:
                            dve.wait_ge(sg("conv_silu"), c)
                            dve.drain()
                            V.memset(cpad2[:, :, :, 0:1], 0.0)
                            V.memset(cpad2[:, :, :, SEQ + 1:SEQ + 2], 0.0)
                            dve.drain().then_inc(sg("conv_pads"), 1)
                        dve.wait_ge(sg("conv_in"), c + 1)
                        if c >= 2:
                            dve.wait_ge(sg("conv_silu"), c - 1)
                            before = conv_turn[c - 2]
                            if before is not None:
                                dve.wait_ge(sg("turn_done"), before + 1)
                        to = conv_sum(p)[:, p["c0"]:T].rearrange("p (s t) -> p s t", t=SEQ)
                        w, pad = taps(p), conv_pad(p)
                        V.tensor_scalar(to, pad[:, s0:2, 1:SEQ + 1], w[1], None, ALU.mult)
                        dve.drain()
                        V.scalar_tensor_tensor(to, pad[:, s0:2, 0:SEQ], w[0], to, ALU.mult, ALU.add)
                        dve.drain()
                        V.scalar_tensor_tensor(to, pad[:, s0:2, 2:SEQ + 2], w[2], to, ALU.mult, ALU.add).then_inc(sg("conv_done"), 1)
                    if j >= 2 and made[j - 2]["turn"] is not None:
                        p = made[j - 2]
                        dve.wait_ge(sg("turn_done"), p["turn"] + 1)
                        V.tensor_copy(dest(p), ps[4 + p["turn"] % 2][:, p["c0"]:T].rearrange("p (t c) -> p t c", c=P)).then_inc(sg("turn_copied"), 1)
                    if gates and 1 <= j < 24 and j % 3 == 1:
                        gla_magnitude(j // 3)
                    if gates and j >= 3 and j % 3 == 0:
                        gla_sums(j // 3 - 1)
                    if j in glu_at:
                        conformer_taps(*glu_at[j])

            def conformer_norm():
                dve.drain().then_inc(sg("conf_ready"), 1)
                dve.wait_ge(sg("conf_sums"), 1)
                V.tensor_scalar(rstd[:, 0:SEQ], ps[6][:, 0:SEQ], 1.0 / D, None, ALU.mult)
                dve.drain()
                for k in range(KD):
                    V.tensor_tensor(conf[:, k, :], conf[:, k, :], rstd[:, 0:SEQ], ALU.subtract).then_inc(sg("conf_centered"), 1)
                dve.wait_ge(sg("conf_sums"), 2)
                dve.drain()
                V.tensor_scalar(rstd[:, 0:SEQ], ps[7][:, 0:SEQ], 1.0 / D, 1e-5, ALU.mult, ALU.add).then_inc(sg("root_in"), 1)
                dve.wait_ge(sg("root_out"), 4)
                V.reciprocal(rstd[:, 0:SEQ], rstd[:, 0:SEQ])
                dve.drain()
                for k in range(KD):
                    V.tensor_tensor(conf[:, k, :], conf[:, k, :], rstd[:, 0:SEQ], ALU.mult).then_inc(sg("conf_scaled"), 1)

            def gdn_gates():
                V.tensor_scalar(rkq[:, :, :], rkq[:, :, :], 1e-6, None, ALU.add).then_inc(sg("root_in"), 1)
                dve.wait_ge(sg("root_out"), 5)
                V.reciprocal(rkq[:, :, :], rkq[:, :, :])
                dve.drain()
                V.tensor_scalar(rkq[:, :, 4:6], rkq[:, :, 4:6], float(P) ** -0.5, None, ALU.mult)
                rows = slice(0, 64)
                z, u, w, l, sp = Lm[0], Um[0], Ym[0], Xm[0], Lm[1]
                V.tensor_scalar(z[rows], small[rows, :], cols[rows, COL_AT["gdn_dtb"]:COL_AT["gdn_dtb"] + 1], None, ALU.add)
                dve.drain()
                V.scalar_tensor_tensor(u[rows], z[rows], -1.0, z[rows], ALU.mult, ALU.max).then_inc(sg("sp_abs"), 1)
                softplus_tail(rows, z, u, w, l, sp)
                V.tensor_scalar(w[rows], sp[rows], alogx[rows, :], -1.0, ALU.mult, ALU.mult)
                dve.drain()
                V.tensor_tensor_scan(gcb[0:32, :], rst128[0:32, :], w[0:32, :], 0.0, ALU.mult, ALU.add)
                V.tensor_tensor_scan(gcb[32:64, ::-1], rst128[32:64, :], w[32:64, ::-1], 0.0, ALU.mult, ALU.add)
                dve.drain()
                V.memset(albuf2, 0.0)
                dve.drain()
                for t in range(NT):
                    for d in range(2):
                        e = t * P + edge(d)
                        last = V.tensor_scalar(albuf2[0:64, t, 32 * d:32 * d + 32], ident[0:64, 32 * d:32 * d + 32], gcb[0:64, e:e + 1], None, ALU.mult)
                last.then_inc(sg("gate_cums"), 1)
                dve.wait_ge(sg("gate_cums_turned"), 2)
                tm = ps[0][:, :].rearrange("p (t d r) -> p t d r", t=NT, d=4)
                V.tensor_copy(gcT, tm[:, :, 0:2, 0:8])
                V.tensor_scalar(ngcT, tm[:, :, 0:2, 0:8], -1.0, None, ALU.mult)
                V.tensor_copy(btT, tm[:, :, 2:4, 0:8])
                V.tensor_copy(egl2, ps[1][:, 0:256].rearrange("p (t d r) -> p t d r", t=NT, d=2)[:, :, :, 0:8])
                dve.drain()
                V.tensor_tensor(ekd, egl2, gcT, ALU.subtract).then_inc(sg("gate_gap"), 1)
                dve.wait_ge(sg("gate_exps"), 2)
                V.tensor_tensor(beg, btT, egc, ALU.mult)
                dve.drain()

            def gdn():
                dve.wait_ge(sg("cd_consts"), 2)
                tiles = [slice(t * P, (t + 1) * P) for t in range(NT)]

                def t4(ap):
                    return ap.rearrange("p (t c) -> p t c", c=P)

                def normed(h):
                    kh, qh = [v[:, bass.ds(h, 1)].rearrange("p a t c -> p (a t) c") for v in (k_t, q_t)]
                    rk = rkq[:, bass.ds(h, 1), :].rearrange("p a t -> p (a t)").unsqueeze(2)
                    V.tensor_tensor(t4(kts), kh, rk[:, 0:4].broadcast_to([P, NT, P]), ALU.mult)
                    V.tensor_tensor(t4(qts), qh, rk[:, 4:6].broadcast_to([P, 2, P]), ALU.mult).then_inc(sg("gdn_ktq"), 1)

                def solve(h, more):
                    def gate(v, t, d):
                        return v[:, t, d, bass.ds(h, 1)]

                    def gates(v, d):
                        return v[:, :, d, bass.ds(h, 1)].broadcast_to([P, NT, P])

                    def head(v):
                        return v[:, bass.ds(h, 1)].rearrange("p a t c -> p (a t) c")

                    idb = ident[:, :].unsqueeze(1).broadcast_to([P, NT, P])
                    m1 = lvm[:, 0:1, :].broadcast_to([P, NT, P])
                    dve.wait_ge(sg("gdn_kk"), h + 1)
                    for d in range(2):
                        dve.wait_ge(sg("gdn_decay"), 2 * h + d + 1)
                        for t in range(NT):
                            last = V.scalar_tensor_tensor(Lm[d][:, tiles[t]], ps[2][:, tiles[t]], gate(btT, t, d), dec[d][:, tiles[t]], ALU.mult, ALU.mult)
                        last.then_inc(sg("gdn_L"), 1)
                        dve.drain()
                        V.tensor_tensor(t4(Xm[d]), t4(Lm[d]), m1, ALU.mult)
                        dve.drain()
                        V.tensor_tensor(t4(Xm[d]), idb, t4(Xm[d]), ALU.subtract).then_inc(sg("gdn_x"), 1)
                    for d in range(2):
                        dve.wait_ge(sg("gdn_Uc"), 2 * h + d + 1)
                        V.tensor_tensor(t4(Ym[d]), t4(Um[d]), m1, ALU.mult)
                        dve.drain()
                        V.tensor_tensor(t4(Ym[d]), idb, t4(Ym[d]), ALU.subtract).then_inc(sg("gdn_y"), 1)
                        if d == 0:
                            dve.wait_ge(sg("gdn_qdecay"), 2 * h + 2)
                            for e in range(2):
                                V.tensor_tensor(aqk[e], ps[5][:, 0:SEQ], aqk[e], ALU.mult)
                    for d in range(2):
                        for t in range(NT):
                            V.tensor_scalar(kdm[d][:, tiles[t]], kts[:, tiles[t]], gate(ekd, t, d), None, ALU.mult)
                    for l in range(6):
                        for d in range(2):
                            if l < 5:
                                dve.wait_ge(sg("gdn_px"), 10 * h + 2 * l + d + 1)
                                V.tensor_tensor(Xm[d], Xm[d], ps[3 * d + 1][:, :], ALU.subtract).then_inc(sg("gdn_x"), 1)
                            dve.wait_ge(sg("gdn_py"), 12 * h + 2 * l + d + 1)
                            V.tensor_tensor(Ym[d], Ym[d], ps[3 * d + 2][:, :], ALU.subtract).then_inc(sg("gdn_y"), 1)
                        if l < 2:
                            V.tensor_tensor(t4(vb[l]), head(v_t), gates(btT, l), ALU.mult)
                            V.tensor_tensor(t4(kbe[l]), t4(kts), gates(beg, l), ALU.mult).then_inc(sg("gdn_rhs"), 1)
                        if l == 2 and more:
                            dve.drain()
                            normed(h + 1)
                    for i in range(NT):
                        for d in range(2):
                            t = (0, 1, 2, 3)[i] if d == 0 else (1, 0, 3, 2)[i]
                            if i == 0:
                                dve.wait_ge(sg("gdn_uwc"), 2 * h + d + 1)
                                V.tensor_copy(vn[d], um[d][:, tiles[t]]).then_inc(sg("gdn_vn"), 1)
                            else:
                                dve.wait_ge(sg("gdn_ws"), 6 * h + 2 * (i - 1) + d + 1)
                                V.tensor_tensor(vn[d], um[d][:, tiles[t]], ps[3 * d + 2][:, 0:P], ALU.subtract).then_inc(sg("gdn_vn"), 1)
                        if i < 3:
                            for d in range(2):
                                t = (0, 1, 2, 3)[i] if d == 0 else (1, 0, 3, 2)[i]
                                dve.wait_ge(sg("gdn_kv"), 6 * h + 2 * i + d + 1)
                                if i == 0:
                                    V.tensor_copy(Sg[d], ps[3 * d + 2][:, P:2 * P]).then_inc(sg("gdn_S"), 1)
                                else:
                                    V.scalar_tensor_tensor(Sg[d], Sg[d], gate(egl2, t, d), ps[3 * d + 2][:, P:2 * P], ALU.mult, ALU.add).then_inc(sg("gdn_S"), 1)
                    dve.wait_ge(sg("gdn_o"), h + 1)
                    o = q_t[:, bass.ds(h, 1), :, :].rearrange("p a t c -> p (a t) c")
                    V.tensor_scalar(o, ps[6][:, 0:256].rearrange("p (t c) -> p t c", t=2), 1.0, None, ALU.mult)
                    for d in range(2):
                        dve.drain()
                        for t in range(2):
                            V.scalar_tensor_tensor(o[:, t, :], ps[7][:, (2 * d + t) * P:(2 * d + t + 1) * P], gate(egc, 2 + t, d), o[:, t, :], ALU.mult, ALU.add)
                    dve.drain().then_inc(sg("gdn_osum"), 1)

                normed(0)
                with dve.Fori(0, KD - 1) as h:
                    solve(h, True)
                solve(KD - 1, False)
                dve.drain()
                sq = hT[:, 0:4, :].rearrange("p a b -> p (a b)").rearrange("p (h t c) -> p h t c", h=8, t=2)
                V.tensor_tensor(sq, q_t[:, :, :, :], q_t[:, :, :, :], ALU.mult)
                dve.drain()
                V.tensor_reduce(onr[:, :, :], sq, AX.X, ALU.add)
                dve.drain()
                V.tensor_scalar(onr[:, :, :], onr[:, :, :], 1.0 / P, 1e-6, ALU.mult, ALU.add).then_inc(sg("root_in"), 1)
                dve.wait_ge(sg("root_out"), 6)
                V.reciprocal(onr[:, :, :], onr[:, :, :])
                dve.drain()
                for g in range(4):
                    og2 = q_t[:, 2 * g:2 * g + 2, :, :]
                    V.tensor_tensor(og2, og2, onr[:, 2 * g:2 * g + 2, :].unsqueeze(3).broadcast_to([P, 2, 2, P]), ALU.mult).then_inc(sg("head_normed"), 1)
                for g in range(4):
                    dve.wait_ge(sg("head_turned"), GH + g + 1)
                    for e in range(2):
                        h = 2 * g + e
                        V.scalar_tensor_tensor(og[:, h, :], ps[g][:, 256 * e:256 * e + 256], col("gdn_g", h), og[:, h, :], ALU.mult, ALU.mult)
                dve.drain().then_inc(sg("head_mixed"), 1)

            def final():
                squares(SEQ)
                dve.wait_ge(sg("norm_sums"), 5)
                V.tensor_scalar(rstd[:, SEQ:T], ps[7][:, 0:SEQ], 1.0 / D, 1e-6, ALU.mult, ALU.add).then_inc(sg("norm_ms"), 1)
                dve.wait_ge(sg("norm_root"), 5)
                V.reciprocal(rstd[:, SEQ:T], rstd[:, SEQ:T])
                dve.drain()
                for k in range(KD):
                    V.scalar_tensor_tensor(hT[:, k, SEQ:T], x[:, k, SEQ:T], col("final", k), rstd[:, SEQ:T], ALU.mult, ALU.mult)
                dve.drain().then_inc(sg("out_ready"), 1)

            def out_projection(layer, streams, bias):
                for s in streams:
                    for h in range(2):
                        last = V.tensor_tensor(gbias[:, 4 * h:4 * h + 4, s], modT[:, layer, 4 + h, :, s], col(bias, 4 * h, 4), ALU.mult)
                last.then_inc(sg("out_bias"), 1)
                if layer == 0:
                    dve.wait_ge(sg("x_again"), 16)
                for c in range(8):
                    dve.wait_ge(sg("out_scaled"), 8 * layer + c + 1)
                    cc = slice(0 if 0 in streams else SEQ, T)
                    last = V.tensor_tensor(x[:, c, cc], x[:, c, cc], hT[:, c % 2, cc], ALU.add).then_inc(sg("out_added"), 1)
                dve.drain().then_inc(sg("x_ready"), 1)

            def route(layer, streams):
                n = 2 * len(streams)
                tl = slice(NT - n, NT)

                def over_experts(v):
                    return v.unsqueeze(2).broadcast_to([P, n, E])

                V.memset(affc[:, :, :], 0.0)
                dve.wait_ge(sg("logits"), layer + 1)
                lg = ps[0][:, 0:NT * E].rearrange("p (t e) -> p t e", t=NT)[:, tl, :]
                V.tensor_reduce(rowst[:, 0, tl], lg, AX.X, ALU.max)
                dve.drain()
                V.tensor_tensor(aff[:, tl, :], lg, over_experts(rowst[:, 0, tl]), ALU.subtract).then_inc(sg("logits_shifted"), 1)
                dve.wait_ge(sg("aff_exp"), layer + 1)
                V.tensor_reduce(rowst[:, 1, tl], aff[:, tl, :], AX.X, ALU.add)
                dve.drain()
                V.reciprocal(rowst[:, 2, tl], rowst[:, 1, tl])
                dve.drain()
                V.tensor_tensor(aff[:, tl, :], aff[:, tl, :], over_experts(rowst[:, 2, tl]), ALU.mult)
                dve.drain()
                for s in streams:
                    V.tensor_copy(affc[:, :, 32 * s:32 * s + E], aff[:, 2 * s:2 * s + 2, :])
                dve.drain().then_inc(sg("affinities"), 1)
                dve.wait_ge(sg("aff_turned"), 2 * layer + 1)
                V.tensor_copy(affT, ps[3][0:48, 0:SEQ])
                dve.drain()
                bufs = [affT, pickw[:, 0, :], pickw[:, 1, :], pickw[:, 0, :], pickw[:, 1, :]]
                for r in range(4):
                    V.max(top8[:, :], bufs[r])
                    dve.drain()
                    V.match_replace(bufs[r + 1], top8[:, :], bufs[r], -1.0)
                    dve.drain()
                V.tensor_scalar(pickv, pickw[:, 1, :], 0.0, None, ALU.is_lt)
                V.memset(affT, 1.0)
                dve.drain()
                V.tensor_tensor_scan(pickw[:, 0, :], affT, pickv, 0.0, ALU.mult, ALU.add)
                dve.drain()
                V.tensor_tensor(pickw[:, 1, :], pickw[:, 0, :], pickv, ALU.mult)
                dve.drain().then_inc(sg("affinities"), 1)
                dve.wait_ge(sg("aff_turned"), 2 * layer + 2)
                V.tensor_copy(slotT[:, :, :], ps[4][:, 0:96].rearrange("p (a b) -> p a b", a=2))
                dve.drain()
                for s in streams:
                    for tt in range(2):
                        pv = pick[:, s, tt, :].rearrange("p (e c) -> p e c", e=E)
                        V.tensor_tensor(pv, slotT[:, tt, 32 * s:32 * s + E].unsqueeze(2).broadcast_to([P, E, CAP]),
                                        iota1[:, :].unsqueeze(1).broadcast_to([P, E, CAP]), ALU.is_equal)
                dve.drain().then_inc(sg("picks"), 1)
                for s in streams:
                    for tt in range(2):
                        V.tensor_tensor(pgate[:, s, tt, :].rearrange("p (e c) -> p e c", e=E), pick[:, s, tt, :].rearrange("p (e c) -> p e c", e=E),
                                        aff[:, 2 * s + tt, :].unsqueeze(2).broadcast_to([P, E, CAP]), ALU.mult)
                dve.drain().then_inc(sg("picks"), 1)
                for i, s in enumerate(streams):
                    for half in range(2):
                        dve.wait_ge(sg("gates_turned"), 4 * layer + 2 * i + half + 1)
                        V.tensor_copy(gateT[:, s, 2 * half:2 * half + 2, :], ps[2 * i + half][:, :].rearrange("p (q t) -> p q t", q=2))
                dve.drain().then_inc(sg("routed"), 1)

            def experts(layer, streams):
                q0 = Q * layer
                with dve.Fori(0, Q) as q:
                    n = 2 * q + 2 * q0
                    for hf in range(2):
                        dve.wait_ge(sg("moe_h3"), n + hf + 1)
                        dve.wait_ge(sg("moe_silu"), n + hf + 1)
                        for s in streams:
                            last = V.tensor_tensor(hid[s][:, 512 * hf:512 * hf + 512], sil[s], ps[2 + s][:, :], ALU.mult)
                        last.then_inc(sg("moe_hid"), 1)
                    for dt in range(KD):
                        dve.wait_ge(sg("moe_sum"), 8 * q + 8 * q0 + dt + 1)
                        for s in streams:
                            cc = slice(s * SEQ, (s + 1) * SEQ)
                            last = V.scalar_tensor_tensor(x[:, dt, cc], ps[7 if dt % 2 else 4][:, cc], mod(layer, 5, dt, s),
                                                          x[:, dt, cc], ALU.mult, ALU.add)
                        last.then_inc(sg("moe_added"), 1)
                dve.drain().then_inc(sg("x_ready"), 1)

            def softplus_tail(rows, z, u, w, l, to):
                dve.wait_ge(sg("sp_u"), 1 if rows.start else 2)
                V.tensor_scalar(w[rows], u[rows], 1.0, None, ALU.add).then_inc(sg("sp_w"), 1)
                dve.drain()
                V.tensor_scalar(to[rows], w[rows], -1.0, TINY, ALU.add, ALU.add)
                dve.drain()
                V.reciprocal(to[rows], to[rows])
                dve.drain()
                V.tensor_tensor(to[rows], to[rows], u[rows], ALU.mult)
                dve.wait_ge(sg("sp_ln"), 1 if rows.start else 2)
                dve.drain()
                V.scalar_tensor_tensor(to[rows], l[rows], TINY, to[rows], ALU.add, ALU.mult)
                dve.drain()
                V.scalar_tensor_tensor(to[rows], z[rows], 0.0, to[rows], ALU.max, ALU.add)
                dve.drain()

            def ssd_gates():
                rows = slice(64, 128)
                dve.wait_ge(sg("conv_silu"), 12)
                dve.drain()
                V.memset(dtc[:, :], 0.0)
                V.memset(ac[:, :], 0.0)
                V.tensor_scalar(sp_z[rows, :], small[rows, :], cols[rows, COL_AT["ssd_dtb"]:COL_AT["ssd_dtb"] + 1], None, ALU.add)
                dve.drain()
                V.scalar_tensor_tensor(sp_u[rows, :], sp_z[rows, :], -1.0, sp_z[rows, :], ALU.mult, ALU.max).then_inc(sg("sp_abs"), 1)
                softplus_tail(rows, sp_z, sp_u, sp_w, sp_l, dtc)
                V.tensor_scalar(sp_w[rows, :], dtc[rows, :], alog_e[rows, :], -1.0, ALU.mult, ALU.mult)
                dve.drain()
                V.tensor_tensor_scan(ac[64:96, :], rst128[64:96, :], sp_w[64:96, :], 0.0, ALU.mult, ALU.add)
                V.tensor_tensor_scan(ac[96:128, ::-1], rst128[96:128, :], sp_w[96:128, ::-1], 0.0, ALU.mult, ALU.add)
                dve.drain()
                for t in range(NT):
                    for d in range(2):
                        e = t * P + edge(d)
                        last = V.tensor_scalar(albuf[:, t, 32 * d:32 * d + 32], ident[:, 64 + 32 * d:96 + 32 * d], ac[:, e:e + 1], None, ALU.mult)
                last.then_inc(sg("gate_cums"), 1)
                modulation(1, 1)
                dve.wait_ge(sg("gate_cums_turned"), 1)
                V.tensor_copy(dtT[:, :, :], ps[0][:, :].rearrange("p (t r) -> p t r", t=NT)[:, :, 64:128])
                V.tensor_copy(acT[:, :, :], ps[1][:, :].rearrange("p (t r) -> p t r", t=NT)[:, :, 64:128])
                V.tensor_scalar(nacT[:, :, :], ps[1][:, :].rearrange("p (t r) -> p t r", t=NT)[:, :, 64:128], -1.0, None, ALU.mult)
                dve.drain()
                V.tensor_tensor(dtw[:, :, :], ps[2][:, 0:256].rearrange("p (t r) -> p t r", t=NT), acT[:, :, :], ALU.subtract).then_inc(sg("gate_gap"), 1)
                dve.wait_ge(sg("gate_exps"), 1)
                V.tensor_tensor(dtw[:, :, :], dtw[:, :, :], dtT[:, :, :], ALU.mult)
                dve.drain()

            def ssd():
                prime(dve, "ssd_mat")
                prime(dve, "ssd_y_added")
                for g in range(2):
                    dve.wait_ge(sg("ssd_cb"), g + 1)
                    V.tensor_copy(cbs, ps[4][:, :])
                    dve.drain().then_inc(sg("ssd_cbm"), 1)
                    for d in range(2):
                        n = 2 * g + d
                        order = [0, 1, 2, 3] if d == 0 else [1, 0, 3, 2]
                        r0 = 32 * d + 8 * g

                        def spread(v, t):
                            return v[:, t, r0:r0 + 8].rearrange("p (c a) -> p c a", a=2).unsqueeze(3).broadcast_to([P, 4, 2, 64])

                        for i in range(3):
                            if i == 2:
                                dve.wait_ge(sg("ssd_kv"), 3 * n + 1)
                            V.tensor_tensor(heads(wv[i % 2]), xs_t[:, 4 * g:4 * g + 4, order[i], :].rearrange("p c (a b) -> p c a b", a=2),
                                            spread(dtw, order[i]), ALU.mult).then_inc(sg("ssd_wv"), 1)
                        if n >= 1:
                            dve.wait_ge(sg("ssd_inter"), 3 * n)
                        for i in range(3):
                            if i > 0:
                                V.tensor_tensor(heads(s_in[:, i, :]), heads(s_in[:, i - 1, :]), spread(eal, order[i]), ALU.mult)
                                dve.drain()
                            dve.wait_ge(sg("ssd_kv"), 3 * n + i + 1)
                            if i == 0:
                                V.tensor_copy(s_in[:, 0, :], ps[5][:, :])
                            else:
                                V.tensor_tensor(s_in[:, i, :], s_in[:, i, :], ps[1 + i][:, :], ALU.add)
                            dve.drain().then_inc(sg("ssd_state"), 1)
                        for i in range(3):
                            dve.wait_ge(sg("ssd_inter"), 3 * n + i + 1)
                            V.tensor_tensor(heads(wv[i % 2]), heads(ps[6 + i % 2][:, :]), spread(cdec, order[i + 1]), ALU.mult).then_inc(sg("ssd_inter_read"), 1)
                            if n == 0 and i == 0:
                                dve.wait_ge(sg("ssd_skip"), 1)
                            dve.drain()
                            yt = ysb[:, order[i + 1], 512 * g:512 * g + 512]
                            V.tensor_tensor(yt, yt, wv[i % 2], ALU.add)
                        dve.drain()
                        with dve.Fori(0, 4) as pair:
                            for hp in range(2):
                                k = 8 * n + 2 + 2 * pair + hp
                                dve.wait_ge(sg("ssd_decay"), k + 1)
                                dve.wait_ge(sg("ssd_y"), k - 1)
                                for t in range(NT):
                                    last = V.scalar_tensor_tensor(mat[hp][:, t * P:t * P + P], seg[hp][:, t * P:t * P + P],
                                                                  dtT[:, t, bass.ds(2 * pair + r0 + hp, 1)], cbs[:, t * P:t * P + P],
                                                                  ALU.mult, ALU.mult)
                                last.then_inc(sg("ssd_mat"), 1)
                            for hp in range(2):
                                k = 8 * n + 2 + 2 * pair + hp
                                dve.wait_ge(sg("ssd_y"), k + 1)
                                yh = ysb[:, :, bass.ds(128 * pair + 512 * g + 64 * hp, 64)]
                                V.tensor_tensor(yh, yh, ps[2 + hp][:, :].rearrange("p (t c) -> p t c", t=NT)[:, :, 64 * hp:64 * hp + 64],
                                                ALU.add).then_inc(sg("ssd_y_added"), 1)
                        dve.drain().then_inc(sg("ssd_pass"), 1)
                for c in range(8):
                    dve.wait_ge(sg("ssd_turned"), c + 1)
                    V.tensor_tensor(zmix[:, c, :], zmix[:, c, :], ps[c % 4][:, :], ALU.mult).then_inc(sg("ssd_gated"), 1)
                for g in range(2):
                    dve.wait_ge(sg("ssd_sums"), g + 1)
                    V.tensor_scalar(rstd[:, :], ps[4 + g][:, :], 1.0 / 512, 1e-6, ALU.mult, ALU.add).then_inc(sg("root_in"), 1)
                    dve.wait_ge(sg("root_out"), g + 2)
                    V.reciprocal(rstd[:, :], rstd[:, :])
                    dve.drain()
                    for c in range(4 * g, 4 * g + 4):
                        V.scalar_tensor_tensor(zmix[:, c, :], zmix[:, c, :], col("ssd_g", c), rstd[:, :], ALU.mult, ALU.mult)
                    dve.drain().then_inc(sg("ssd_mixed"), 1)

            def gla():
                def row_of(v, i):
                    return v[:, bass.ds(i, 1), :].rearrange("p a c -> p (a c)")

                def gap(n, d):
                    g3 = row_of(gcum, n).rearrange("p (c j) -> p c j", j=CH)
                    edge = CH - 1 if d == 0 else 0
                    V.tensor_tensor(K1[d].rearrange("p (c j) -> p c j", j=CH), g3[:, :, edge:edge + 1].broadcast_to([P, NC, CH]),
                                    g3, ALU.subtract).then_inc(sg("gla_gap"), 1)

                def gated(n, h, d):
                    dve.wait_ge(sg("gla_exps"), n + 1)
                    V.scalar_tensor_tensor(QG[d], row_of(g_q, h), float(P) ** -0.5, QG[d], ALU.mult, ALU.mult)
                    V.tensor_tensor(K0[d], row_of(g_k, h), K0[d], ALU.mult)
                    V.tensor_tensor(K1[d], row_of(g_k, h), K1[d], ALU.mult).then_inc(sg("gla_gated"), 1)

                def direction(h, d, more):
                    n = 2 * h + d
                    if more:
                        if d == 1:
                            gap(n + 1, 0)
                        else:
                            gap(n + 1, 1)
                    dve.wait_ge(sg("gla_att"), n + 1)
                    V.tensor_copy(mrow[:, 0:1], ones[:, 0:1])
                    V.copy_predicated(attm[:, d, :, :], m_gla[:, d:d + 1, :].broadcast_to([P, NT, P]),
                                      ps[1][:, :].rearrange("p (t i) -> p t i", t=NT)).then_inc(sg("gla_masked"), 1)
                    if more:
                        gated(n + 1, h + d, 1 - d)
                    dve.wait_ge(sg("gla_kv"), n + 1)
                    dve.wait_ge(sg("gla_o"), n)
                    order = [0, 1, 2, 3, 4, 5, 6, 7] if d == 0 else [3, 2, 1, 0, 7, 6, 5, 4]
                    for a, b in zip(order, order[1:]):
                        kv = ps[2 + a // 2][:, 256 * (a % 2):256 * (a % 2) + 256]
                        if a == order[0]:
                            last = V.tensor_scalar(sS[:, b, :], kv, ones[:, 0:1], None, ALU.mult)
                        else:
                            last = V.scalar_tensor_tensor(sS[:, b, :], sS[:, a, :], egl[:, d, a:a + 1], kv, ALU.mult, ALU.add)
                        if b != order[-1]:
                            dve.drain()
                    last.then_inc(sg("gla_S"), 1)

                dve.drain()
                V.memset(kdt[:, :, :, :], 0.0)
                V.memset(sS[:, :, :], 0.0)
                V.memset(attm[:, :, :, :], 0.0)
                dve.drain().then_inc(sg("gla_zeroed"), 1)
                gap(0, 0)
                gated(0, 0, 0)
                with dve.Fori(0, GH - 1) as h:
                    direction(h, 0, True)
                    direction(h, 1, True)
                direction(GH - 1, 0, True)
                direction(GH - 1, 1, False)
                dve.wait_ge(sg("head_squares"), 1)
                for a in range(2):
                    V.tensor_reduce(ssq[:, a, :, :].rearrange("p h t -> p (h t)"), x[:, 4 * a:4 * a + 4, :].rearrange("p a (t e) -> p (a t) e", t=2),
                                    AX.X, ALU.add)
                dve.drain()
                V.tensor_scalar(ssq[:, :, :, :], ssq[:, :, :, :], 1.0 / GDV, 1e-6, ALU.mult, ALU.add).then_inc(sg("root_in"), 1)
                dve.wait_ge(sg("root_out"), 1)
                V.reciprocal(ssq[:, :, :, :], ssq[:, :, :, :])
                dve.drain()
                for h in range(GH):
                    for a in range(2):
                        oh = (g_k if a else g_q)[:, h, :].rearrange("p (t e) -> p t e", t=2)
                        last = V.tensor_tensor(oh, oh, ssq[:, a, h, :].unsqueeze(2).broadcast_to([P, 2, GDV]), ALU.mult)
                    last.then_inc(sg("head_normed"), 1)
                for h in range(GH):
                    dve.wait_ge(sg("head_turned"), h + 1)
                    for e in range(2):
                        c = 2 * h + e
                        last = V.scalar_tensor_tensor(mixA[:, c, :], ps[2 * (h % 2) + e][:, :], col("gla_g", c), mixA[:, c, :], ALU.mult, ALU.mult)
                    last.then_inc(sg("head_mixed"), 1)

            def dest(p):
                if p["group"] >= rg.first["cd"]:
                    return {"v": v_t, "q": q_t, "k": k_t}[p["kind"]][:, p["i"], :, :]
                return {"v": g_v, "xs": xs_t, "bm": bm_t}[p["kind"]][:, p["i"], :, :]

            def cd_taps(p):
                return [col("gdn_cw", 24 * w + 8 * "qkv".index(p["kind"]) + p["i"]) for w in range(3)]

            def ssd_taps(p):
                return [col("ssd_cw", 12 * w + {"xs": 0, "bm": 8, "cm": 10}[p["kind"]] + p["i"]) for w in range(3)]

            dve.wait_ge(consts_in, 48)
            V.memset(act_c[:, :, :], 0.0).then_inc(sg("cond_zeroed"), 1)
            norm(0, T)
            for r in range(3):
                modulation(0, r)
            project(PLAN["gla"], dest, gates=True)
            gla()
            modulation(1, 0)
            V.memset(cpad[:, :, :, 0:1], 0.0)
            V.memset(cpad[:, :, :, SEQ + 1:SEQ + 2], 0.0)
            dve.drain().then_inc(sg("conv_pads"), 1)
            project(PLAN["ssd"], dest, ssd_taps)
            ssd_gates()
            ssd()
            modulation(1, 2)
            out_projection(0, (0, 1), "ab_bout")
            norm(1, T)
            route(0, (0, 1))
            experts(0, (0, 1))
            norm(2, T)
            dve.wait_ge(sg("cd_consts"), 1)
            project(PLAN["cd"], dest, cd_taps)
            conformer_norm()
            gdn_gates()
            gdn()
            out_projection(1, (1,), "cd_bout")
            norm(3, SEQ)
            route(1, (1,))
            experts(1, (1,))
            final()

        @block.gpsimd
        def _(pool):
            G = nc.gpsimd
            G.memset(ident[:, :], 0.0)
            G.memset(ones[:, :], 1.0)
            G.memset(identb[:, :], 0.0)
            G.memset(m_far[:, :, :], 0.0)
            G.memset(m_near[:, :, :], 0.0)
            G.memset(m_gla[:, :, :], 1)
            G.memset(rst64[:, :], 1.0)
            G.memset(rst128[:, :], 1.0)
            G.iota(iota1[:, :], [[1, CAP]], base=1, channel_multiplier=0, allow_small_or_imprecise_dtypes=True)
            pool.drain()
            G.memset(rst64[:, :].rearrange("p (c j) -> p c j", j=CH)[:, :, 0:1], 0.0)
            G.memset(rst128[:, :].rearrange("p (c j) -> p c j", j=P)[:, :, 0:1], 0.0)
            G.affine_select(out=ident[:, :], in_=ident[:, :], compare_op=ALU.not_equal, fill=1.0, base=0,
                            pattern=[[-1, P]], channel_multiplier=1)
            G.affine_select(out=identb[:, :], in_=identb[:, :], compare_op=ALU.not_equal, fill=1.0, base=0,
                            pattern=[[-1, P]], channel_multiplier=1)
            for d in range(2):
                sign = 1 - 2 * d
                G.affine_select(out=m_far[:, d, :], in_=m_far[:, d, :], compare_op=ALU.is_ge, fill=-1e30, base=0,
                                pattern=[[sign, P]], channel_multiplier=-sign)
                G.affine_select(out=m_gla[:, d, :], in_=m_gla[:, d, :], compare_op=ALU.is_ge, fill=0, base=0,
                                pattern=[[sign, P]], channel_multiplier=-sign)
                G.affine_select(out=m_near[:, d, :], in_=m_near[:, d, :], compare_op=ALU.is_gt, fill=1e30, base=0,
                                pattern=[[-sign, P]], channel_multiplier=sign)
            pool.drain()
            G.memset(m_gla[0:64, :, 64:128], 0)
            G.memset(m_gla[64:128, :, 0:64], 0)
            pool.drain().then_inc(consts_made, 1)

            def ssd():
                pool.wait_ge(sg("gate_cums"), 1)
                pool.wait_ge(sg("gate_gap"), 1)
                for t in range(NT):
                    G.tensor_tensor(heads(ysb[:, t, :]), xs_t[:, :, t, :].rearrange("p c (a b) -> p c a b", a=2),
                                    dsk[:, :].rearrange("p (c a) -> p c a", a=2).unsqueeze(3).broadcast_to([P, 8, 2, 64]), ALU.mult)
                pool.drain().then_inc(sg("ssd_skip"), 1)
                prime(pool, "ssd_row")
                for g in range(2):
                    for d in range(2):
                        with pool.Fori(0, 4) as pair:
                            for hp in range(2):
                                k = 16 * g + 8 * d + 2 + 2 * pair + hp
                                pool.wait_ge(sg("ssd_bc"), k - 1)
                                G.tensor_tensor(row[hp], ac[:, :], ident[:, bass.ds(2 * pair + 64 + 32 * d + 8 * g + hp, 1)].broadcast_to([P, T]),
                                                ALU.mult).then_inc(sg("ssd_row"), 1)

            def gdn():
                pool.wait_ge(sg("x_ready"), 2)
                G.memset(gluR[:, :, :, :], 0.0)
                pool.drain().then_inc(sg("cd_consts"), 1)
                G.memset(lvm[:, :, :], 1.0)
                for l in range(7):
                    pool.drain()
                    b = 2 << l
                    v = lvm[:, l, :].rearrange("p (n c) -> p n c", c=b)
                    G.affine_select(out=v, in_=v, compare_op=ALU.is_ge, fill=0.0, base=0, pattern=[[-b, P // b], [0, b]], channel_multiplier=1)
                    pool.drain()
                    G.affine_select(out=v, in_=v, compare_op=ALU.is_ge, fill=0.0, base=b - 1, pattern=[[b, P // b], [0, b]], channel_multiplier=-1)
                pool.drain()
                for l in range(6, 0, -1):
                    G.tensor_tensor(lvm[:, l, :], lvm[:, l, :], lvm[:, l - 1, :], ALU.subtract)
                    pool.drain()
                G.tensor_tensor(lvm[:, 0, :], lvm[:, 0, :], ident[:, :], ALU.subtract)
                pool.drain().then_inc(sg("cd_consts"), 1)
                pool.wait_ge(sg("gate_gap"), 2)
                with pool.Fori(0, KD) as h:
                    pool.wait_ge(sg("gdn_bc"), 4 * h)
                    for d in range(2):
                        G.tensor_tensor(grow[d], gcb, ident[:, bass.ds(h + 32 * d, 1)].broadcast_to([P, T]), ALU.mult).then_inc(sg("gdn_row"), 1)
                    for l in range(6):
                        for d in range(2):
                            if l == 0:
                                pool.wait_ge(sg("gdn_Uc"), 2 * h + d + 1)
                                pool.wait_ge(sg("gdn_uw"), 2 * h)
                            else:
                                pool.wait_ge(sg("gdn_z"), 12 * h + 2 * l + d - 1)
                            G.tensor_tensor(Bm[d].rearrange("p (t c) -> p t c", c=P), Um[d].rearrange("p (t c) -> p t c", c=P),
                                            lvm[:, l + 1:l + 2, :].broadcast_to([P, NT, P]), ALU.mult).then_inc(sg("gdn_bt"), 1)

            ssd()
            gdn()


def pack_columns(np, a):
    got = np.zeros((P, NCOLS), np.float32)

    def put(name, vec, at=0):
        v = np.asarray(vec).reshape(-1, P).T
        got[:, COL_AT[name] + at:COL_AT[name] + at + v.shape[1]] = v

    def tiles(vec, order, place):
        for j, (kind, i) in enumerate(order):
            if kind != "small":
                o = place[kind] + i * P
                got[:, at0 + j] = vec[o:o + P]

    put("mod_b0", a["mod_b"][0])
    put("mod_b1", a["mod_b"][1])
    put("norm1", a["norm1_g"])
    put("norm2", a["norm2_g"])
    put("final", a["final_norm_g"])
    put("cvec", a["c_ctx"])
    put("cvec", a["c"][0], 8)
    b = a["ab_b_in"][0]
    at0 = COL_AT["ab_b"]
    tiles(b, AB_GLA + AB_SSD, AB_PLACE)
    for dst, src, n in AB_SMALL:
        got[dst:dst + n, at0] = b[src:src + n]
    put("ab_bout", a["ab_b_out"][0])
    put("gla_bg", a["gla_b_gate2"][0])
    put("gla_g", a["gla_norm_g"][0])
    put("ssd_cw", a["ssd_conv_w"][0])
    put("ssd_cb", a["ssd_conv_b"][0])
    put("ssd_g", a["ssd_norm_g"][0])
    for d in range(2):
        got[64 + 32 * d:80 + 32 * d, COL_AT["ssd_dtb"]] = a["ssd_dt_bias"][0, d]
        got[64 + 32 * d:80 + 32 * d, COL_AT["ssd_alog"]] = a["ssd_a_log"][0, d]
        got[32 * d:32 * d + 8, COL_AT["gdn_dtb"]] = a["gdn_dt_bias"][0, d]
        got[32 * d:32 * d + 8, COL_AT["gdn_alog"]] = a["gdn_a_log"][0, d]
    b = a["cd_b_in"][0]
    at0 = COL_AT["cd_b"]
    tiles(b, CD_ALL, CD_PLACE)
    for dst, src, n in CD_SMALL:
        got[dst:dst + n, at0] = b[src:src + n]
    put("cd_bout", a["cd_b_out"][0])
    put("conf_w", a["conf_dw_w"][0])
    put("conf_b", a["conf_dw_b"][0])
    put("conf_g", a["conf_ln_g"][0])
    put("conf_bb", a["conf_ln_b"][0])
    put("gdn_cw", a["gdn_conv_w"][0])
    put("gdn_g", a["gdn_norm_g"][0])
    return got


AB_PLACE = {"q": 0, "k": 512, "v": 1024, "r": 2048, "z": 3104, "xs": 4128, "bm": 5152, "cm": 5408}
AB_SMALL = [(0, 3072, 16), (32, 3088, 16), (64, 5664, 16), (96, 5680, 16)]
CD_PLACE = {"ga": 0, "gb": 1024, "q": 2048, "k": 3072, "v": 4096, "og": 5120}
CD_SMALL = [(0, 6144, 8), (32, 6152, 8), (64, 6160, 8), (96, 6168, 8)]


def pack_projection(np, w, order, place, gates):
    got = np.zeros((len(order), P, KD, P), np.float32)
    for j, (kind, i) in enumerate(order):
        if kind == "small":
            for dst, src, n in gates:
                got[j, :, :, dst:dst + n] = w[:, src:src + n].reshape(KD, P, n).transpose(1, 0, 2)
        else:
            o = place[kind] + i * P
            got[j] = w[:, o:o + P].reshape(KD, P, P).transpose(1, 0, 2)
    return got.reshape(len(order), P, KD * P)


def pack_out(np, w):
    return np.ascontiguousarray(w.reshape(16, P, KD, P).transpose(2, 1, 0, 3)).reshape(KD, P, 16 * P)


def lay_out(np, a):
    w2p = np.zeros((P, 8, P), np.float32)
    for d in range(2):
        w2p[32 * d:32 * d + 16, 4 * d:4 * d + 4] = a["gla_w_gate2"][0, d].reshape(16, GH, P)
    return {
        "xT": np.ascontiguousarray(np.concatenate([a["ctx"][0].T, a["x"][0].T], axis=1)),
        "cols": pack_columns(np, a),
        "mod_w": a["mod_w"],
        "ab_w": pack_projection(np, a["ab_w_in"][0], AB_GLA + AB_SSD, AB_PLACE, AB_SMALL),
        "ab_wo": pack_out(np, a["ab_w_out"][0]),
        "cd_w": pack_projection(np, a["cd_w_in"][0], CD_ALL, CD_PLACE, CD_SMALL),
        "cd_wo": pack_out(np, a["cd_w_out"][0]),
        "w2p": w2p,
        "ssd_d": a["ssd_d"],
        "router": np.ascontiguousarray(a["moe_router"].reshape(2, KD, P, E).transpose(0, 2, 1, 3)),
        "w1": a["moe_w1"], "w3": a["moe_w3"], "w2": a["moe_w2"],
    }


def kernel(**inputs):
    import numpy as np
    import concourse.bacc as bacc
    from concourse import mybir as _mybir
    from concourse.bass_utils import run_bass_kernel_spmd as run

    nc = bacc.Bacc("TRN2", target_bir_lowering=False, num_devices=1, dynamic_dma_scratch_size=1024)
    arrays, args = {}, {}
    for name, a in lay_out(np, {k: np.asarray(v) for k, v in inputs.items()}).items():
        arrays[f"in_{name}"] = a
        args[name] = nc.dram_tensor(f"in_{name}", a.shape, _mybir.dt.from_np(a.dtype), kind="ExternalInput").ap()
    out = nc.dram_tensor("out_t", (D, SEQ), F32, kind="ExternalOutput").ap()
    hybrid_backbone(nc, args, out)
    r = run(nc, [arrays], core_ids=[0])
    return np.ascontiguousarray(r.results[0]["out_t"].T)[None]
```
